# Optimizing a Trainium2 kernel written in Bass

```python
import jax, jax.numpy as jnp
from jax import lax
import numpy as np

D_MODEL = 2048
BATCH = 1
SEQ = 1024
DEPTH = 1

CHUNK = 64
EPS = 1e-6
NEG = -1e30

A_HEADS = 16
A_HEAD_DIM = 64
A_WIDTH = A_HEADS * A_HEAD_DIM
A_PREV = 8
REL_CLIP = 128

B_Q_HEADS = 16
B_KV_HEADS = 2
B_GROUP = B_Q_HEADS // B_KV_HEADS
B_HEAD_DIM = 64
B_WIDTH = B_Q_HEADS * B_HEAD_DIM
B_KV_WIDTH = B_KV_HEADS * B_HEAD_DIM
WINDOW = 128
B_PREV = WINDOW // CHUNK - 1

T5_BUCKETS = 32
T5_MAX_DIST = 128

IN_WIDTHS = [A_WIDTH, A_WIDTH, A_WIDTH, A_WIDTH,
             B_WIDTH, B_KV_WIDTH, B_KV_WIDTH, B_WIDTH,
             D_MODEL, D_MODEL]
IN_COLS = sum(IN_WIDTHS)

kernel_name = "hybrid_chunked_relbias_swa_sink_gated_merge"

def rmsnorm(x, g):
    x32 = x.astype(jnp.float32)
    y = x32 * lax.rsqrt(jnp.mean(x32 * x32, axis=-1, keepdims=True) + EPS)
    return y.astype(x.dtype) * g

def chunk_band(t, n_prev):
    b, s, h, d = t.shape
    nc = s // CHUNK
    tc = t.reshape(b, nc, CHUNK, h, d)
    pad = jnp.pad(tc, ((0, 0), (n_prev, 0), (0, 0), (0, 0), (0, 0)))
    return jnp.concatenate([pad[:, j:j + nc] for j in range(n_prev + 1)], axis=2)

def band_geometry(nc, n_prev):
    k_len = (n_prev + 1) * CHUNK
    i = np.arange(CHUNK)[:, None]
    kk = np.arange(k_len)[None, :]
    rel = n_prev * CHUNK + i - kk
    valid = ((np.arange(nc)[:, None] - n_prev) * CHUNK + kk) >= 0
    return rel.astype(np.int32), valid

def t5_bucket(rel_pos):
    nb = T5_BUCKETS // 2
    ret = (rel_pos > 0).astype(np.int32) * nb
    n = np.abs(rel_pos)
    max_exact = nb // 2
    large = max_exact + (np.log(np.maximum(n, 1) / max_exact)
                         / np.log(T5_MAX_DIST / max_exact) * (nb - max_exact)).astype(np.int32)
    large = np.minimum(large, nb - 1)
    return (ret + np.where(n < max_exact, n, large)).astype(np.int32)

def chunked_relbias_attention(q, k, v, rel_table):
    b, s, h, d = q.shape
    nc = s // CHUNK
    qc = q.reshape(b, nc, CHUNK, h, d) * (d ** -0.5)
    kb = chunk_band(k, A_PREV)
    vb = chunk_band(v, A_PREV)
    rel, valid = band_geometry(nc, A_PREV)
    idx = np.clip(rel, -REL_CLIP, REL_CLIP) + REL_CLIP
    bias = rel_table[:, idx].astype(jnp.float32)
    sc = jnp.einsum('bcqhd,bckhd->bhcqk', qc, kb).astype(jnp.float32)
    sc = sc + bias[None, :, None]
    sc = jnp.where(valid[None, None, :, None, :], sc, NEG)
    p = jax.nn.softmax(sc, axis=-1).astype(v.dtype)
    o = jnp.einsum('bhcqk,bckhd->bcqhd', p, vb)
    return o.reshape(b, s, h * d)

def sliding_window_sink_gqa(q, k, v, t5_table, sinks):
    b, s, _, d = q.shape
    nc = s // CHUNK
    qc = q.reshape(b, nc, CHUNK, B_KV_HEADS, B_GROUP, d) * (d ** -0.5)
    kb = chunk_band(k, B_PREV)
    vb = chunk_band(v, B_PREV)
    rel, valid = band_geometry(nc, B_PREV)
    bucket = t5_bucket(-rel)
    bias = jnp.transpose(t5_table[bucket], (2, 0, 1)).astype(jnp.float32)
    bias = bias.reshape(B_KV_HEADS, B_GROUP, CHUNK, -1)
    sc = jnp.einsum('bcqhgd,bckhd->bhgcqk', qc, kb).astype(jnp.float32)
    sc = sc + bias[None, :, :, None]
    sc = jnp.where(valid[None, None, None, :, None, :], sc, NEG)
    sink = sinks.astype(jnp.float32).reshape(B_KV_HEADS, B_GROUP)[None, :, :, None, None, None]
    m = jnp.maximum(jnp.max(sc, axis=-1, keepdims=True), sink)
    e = jnp.exp(sc - m)
    p = (e / (jnp.sum(e, axis=-1, keepdims=True) + jnp.exp(sink - m))).astype(v.dtype)
    o = jnp.einsum('bhgcqk,bckhd->bcqhgd', p, vb)
    return o.reshape(b, s, B_Q_HEADS * d)

def setup_inputs(seed: int = 0) -> dict:
    key = jax.random.key(seed)
    ks = jax.random.split(key, 10)
    f32 = jnp.float32
    return {
        "x": jax.random.normal(ks[0], (BATCH, SEQ, D_MODEL), f32),
        "norm_gain": 1.0 + 0.01 * jax.random.normal(ks[1], (D_MODEL,), f32),
        "w_in": jax.random.normal(ks[2], (D_MODEL, IN_COLS), f32) * D_MODEL ** -0.5,
        "rel_bias_a": 0.1 * jax.random.normal(ks[3], (A_HEADS, 2 * REL_CLIP + 1), f32),
        "t5_bias": 0.1 * jax.random.normal(ks[4], (T5_BUCKETS, B_Q_HEADS), f32),
        "sinks_b": 0.5 * jax.random.normal(ks[5], (B_Q_HEADS,), f32),
        "w_branch_a": jax.random.normal(ks[6], (A_WIDTH, D_MODEL), f32) * A_WIDTH ** -0.5,
        "w_branch_b": jax.random.normal(ks[7], (B_WIDTH, D_MODEL), f32) * B_WIDTH ** -0.5,
        "w_out": jax.random.normal(ks[8], (D_MODEL, D_MODEL), f32) * D_MODEL ** -0.5,
        "final_gain": 1.0 + 0.01 * jax.random.normal(ks[9], (D_MODEL,), f32),
    }

def reference(x, norm_gain, w_in, rel_bias_a, t5_bias, sinks_b, w_branch_a, w_branch_b, w_out, final_gain):
    b, s, _ = x.shape
    for _layer in range(DEPTH):
        h = rmsnorm(x, norm_gain)
        proj = h @ w_in
        q_a, k_a, v_a, z_a, q_b, k_b, v_b, z_b, g_a, g_b = jnp.split(
            proj, list(np.cumsum(IN_WIDTHS)[:-1]), axis=-1)
        att_a = chunked_relbias_attention(
            q_a.reshape(b, s, A_HEADS, A_HEAD_DIM),
            k_a.reshape(b, s, A_HEADS, A_HEAD_DIM),
            v_a.reshape(b, s, A_HEADS, A_HEAD_DIM), rel_bias_a)
        u_a = (jax.nn.silu(z_a) * att_a) @ w_branch_a
        att_b = sliding_window_sink_gqa(
            q_b.reshape(b, s, B_Q_HEADS, B_HEAD_DIM),
            k_b.reshape(b, s, B_KV_HEADS, B_HEAD_DIM),
            v_b.reshape(b, s, B_KV_HEADS, B_HEAD_DIM), t5_bias, sinks_b)
        u_b = (jax.nn.silu(z_b) * att_b) @ w_branch_b
        mixed = jax.nn.sigmoid(g_a) * u_a + jax.nn.sigmoid(g_b) * u_b
        x = x + mixed @ w_out
    return rmsnorm(x, final_gain)


_drawn_inputs = setup_inputs


def setup_inputs(seed=0):
    import zlib

    import numpy as np

    out = dict(_drawn_inputs(seed))
    spreads = {}
    factors = {'norm_gain': 8.0, 'rel_bias_a': 8.0, 't5_bias': 8.0, 'sinks_b': 8.0, 'final_gain': 5.57}
    for name, (base, spread) in spreads.items():
        noise = np.random.default_rng([zlib.crc32(name.encode()), seed]).standard_normal(out[name].shape)
        drawn = base * np.exp(spread * noise) if base else spread * noise
        out[name] = __import__('jax').numpy.asarray(drawn.astype(out[name].dtype))
    for name, factor in factors.items():
        out[name] = (out[name] * factor).astype(out[name].dtype)
    return out
```

```python
import math
from contextlib import ExitStack

import numpy as np

import concourse.bass as bass
from concourse import mybir

F32 = mybir.dt.float32
F32R = mybir.dt.float32r
ALU = mybir.AluOpType
ACT = mybir.ActivationFunctionType
AX = mybir.AxisListType

P = 128
HALF = 512
NEG = -1e30
EPS = 1e-6

D_MODEL, SEQ, CHUNK = 2048, 1024, 64
HEADS, HEAD_DIM = 16, 64
KV_HEADS = 2
A_PREV, B_PREV = 8, 1
REL_CLIP = 128
T5_BUCKETS, T5_MAX_DIST = 32, 128
WIDTH = HEADS * HEAD_DIM
KV_WIDTH = KV_HEADS * HEAD_DIM

PAIRS = HEADS // 2
KT = D_MODEL // P
QT = SEQ // P
SPAN = A_PREV * CHUNK // P + 1
PIECE = 8
COLS = PIECE * P
EXT = 3 * P
BIAS_ROWS = 2 * P

IN_WIDTHS = [WIDTH, WIDTH, WIDTH, WIDTH, WIDTH, KV_WIDTH, KV_WIDTH, WIDTH, D_MODEL, D_MODEL]
STARTS = [sum(IN_WIDTHS[:i]) // P for i in range(len(IN_WIDTHS))]
QA, KA, VA, ZA, QB, KB, VB, ZB, GA, GB = STARTS
GATES = 2 * D_MODEL // P

A_GATES, B_GATES = 2, 1
A_TILES = 4 + A_GATES
B_TILES = 2 + B_GATES
TAIL_TILES = GATES - PAIRS * (A_GATES + B_GATES)
OUT_BLOCKS = D_MODEL // HALF

A_PIECES = 2 * A_TILES
B_PIECES = 2 * B_TILES
AT_B0 = PAIRS * A_PIECES
AT_B = AT_B0 + 4
AT_TAIL = AT_B + PAIRS * B_PIECES
AT_MERGE = AT_TAIL + 2 * TAIL_TILES
AT_OUT = AT_MERGE + 2 * KT
PIECES = AT_OUT + OUT_BLOCKS * KT // 2
PER_PIECE = PIECE * 2 * 3

A_LEAD, B_LEAD = 3, 1
A_STEPS, B_STEPS = 2 * QT, QT
A_SLOTS = A_LEAD + A_STEPS + 2
B_SLOTS = B_LEAD + B_STEPS + 3


def in_tile_order():
    order = []
    for p in range(PAIRS):
        order += [VA + p, QA + p, KA + p, ZA + p] + [GA + A_GATES * p + j for j in range(A_GATES)]
    order += [VB, KB]
    for p in range(PAIRS):
        order += [QB + p, ZB + p] + [GA + A_GATES * PAIRS + B_GATES * p + j for j in range(B_GATES)]
    order += [GA + (A_GATES + B_GATES) * PAIRS + j for j in range(TAIL_TILES)]
    return order


def t5_bucket(rel_pos):
    nb = T5_BUCKETS // 2
    ret = (rel_pos > 0).astype(np.int32) * nb
    n = np.abs(rel_pos)
    exact = nb // 2
    large = exact + (np.log(np.maximum(n, 1) / exact) / np.log(T5_MAX_DIST / exact) * (nb - exact)).astype(np.int32)
    return (ret + np.where(n < exact, n, np.minimum(large, nb - 1))).astype(np.int32)


def selections():
    rel = 2 * P - 1 - np.arange(EXT)
    row = np.clip(rel, -REL_CLIP, REL_CLIP) + REL_CLIP - 1
    a = np.zeros((BIAS_ROWS, EXT), np.float32)
    n = np.arange(EXT)
    used = n < EXT - 1
    a[row[used], n[used]] = 1
    a[BIAS_ROWS - 1] -= used
    b = np.zeros((T5_BUCKETS, EXT), np.float32)
    b[t5_bucket(-rel)[used], n[used]] = 1
    return a, b


def masks():
    q = np.arange(P)[:, None] // CHUNK
    k = np.arange(2 * P)[None, :] // CHUNK - 2
    out = []
    for prev in (A_PREV, B_PREV):
        out.append(np.where((k <= q) & (k >= q - prev), 0.0, NEG).astype(np.float32))
    return np.stack(out, 1)


def at(i, per, base):
    return base if i is None else i * per + base


ROUND_TILES = A_TILES
ROUND_PAIRS_B = 2
B0_TILE, B_TILE = AT_B0 // 2, AT_B // 2
TAIL_TILE = AT_TAIL // 2
assert B_TILES * ROUND_PAIRS_B == ROUND_TILES and B0_TILE % 2 == B_TILE % 2 == TAIL_TILE % 2 == 0


def build(nc, x, gain, final_gain, weights, table_a, table_b, sinks, sel_a, sel_b, mask, ident_in, out):
    gates_dram = nc.dram_tensor("gates_dram", (GATES, P, SEQ), F32, kind="Internal").ap()
    gated_dram = nc.dram_tensor("gated_dram", (2 * PAIRS, P, SEQ), F32, kind="Internal").ap()
    bias_dram = nc.dram_tensor("bias_dram", (2, HEADS, P, 2 * P), F32, kind="Internal").ap()
    ext_dram = nc.dram_tensor("ext_dram", (2, HEADS, EXT), F32, kind="Internal").ap()

    with ExitStack() as ctx:
        place = [640]

        def sb(name, shape, dt=F32, where=None):
            size = 4 * math.prod(shape[1:])
            size += -size % 32
            start = place[0] if where is None else where[0]
            if where is None:
                place[0] += size
            else:
                where[0] += size
            return nc.alloc_sbuf_tensor_at(name, shape, dt, offset=start)

        def sem(name):
            return ctx.enter_context(nc.semaphore(name))

        act_hi = sb("act_hi", [P, KT, SEQ], F32R)
        act_lo = sb("act_lo", [P, KT, SEQ], F32R)
        raw = sb("raw", [P, 2, COLS])
        w_hi = sb("w_hi", [P, 2, COLS], F32R)
        w_lo = sb("w_lo", [P, 2, COLS], F32R)
        ident = sb("ident", [P, P])
        masks_sb = sb("masks_sb", [P, 2, 2 * P])
        gain_sb = sb("gain_sb", [P, KT])
        sig = sb("sig", [P, 2, HALF])
        small = sb("small", [P, 80])
        overlay = place[0]

        def over(name, shape, dt, tensor_at):
            return nc.alloc_sbuf_tensor_at(name, shape, dt, offset=tensor_at)

        x_sb = over("x_sb", [P, QT, D_MODEL], F32, overlay)
        w_hi_at, w_lo_at, raw_at = (640 + 8 * KT * SEQ + n * 8 * COLS for n in (1, 2, 0))
        sel_a_sb = over("sel_a_sb", [P, 2, EXT], F32, w_hi_at)
        sel_b_sb = over("sel_b_sb", [T5_BUCKETS, EXT], F32, w_hi_at + 4096)
        table_a_sb = over("table_a_sb", [P, 2, HEADS], F32, w_hi_at + 6144)
        table_b_sb = over("table_b_sb", [T5_BUCKETS, HEADS], F32, w_hi_at + 7168)
        ext_sb = over("ext_sb", [HEADS, 2, EXT], F32, w_lo_at)

        here = [overlay]
        q_stack = sb("q_stack", [P, 2, SEQ], F32R, where=here)
        k_hi2 = sb("k_hi2", [P, 2, SEQ], F32R, where=here)
        k_lo2 = sb("k_lo2", [P, 2, SEQ], F32R, where=here)
        v_parts = sb("v_parts", [P, QT, 2, 2, HEAD_DIM], F32R, where=here)
        vT = sb("vT", [P, SEQ], where=here)
        z_silu = sb("z_silu", [P, SEQ], where=here)
        probs = sb("probs", [P, 2, SPAN * P], where=here)
        pT_hi = sb("pT_hi", [P, 2, SPAN * P], F32R, where=here)
        pT_lo = sb("pT_lo", [P, 2, SPAN * P], F32R, where=here)
        o_rest = sb("o_rest", [P, 2, HEAD_DIM], where=here)
        o_pair = sb("o_pair", [P, 2, P], where=here)
        oT = sb("oT", [P, SEQ], where=here)
        bias = sb("bias", [P, 2, 2 * P], where=here)
        sink = sb("sink", [P, 2], where=here)
        att_end = here[0]

        mixed = over("mixed", [P, KT, SEQ], F32, overlay)
        y = over("y", [P, QT, D_MODEL], F32, overlay)
        final_gain_sb = over("final_gain_sb", [P, D_MODEL], F32, raw_at)
        end = max(att_end, overlay + 4 * KT * SEQ)
        assert end <= nc.sbuf_usable_end, (end, nc.sbuf_usable_end)

        sumsq = small[:, 0:QT]
        rms = small[:, QT:2 * QT]
        eps = small[:, 16:17]
        neg_max = small[:, 17:21]
        exp_sum = small[:, 21:25]
        exp_inv = small[:, 25:29]
        exp_sink = small[:, 29:33]
        part = small[:, 33:37]
        y_parts = small[:, 40:40 + QT * OUT_BLOCKS]
        y_stats = small[:, 72:80]

        ps = ctx.enter_context(nc.psum_tensor("ps", [P, 8, HALF], F32))
        flat = ps[:, :, :].rearrange("p b n -> p (b n)")
        TURN = 3
        S = flat[:, 3 * HALF:5 * HALF]
        T = flat[:, 5 * HALF:7 * HALF]
        O = flat[:, 7 * HALF:7 * HALF + 2 * P]
        OUT_T = flat[:, 7 * HALF + 2 * P:7 * HALF + 3 * P]

        x_ready = [sem(f"x_ready{t}") for t in range(QT)]
        consts_ready = sem("consts_ready")
        eps_ready = sem("eps_ready")
        squared = sem("squared")
        rooted = sem("rooted")
        rms_ready = sem("rms_ready")
        x_scaled = sem("x_scaled")
        x_turned = sem("x_turned")
        h_hi_ready = sem("h_hi_ready")
        h_ready = sem("h_ready")
        ext_made = sem("ext_made")
        ext_copied = sem("ext_copied")
        ext_stored = sem("ext_stored")
        windows_stored = sem("windows_stored")

        raw_ready = [sem("raw_ready0"), sem("raw_ready1")]
        hi_ready = sem("hi_ready")
        lo_ready = sem("lo_ready")
        piece_used = sem("piece_used")
        half_summed = sem("half_summed")
        bank_taken = [sem(f"bank_taken{b}") for b in range(3)]
        part_hi = sem("part_hi")

        vT_ready = sem("vT_ready")
        v_turned = sem("v_turned")
        v_hi_ready = sem("v_hi_ready")
        v_ready = sem("v_ready")
        k_doubled = sem("k_doubled")
        bias_ready = sem("bias_ready")
        bias_masked = sem("bias_masked")
        scores_ready = sem("scores_ready")
        biased = sem("biased")
        max_found = sem("max_found")
        max_ready = sem("max_ready")
        exp_ready = sem("exp_ready")
        sink_added = sem("sink_added")
        inv_ready = sem("inv_ready")
        turned = sem("turned")
        pT_hi_ready = sem("pT_hi_ready")
        pT_ready = sem("pT_ready")
        pv_ready = sem("pv_ready")
        rest_ready = sem("rest_ready")
        o_ready = sem("o_ready")
        oT_turned = sem("oT_turned")
        oT_ready = sem("oT_ready")
        gated_ready = sem("gated_ready")
        gated_stored = sem("gated_stored")
        exp_z = sem("exp_z")
        one_added = sem("one_added")
        sig_ready = sem("sig_ready")
        silu_ready = sem("silu_ready")
        gate_stored = [sem("gate_stored0"), sem("gate_stored1")]

        gated_loaded = [sem(f"gated_loaded{k}") for k in range(4)]
        conv_hi = sem("conv_hi")
        conv_ready = sem("conv_ready")
        gates_loaded = sem("gates_loaded")
        a_scaled = sem("a_scaled")
        b_scaled = sem("b_scaled")
        mixed_ready = sem("mixed_ready")
        residual_loaded = [sem(f"residual_loaded{b}") for b in range(OUT_BLOCKS)]
        bank_summed = sem("bank_summed")
        block_ready = sem("block_ready")
        y_ready = sem("y_ready")
        y_squared = sem("y_squared")
        y_summed = sem("y_summed")
        y_rooted = sem("y_rooted")
        y_inv = sem("y_inv")
        final_gain_loaded = sem("final_gain_loaded")
        y_scaled = sem("y_scaled")
        out_stored = sem("out_stored")

        SIGS_A = 2 * (1 + A_GATES)
        SIGS_B = 2 * (1 + B_GATES)
        BIASED_A = 2 * QT + 2 * (QT - SPAN + 1)

        def spans(t):
            return min(t + 1, SPAN)

        def raw_wait(eng, i, per, g):
            eng.wait_ge(raw_ready[g % 2], at(i, 8 * per, 16 * (g // 2 + 1)))

        def split_hi(act, i, per, g):
            raw_wait(act, i, per, g)
            if g >= 2 or i is not None:
                act.wait_ge(piece_used, at(i, per, g - 1))
            nc.scalar.activation(w_hi[:, g % 2], raw[:, g % 2], ACT.Copy).then_inc(hi_ready, 1)

        def split_lo(dve, i, per, g):
            dve.wait_ge(hi_ready, at(i, per, g + 1))
            nc.vector.tensor_tensor(w_lo[:, g % 2], raw[:, g % 2], w_hi[:, g % 2].bitcast(F32),
                                    ALU.subtract).then_inc(lo_ready, 1)

        def bank(tile, h):
            return (2 * tile + h) % TURN

        def project(pe, i, per, g, tile, first, last):
            b = g % 2
            if first >= last:
                return
            for n in range(first, last):
                h, k, m = n // (3 * PIECE), n // 3 % PIECE, n % 3
                if n == 0:
                    pe.wait_ge(lo_ready, at(i, per, g + 1))
                if b == 0 and n % (3 * PIECE) == 0 and (i is not None or 2 * tile + h >= TURN):
                    pe.wait_ge(bank_taken[bank(tile, h)], at(i, per // TURN, (2 * tile + h) // TURN))
                w, a = ((w_hi, act_hi), (w_hi, act_lo), (w_lo, act_hi))[m]
                kt = PIECE * b + k
                mm = nc.tensor.matmul(ps[:, bank(tile, h)], w[:, b, k * P:(k + 1) * P],
                                      a[:, kt, h * HALF:(h + 1) * HALF],
                                      start=(kt == 0 and m == 0), stop=(kt == KT - 1 and m == 2))
                if n == PER_PIECE - 1:
                    mm.then_inc(piece_used, 1)
                elif b and n == 3 * PIECE - 1:
                    mm.then_inc(half_summed, 1)

        def taken(eng, i, tile, h, per=2 * ROUND_TILES):
            eng.wait_ge(bank_taken[bank(tile, h)], at(i, per // TURN, (2 * tile + h) // TURN + 1))

        def half_done(eng, i, tile, h, per=2 * ROUND_TILES):
            if h == 0:
                eng.wait_ge(half_summed, at(i, per // 2, tile + 1))
            else:
                eng.wait_ge(piece_used, at(i, per, 2 * tile + 2))

        def a_step(s):
            t, a = s // 2, s % 2
            return t, a, (SPAN + 1 - spans(t)) * P

        def a_scores(pe, i, n0, s):
            t, a, c0 = a_step(s)
            if s == 0:
                for h in range(2):
                    taken(pe, i, 1, h)
                pe.wait_ge(k_doubled, at(i, 1, 1))
            pe.wait_ge(exp_ready, at(i, A_STEPS, n0 + s))
            for lo, hi in ((c0, 4 * P), (max(c0, 4 * P), 6 * P)):
                if lo >= hi:
                    continue
                keys = (t + 1) * P - 6 * P
                for j, k in enumerate((k_hi2, k_lo2)):
                    mm = nc.tensor.matmul(S[:, lo:hi], q_stack[:, a, t * P:(t + 1) * P],
                                          k[:, a, keys + lo:keys + hi], start=(j == 0), stop=(j == 1))
            mm.then_inc(scores_ready, 1)

        def a_softmax(dve, i, n0, s, b0):
            t, a, c0 = a_step(s)
            near = max(c0, 4 * P)
            if s == 0:
                dve.wait_ge(bias_masked, at(i, 1, 1))
            dve.wait_ge(scores_ready, at(i, A_STEPS, n0 + s + 1))
            nc.vector.tensor_tensor(S[:, near:6 * P], S[:, near:6 * P], bias[:, a, near - 4 * P:],
                                    ALU.add).then_inc(biased, 1)
            if t >= SPAN - 1:
                nc.vector.memset(S[CHUNK:, c0:c0 + CHUNK], NEG).then_inc(biased, 1)
            done = sum(1 + (r // 2 >= SPAN - 1) for r in range(s + 1))
            dve.wait_ge(biased, at(i, BIASED_A, b0 + done))
            nc.vector.tensor_reduce(neg_max[:, 2 * a:2 * a + 1], S[:, c0:6 * P], axis=AX.X, op=ALU.max,
                                    negate=True).then_inc(max_ready, 1)

        def a_exp(act, i, n0, s):
            t, a, c0 = a_step(s)
            act.wait_ge(max_ready, at(i, A_STEPS, n0 + s + 1))
            nc.scalar.activation(probs[:, s % 2, :6 * P - c0], S[:, c0:6 * P], ACT.Exp,
                                 bias=neg_max[:, 2 * a:2 * a + 1],
                                 accum_out=exp_sum[:, 2 * a:2 * a + 1]).then_inc(exp_ready, 1)

        def a_turn(pe, i, n0, s):
            t, a, c0 = a_step(s)
            pe.wait_ge(exp_ready, at(i, A_STEPS, n0 + s + 1))
            if s == 0:
                pe.wait_ge(v_ready, at(i, 1, 1))
            pe.wait_ge(pT_ready, at(i, A_STEPS, n0 + s))
            for j in range(spans(t)):
                tr = nc.tensor.transpose(T[:, j * P:(j + 1) * P], probs[:, s % 2, j * P:(j + 1) * P], ident[:, :])
            tr.then_inc(turned, 1)

        def turned_hi(act, i, per, n, cols):
            act.wait_ge(turned, at(i, per, n + 1))
            if n:
                act.wait_ge(pv_ready, at(i, per, n - 1))
            nc.scalar.activation(pT_hi[:, n % 2, :cols], T[:, :cols], ACT.Copy).then_inc(pT_hi_ready, 1)

        def turned_lo(dve, i, per, n, cols):
            dve.wait_ge(pT_hi_ready, at(i, per, n + 1))
            nc.vector.tensor_tensor(pT_lo[:, n % 2, :cols], T[:, :cols], pT_hi[:, n % 2, :cols].bitcast(F32),
                                    ALU.subtract).then_inc(pT_ready, 1)

        def a_inverse(dve, i, n0, s):
            a = s % 2
            dve.wait_ge(o_ready, at(i, A_STEPS, max(n0 + s - 1, 0)))
            dve.wait_ge(exp_ready, at(i, A_STEPS, n0 + s + 1))
            nc.vector.reciprocal(exp_inv[:, 2 * a:2 * a + 1], exp_sum[:, 2 * a:2 * a + 1]).then_inc(inv_ready, 1)

        def a_values(pe, i, n0, s):
            t, a, c0 = a_step(s)
            pe.wait_ge(pT_ready, at(i, A_STEPS, n0 + s + 1))
            if n0 + s:
                pe.wait_ge(o_ready, at(i, A_STEPS, n0 + s))
            for j in range(spans(t)):
                for r, part_of in enumerate((pT_hi, pT_lo)):
                    mm = nc.tensor.matmul(O[:, a * P:(a + 1) * P], part_of[:, s % 2, j * P:(j + 1) * P],
                                          v_parts[:, t + 1 - spans(t) + j, a].rearrange("p h d -> p (h d)"),
                                          start=(j == 0 and r == 0), stop=(j == spans(t) - 1 and r == 1))
            mm.then_inc(pv_ready, 1)

        def o_rest_of(act, i, n, heads):
            act.wait_ge(pv_ready, at(i, A_STEPS, n + 1))
            act.wait_ge(inv_ready, at(i, A_STEPS, n + 1))
            for a, col in heads:
                last = nc.scalar.activation(o_rest[:, a], O[:, a * P + HEAD_DIM:(a + 1) * P], ACT.Copy,
                                            scale=exp_inv[:, col:col + 1])
            last.then_inc(rest_ready, 1)

        def o_whole(dve, i, n, heads, t, pairs, m):
            dve.wait_ge(rest_ready, at(i, A_STEPS, n + 1))
            dve.wait_ge(oT_turned, at(i, QT * m, QT * pairs + max(t - 1, 0)))
            for a, col in heads:
                last = nc.vector.scalar_tensor_tensor(
                    o_pair[:, t % 2, a * HEAD_DIM:(a + 1) * HEAD_DIM], O[:, a * P:a * P + HEAD_DIM],
                    exp_inv[:, col:col + 1], o_rest[:, a], ALU.mult, ALU.add)
            last.then_inc(o_ready, 1)

        def o_turn(pe, i, n, t, pairs, m):
            pe.wait_ge(o_ready, at(i, A_STEPS, n + 1))
            pe.wait_ge(oT_ready, at(i, QT * m, QT * pairs + t))
            nc.tensor.transpose(OUT_T, o_pair[:, t % 2], ident[:, :]).then_inc(oT_turned, 1)

        def oT_take(act, i, t, pairs, m):
            act.wait_ge(oT_turned, at(i, QT * m, QT * pairs + t + 1))
            if t == 0:
                act.wait_ge(gated_stored, at(i, 16 * m, 16 * pairs))
            nc.scalar.activation(oT[:, t * P:(t + 1) * P], OUT_T, ACT.Copy).then_inc(oT_ready, 1)

        def b_scores(pe, i, n0, s, kv, q_tile):
            if s == 0:
                for h in range(2):
                    taken(pe, i, q_tile, h)
                pe.wait_ge(k_doubled, PAIRS + 1)
            pe.wait_ge(exp_ready, at(i, 2 * B_STEPS, n0 + s))
            c0 = P if s == 0 else 0
            keys = (s - 1) * P
            for a in range(2):
                for j, k in enumerate((k_hi2, k_lo2)):
                    mm = nc.tensor.matmul(S[:, a * HALF + c0:a * HALF + 2 * P], q_stack[:, a, s * P:(s + 1) * P],
                                          k[:, kv, keys + c0:keys + 2 * P], start=(j == 0), stop=(j == 1))
            mm.then_inc(scores_ready, 1)

        SB = S.rearrange("p (a n) -> p a n", a=2)

        def b_softmax(dve, i, n0, s, pair):
            c0 = P if s == 0 else 0
            n, before = n0 + s, pair * B_STEPS + s
            if s == 0:
                dve.wait_ge(bias_masked, at(i, 2, PAIRS + pair + 1))
            dve.wait_ge(scores_ready, at(i, 2 * B_STEPS, n + 1))
            nc.vector.tensor_tensor(SB[:, :, c0:2 * P], SB[:, :, c0:2 * P], bias[:, :, c0:], ALU.add)\
                .then_inc(biased, 1)
            dve.wait_ge(biased, at(i, 2 * B_STEPS, PAIRS * BIASED_A + before + 1))
            nc.vector.tensor_reduce(part[:, 0:2], SB[:, :, c0:2 * P], axis=AX.X, op=ALU.max, negate=True)\
                .then_inc(max_found, 1)
            dve.wait_ge(max_found, at(i, 2 * B_STEPS, before + 1))
            nc.vector.scalar_tensor_tensor(neg_max[:, 2 * (n % 2):2 * (n % 2) + 2], sink[:, :], -1.0,
                                           part[:, 0:2], ALU.mult, ALU.min).then_inc(max_ready, 1)

        def b_exp(act, i, n0, s):
            c0 = P if s == 0 else 0
            n = n0 + s
            act.wait_ge(max_ready, at(i, 2 * B_STEPS, n + 1))
            for a in range(2):
                col = 2 * (n % 2) + a
                nc.scalar.activation(exp_sink[:, col:col + 1], sink[:, a:a + 1], ACT.Exp,
                                     bias=neg_max[:, col:col + 1])
                last = nc.scalar.activation(probs[:, n % 2, a * 2 * P + c0:(a + 1) * 2 * P],
                                            S[:, a * HALF + c0:a * HALF + 2 * P], ACT.Exp,
                                            bias=neg_max[:, col:col + 1],
                                            accum_out=exp_sum[:, col:col + 1])
            last.then_inc(exp_ready, 1)

        def b_turn(pe, i, n0, s):
            n = n0 + s
            if s == 0:
                pe.wait_ge(v_ready, PAIRS + 1)
            pe.wait_ge(exp_ready, at(i, 2 * B_STEPS, n0 + s + 1))
            pe.wait_ge(pT_ready, at(i, 2 * B_STEPS, n0 + s))
            for j in range(4):
                if s or j % 2:
                    tr = nc.tensor.transpose(T[:, j * P:(j + 1) * P], probs[:, n % 2, j * P:(j + 1) * P], ident[:, :])
            tr.then_inc(turned, 1)

        def b_turned(s, n, buf):
            return buf.rearrange("p (j n) -> p j n", n=P)[:, (1 - min(s, 1)):4:(2 if s == 0 else 1)]

        def b_turned_hi(act, i, n0, s):
            n = n0 + s
            act.wait_ge(turned, at(i, 2 * B_STEPS, n + 1))
            act.wait_ge(pv_ready, at(i, 2 * B_STEPS, n - 1))
            nc.scalar.activation(b_turned(s, n, pT_hi[:, n % 2, :4 * P]), b_turned(s, n, T[:, :4 * P]), ACT.Copy)\
                .then_inc(pT_hi_ready, 1)

        def b_turned_lo(dve, i, n0, s):
            n = n0 + s
            dve.wait_ge(pT_hi_ready, at(i, 2 * B_STEPS, n + 1))
            nc.vector.tensor_tensor(b_turned(s, n, pT_lo[:, n % 2, :4 * P]), b_turned(s, n, T[:, :4 * P]),
                                    b_turned(s, n, pT_hi[:, n % 2, :4 * P]).bitcast(F32), ALU.subtract)\
                .then_inc(pT_ready, 1)

        def b_inverse(dve, i, n0, s, pair):
            two = slice(2 * ((n0 + s) % 2), 2 * ((n0 + s) % 2) + 2)
            dve.wait_ge(o_ready, at(i, 2 * B_STEPS, n0 + s - 1))
            dve.wait_ge(exp_ready, at(i, 2 * B_STEPS, n0 + s + 1))
            nc.vector.tensor_tensor(part[:, 2:4], exp_sum[:, two], exp_sink[:, two], ALU.add).then_inc(sink_added, 1)
            dve.wait_ge(sink_added, at(i, 2 * B_STEPS, pair * B_STEPS + s + 1))
            nc.vector.reciprocal(exp_inv[:, two], part[:, 2:4]).then_inc(inv_ready, 1)

        def b_values(pe, i, n0, s, kv):
            n = n0 + s
            pe.wait_ge(pT_ready, at(i, 2 * B_STEPS, n + 1))
            pe.wait_ge(o_ready, at(i, 2 * B_STEPS, n))
            for a in range(2):
                tiles = (1,) if s == 0 else (0, 1)
                for j in tiles:
                    for r, part_of in enumerate((pT_hi, pT_lo)):
                        c = (2 * a + j) * P
                        mm = nc.tensor.matmul(O[:, a * P:(a + 1) * P], part_of[:, n % 2, c:c + P],
                                              v_parts[:, s - 1 + j, kv].rearrange("p h d -> p (h d)"),
                                              start=(j == tiles[0] and r == 0), stop=(j == 1 and r == 1))
            mm.then_inc(pv_ready, 1)

        def q_hi(act, i, tile, h):
            half_done(act, i, tile, h)
            for a in range(2):
                last = nc.scalar.activation(q_stack[0:64, a, h * HALF:(h + 1) * HALF],
                                            ps[a * 64:a * 64 + 64, bank(tile, h)], ACT.Copy,
                                            scale=HEAD_DIM ** -0.5)
            last.then_inc(part_hi, 1)

        def q_lo(dve, i, n, tile, h):
            dve.wait_ge(part_hi, at(i, 4, n))
            for a in range(2):
                last = nc.vector.scalar_tensor_tensor(
                    q_stack[64:128, a, h * HALF:(h + 1) * HALF], ps[a * 64:a * 64 + 64, bank(tile, h)],
                    HEAD_DIM ** -0.5, q_stack[0:64, a, h * HALF:(h + 1) * HALF].bitcast(F32),
                    ALU.mult, ALU.subtract)
            last.then_inc(bank_taken[bank(tile, h)], 1)

        def k_hi(act, i, tile, h):
            half_done(act, i, tile, h)
            for a in range(2):
                last = nc.scalar.activation(k_hi2[0:64, a, h * HALF:(h + 1) * HALF],
                                            ps[a * 64:a * 64 + 64, bank(tile, h)], ACT.Copy)
            last.then_inc(part_hi, 1)

        def k_lo(dve, i, n, tile, h):
            dve.wait_ge(part_hi, at(i, 4, n))
            for a in range(2):
                last = nc.vector.tensor_tensor(
                    k_lo2[0:64, a, h * HALF:(h + 1) * HALF], ps[a * 64:a * 64 + 64, bank(tile, h)],
                    k_hi2[0:64, a, h * HALF:(h + 1) * HALF].bitcast(F32), ALU.subtract)
            last.then_inc(bank_taken[bank(tile, h)], 1)

        def k_double(dve, i, tile):
            for h in range(2):
                taken(dve, i, tile, h)
            for k in (k_hi2, k_lo2):
                last = nc.vector.tensor_copy(k[64:128, :, :], k[0:64, :, :])
            last.then_inc(k_doubled, 1)

        def v_copy(dve, i, tile, h):
            half_done(dve, i, tile, h)
            nc.vector.tensor_copy(vT[:, h * HALF:(h + 1) * HALF], ps[:, bank(tile, h)])\
                .then_inc(bank_taken[bank(tile, h)], 1)

        def v_turn(pe, i, tile, pairs):
            for h in range(2):
                taken(pe, i, tile, h)
            pe.wait_ge(oT_ready, at(i, QT, QT * pairs))
            for t in range(QT):
                tr = nc.tensor.transpose(T[:, t * P:(t + 1) * P], vT[:, t * P:(t + 1) * P], ident[:, :])
            tr.then_inc(v_turned, 1)

        v_view = v_parts[:, :, :, :, :].rearrange("p t a h d -> p (t a) h d")
        T_view = T.rearrange("p (m d) -> p m d", d=HEAD_DIM)

        def v_hi(act, i, n):
            act.wait_ge(v_turned, at(i, 1, n + 1))
            nc.scalar.activation(v_view[:, :, 0, :], T_view, ACT.Copy).then_inc(v_hi_ready, 1)

        def v_lo(dve, i, n):
            dve.wait_ge(v_hi_ready, at(i, 1, n + 1))
            nc.vector.tensor_tensor(v_view[:, :, 1, :], T_view, v_view[:, :, 0, :].bitcast(F32),
                                    ALU.subtract).then_inc(v_ready, 1)

        def z_exp(act, i, tile, h, gates, m):
            half_done(act, i, tile, h)
            act.wait_ge(gate_stored[h], at(i, 16 * m, 16 * gates))
            nc.scalar.activation(sig[:, h], ps[:, bank(tile, h)], ACT.Exp, scale=-1.0).then_inc(exp_z, 1)

        def gate_exp(act, i, tile, h, gates=None, m=0, z_tile=None, per=2 * ROUND_TILES):
            half_done(act, i, tile, h, per)
            if z_tile is None:
                act.wait_ge(gate_stored[h], at(i, 16 * m, 16 * gates))
            else:
                taken(act, i, z_tile, h)
            nc.scalar.activation(sig[:, h], ps[:, bank(tile, h)], ACT.Exp, scale=-1.0)\
                .then_inc(bank_taken[bank(tile, h)], 1)

        def sig_inverse(dve, i, n, per, tile, h, z=None):
            if z:
                dve.wait_ge(exp_z, at(i, z[1], z[0] + h + 1))
            else:
                taken(dve, i, tile, h)
            nc.vector.tensor_scalar(sig[:, h], sig[:, h], 1.0, None, ALU.add).then_inc(one_added, 1)
            dve.wait_ge(one_added, at(i, per, n + h + 1))
            nc.vector.reciprocal(sig[:, h], sig[:, h]).then_inc(sig_ready, 1)
            if z:
                dve.wait_ge(sig_ready, at(i, per, n + h + 1))
                nc.vector.tensor_tensor(z_silu[:, h * HALF:(h + 1) * HALF], ps[:, bank(tile, h)],
                                        sig[:, h], ALU.mult).then_inc(bank_taken[bank(tile, h)], 1)

        def gate_store(act, i, n, per, gate, per_gate, h):
            act.wait_ge(sig_ready, at(i, per, n + h + 1))
            act.dma_start(gates_dram[at(i, per_gate, gate), :, h * HALF:(h + 1) * HALF], sig[:, h])\
                .then_inc(gate_stored[h], 16)

        def gate_pair(pool, i, pairs, m, z_tile):
            for h in range(2):
                taken(pool, i, z_tile, h)
            pool.wait_ge(oT_ready, at(i, QT * m, QT * (pairs + 1)))
            nc.gpsimd.tensor_tensor(oT[:, :], oT[:, :], z_silu[:, :], ALU.mult).then_inc(gated_ready, 1)

        def pair_store(act, i, pairs, m):
            act.wait_ge(gated_ready, at(i, m, pairs + 1))
            act.dma_start(gated_dram[at(i, m, pairs)], oT[:, :]).then_inc(gated_stored, 16)

        def mask_bias(pool, i, mixer, loads, per, n):
            pool.wait_ge(bias_ready, at(i, per, loads))
            for a in range(2):
                last = nc.gpsimd.tensor_tensor(bias[:, a], bias[:, a], masks_sb[:, mixer], ALU.add)
            last.then_inc(bias_masked, 1)

        def slot_tasks(slots, tiles):
            total = tiles * 2 * PER_PIECE

            def after(products):
                return next(s for s in range(slots + 1) if s * total // slots >= products)

            splits = {after(c * PER_PIECE): c for c in range(2 * tiles)}
            takes = {after((4 * m + 3 + h) * PER_PIECE // 2): (m, h) for m in range(tiles) for h in range(2)}
            assert len(splits) == 2 * tiles and len(takes) == 2 * tiles
            return splits, takes

        A_LATE, B_LATE = 1 + A_GATES, 1 + B_GATES
        A_SPLITS, A_TAKES = slot_tasks(A_SLOTS, A_LATE)
        B_SPLITS, B_TAKES = slot_tasks(B_SLOTS, B_LATE)
        A_FIRST, B_FIRST = A_PIECES - 2 * A_LATE, B_PIECES - 2 * B_LATE
        PER = 2 * ROUND_TILES
        GATES_BEFORE_B = PAIRS * A_GATES
        B_ROUNDS = PAIRS // KV_HEADS // ROUND_PAIRS_B
        A_DONE = PAIRS * A_STEPS

        def slot_share(pe, i, slot, slots, tiles, g0):
            total = tiles * 2 * PER_PIECE
            first, last = slot * total // slots, (slot + 1) * total // slots
            for c in range(2 * tiles):
                project(pe, i, PER, g0 + c, (g0 + c) // 2, max(first - c * PER_PIECE, 0),
                        min(last - c * PER_PIECE, PER_PIECE))

        def b_rounds():
            for kv in range(KV_HEADS):
                yield kv, kv * (PAIRS // KV_HEADS)

        block = ctx.enter_context(nc.Block())

        @block.sync
        def _(sp):
            for t in range(QT):
                sp.dma_start(x_sb[:, t, :], x[0, t * P:(t + 1) * P, :]).then_inc(x_ready[t], 16)

            def load(i, per, g):
                if g >= 2:
                    sp.wait_ge(lo_ready, at(i, per, g - 1))
                sp.dma_start(raw[:, g % 2], weights[at(i, per, g)]).then_inc(raw_ready[g % 2], 16)

            load(None, 0, 0)
            load(None, 0, 1)
            sp.wait_ge(ext_copied, 2)
            sp.dma_start(ext_dram.rearrange("m h n -> h m n"), ext_sb[:, :, :]).then_inc(ext_stored, 16)
            sp.wait_ge(ext_stored, 16)
            for mixer in range(2):
                rows = bass.AP(ext_dram.tensor, mixer * HEADS * EXT + P - 1, [[EXT, HEADS], [-1, P], [1, 2 * P]])
                sp.dma_start(bias_dram[mixer], rows).then_inc(windows_stored, 16)
            sp.wait_ge(windows_stored, 32)

            with sp.Fori(0, PAIRS) as i:
                for c in range(A_PIECES):
                    if c == 2:
                        sp.wait_ge(biased, at(i, BIASED_A, 0))
                        sp.dma_start(bias[:, :, :], bias_dram[0, bass.ds(2 * i, 2)].rearrange("h p n -> p h n"))\
                            .then_inc(bias_ready, 16)
                    load(i, PER, 2 + c)
            for c in range(4):
                load(None, 0, AT_B0 + 2 + c)
            for kv, before in b_rounds():
                with sp.Fori(0, B_ROUNDS) as i:
                    for u in range(ROUND_PAIRS_B):
                        pair = before + u
                        head = i * 4 + 2 * pair
                        sp.wait_ge(exp_ready, at(i, 2 * B_STEPS, A_DONE + pair * B_STEPS))
                        sp.dma_start(bias[:, :, :], bias_dram[1, bass.ds(head, 2)].rearrange("h p n -> p h n"))\
                            .then_inc(bias_ready, 16)
                        sp.dma_start(sink[:, :], sinks[bass.ds(head, 2)].partition_broadcast(P))\
                            .then_inc(bias_ready, 16)
                        for c in range(B_PIECES):
                            load(i, PER, AT_B + pair * B_PIECES + 2 + c)
            for c in range(2 * TAIL_TILES):
                load(None, 0, AT_TAIL + 2 + c)
                if c % 2 and c < 8:
                    sp.wait_ge(gated_stored, 16 * 2 * PAIRS)
                    k = 4 * (c // 2)
                    sp.dma_start(mixed[:, k:k + 4], gated_dram[k:k + 4].rearrange("k p n -> p k n"))\
                        .then_inc(gated_loaded[c // 2], 16)

            def load_gates(i, m):
                for b in range(2):
                    load(i, 4, AT_MERGE + 2 + 2 * m + b)
                for h in range(2):
                    n = 2 * m + h
                    if i is not None or n:
                        sp.wait_ge(mixed_ready, at(i, 4, n))
                    for branch in range(2):
                        sp.dma_start(sig[:, branch],
                                     gates_dram[at(i, 2, branch * KT + m), :, h * HALF:(h + 1) * HALF])\
                            .then_inc(gates_loaded, 16)

            for b in range(2):
                sp.wait_ge(gate_stored[b], 16 * GATES)
            for m in range(2):
                load_gates(None, m)
            with sp.Fori(1, KT // 2) as i:
                for m in range(2):
                    load_gates(i, m)
            for c in range(KT // 2):
                load(None, 0, AT_OUT + 2 + c)
                if c == 3:
                    sp.wait_ge(conv_ready, 2 * KT)
                    for b in range(OUT_BLOCKS):
                        sp.dma_start(y[:, :, b * HALF:(b + 1) * HALF],
                                     x[0].rearrange("(t p) n -> p t n", p=P)[:, :, b * HALF:(b + 1) * HALF])\
                            .then_inc(residual_loaded[b], 16)
            with sp.Fori(1, OUT_BLOCKS - 1) as i:
                for c in range(KT // 2):
                    load(i, KT // 2, AT_OUT + 2 + c)
            for g in range(AT_OUT + (OUT_BLOCKS - 1) * KT // 2 + 2, PIECES):
                load(None, 0, g)
            sp.wait_ge(lo_ready, PIECES)
            sp.dma_start(final_gain_sb[:, :], final_gain.partition_broadcast(P)).then_inc(final_gain_loaded, 16)
            for t in range(QT):
                sp.wait_ge(y_scaled, t + 1)
                sp.dma_start(out[0, t * P:(t + 1) * P, :], y[:, t, :]).then_inc(out_stored, 16)
            sp.wait_ge(out_stored, 16 * QT)

        @block.tensor
        def _(pe):
            pe.wait_ge(consts_ready, 16 * 7)
            for r in range(2):
                mm = nc.tensor.matmul(ps[:HEADS, 0, :EXT], table_a_sb[:, r], sel_a_sb[:, r], start=(r == 0), stop=(r == 1))
            mm.then_inc(ext_made, 1)
            nc.tensor.matmul(ps[:HEADS, 1, :EXT], table_b_sb[:, :], sel_b_sb[:, :], start=True, stop=True)\
                .then_inc(ext_made, 1)
            pe.wait_ge(ext_copied, 2)
            for half in range(2):
                for t in range(4):
                    pe.wait_ge(x_scaled, 4 * half + t + 1)
                for k in range(KT):
                    n = half * KT + k
                    if n >= 4:
                        pe.wait_ge(h_ready, n - 3)
                    for t in range(4):
                        tr = nc.tensor.transpose(ps[:, n % 4, t * P:(t + 1) * P],
                                                 x_sb[:, 4 * half + t, k * P:(k + 1) * P], ident[:, :])
                    tr.then_inc(x_turned, 1)
            pe.wait_ge(h_ready, 2 * KT)

            with pe.Fori(0, PAIRS) as i:
                for c in range(A_FIRST):
                    if c == 3:
                        v_turn(pe, i, 0, 0)
                    project(pe, i, PER, c, c // 2, 0, PER_PIECE)
                for slot in range(A_SLOTS):
                    s = slot - A_LEAD
                    if 0 <= s < A_STEPS:
                        a_scores(pe, i, 0, s)
                    if 1 <= s <= A_STEPS:
                        a_turn(pe, i, 0, s - 1)
                    if 2 <= s <= A_STEPS + 1:
                        a_values(pe, i, 0, s - 2)
                    if s >= 4 and s % 2 == 0:
                        o_turn(pe, i, s - 3, (s - 4) // 2, 0, 1)
                    slot_share(pe, i, slot, A_SLOTS, A_LATE, A_FIRST)
                o_turn(pe, i, A_STEPS - 1, QT - 1, 0, 1)

            for c in range(4):
                if c == 3:
                    v_turn(pe, None, B0_TILE, PAIRS)
                project(pe, None, 0, AT_B0 + c, B0_TILE + c // 2, 0, PER_PIECE)
            for kv, before in b_rounds():
                with pe.Fori(0, B_ROUNDS) as i:
                    for u in range(ROUND_PAIRS_B):
                        pair = before + u
                        g0, n0 = AT_B + pair * B_PIECES, A_DONE + pair * B_STEPS
                        for c in range(B_FIRST):
                            project(pe, i, PER, g0 + c, (g0 + c) // 2, 0, PER_PIECE)
                        for slot in range(B_SLOTS):
                            s = slot - B_LEAD
                            if 0 <= s < B_STEPS:
                                b_scores(pe, i, n0, s, kv, g0 // 2)
                            if 1 <= s <= B_STEPS:
                                b_turn(pe, i, n0, s - 1)
                            if 2 <= s <= B_STEPS + 1:
                                b_values(pe, i, n0, s - 2, kv)
                            if s >= 3:
                                o_turn(pe, i, n0 + s - 3, s - 3, PAIRS + pair, 2)
                            slot_share(pe, i, slot, B_SLOTS, B_LATE, g0 + B_FIRST)

            with pe.Fori(0, TAIL_TILES // TURN) as i:
                for c in range(2 * TURN):
                    project(pe, i, 2 * TURN, AT_TAIL + c, TAIL_TILE + c // 2, 0, PER_PIECE)
            for c in range(2 * (TAIL_TILES - TAIL_TILES % TURN), 2 * TAIL_TILES):
                project(pe, None, 0, AT_TAIL + c, TAIL_TILE + c // 2, 0, PER_PIECE)

            def merge_piece(i, c):
                g, tile, branch = AT_MERGE + c, c // 2, c % 2
                pe.wait_ge(lo_ready, at(i, 4, g + 1))
                if i is None and tile == 0:
                    for h in range(2 * (TAIL_TILE + TAIL_TILES) - TURN, 2 * (TAIL_TILE + TAIL_TILES)):
                        taken(pe, None, h // 2, h % 2)
                    pe.wait_ge(oT_ready, QT * 2 * PAIRS)
                elif i is None:
                    pass
                else:
                    pe.wait_ge(a_scaled if branch == 0 else b_scaled, at(i, 4, 2 * tile - 2))
                for k in range(PIECE):
                    if i is None and tile == 0:
                        pe.wait_ge(conv_ready, PIECE * branch + k + 1)
                    for m, (w, a, half) in enumerate(((w_hi, act_hi, 0), (w_hi, act_lo, 0), (w_hi, act_hi, 1),
                                                      (w_hi, act_lo, 1), (w_lo, act_hi, 0), (w_lo, act_hi, 1))):
                        mm = nc.tensor.matmul(ps[:, 4 * tile + 2 * branch + half], w[:, g % 2, k * P:(k + 1) * P],
                                              a[:, PIECE * branch + k, half * HALF:(half + 1) * HALF],
                                              start=(k == 0 and m in (0, 2)), stop=(k == PIECE - 1 and m >= 4))
                mm.then_inc(piece_used, 1)

            for c in range(4):
                merge_piece(None, c)
            with pe.Fori(1, KT // 2) as i:
                for c in range(4):
                    merge_piece(i, c)

            def out_block(i):
                for c in range(KT // 2):
                    g = AT_OUT + c
                    pe.wait_ge(lo_ready, at(i, KT // 2, g + 1))
                    if i is None:
                        pe.wait_ge(conv_ready, KT + 2 * c + 2)
                    for t in range(QT):
                        if c == 0 and i is None:
                            pe.wait_ge(b_scaled, 2 * KT - (2 if t < 4 else 0))
                        elif c == 0:
                            pe.wait_ge(block_ready, at(i, QT, t + 1 - QT))
                        for kk in range(2):
                            k = 2 * c + kk
                            for m, (a, w) in enumerate(((act_hi, w_hi), (act_hi, w_lo), (act_lo, w_hi))):
                                mm = nc.tensor.matmul(ps[:, t], a[:, k, t * P:(t + 1) * P],
                                                      w[:, g % 2, kk * HALF:(kk + 1) * HALF],
                                                      start=(k == 0 and m == 0), stop=(k == KT - 1 and m == 2))
                        if t == QT - 1:
                            mm.then_inc(piece_used, 1)
                        elif c == KT // 2 - 1:
                            mm.then_inc(bank_summed, 1)

            out_block(None)
            with pe.Fori(1, OUT_BLOCKS) as i:
                out_block(i)

        @block.scalar
        def _(act):
            act.dma_start(table_a_sb[:, :, :], table_a).then_inc(consts_ready, 16)
            act.dma_start(sel_a_sb[:, :, :], sel_a).then_inc(consts_ready, 16)
            act.dma_start(table_b_sb[:, :], table_b).then_inc(consts_ready, 16)
            act.dma_start(sel_b_sb[:, :], sel_b).then_inc(consts_ready, 16)
            act.dma_start(ident[:, :], ident_in).then_inc(consts_ready, 16)
            act.dma_start(masks_sb[:, :, :], mask).then_inc(consts_ready, 16)
            act.dma_start(gain_sb[:, :], gain).then_inc(consts_ready, 16)
            act.wait_ge(eps_ready, 1)

            def square(t):
                act.wait_ge(x_ready[t], 16)
                nc.scalar.activation(flat[:, 4 * HALF:8 * HALF], x_sb[:, t, :], ACT.Square,
                                     accum_out=sumsq[:, t:t + 1]).then_inc(squared, 1)
                act.wait_ge(squared, t + 1)
                nc.scalar.activation(rms[:, t:t + 1], sumsq[:, t:t + 1], ACT.Sqrt, bias=eps[:, :],
                                     scale=1.0 / D_MODEL).then_inc(rooted, 1)

            for t in range(4):
                square(t)
            for n in range(2 * KT):
                half, k = divmod(n, KT)
                if half == 0 and k % 4 == 0:
                    square(4 + k // 4)
                act.wait_ge(x_turned, n + 1)
                if n == 0:
                    act.wait_ge(consts_ready, 16 * 7)
                nc.scalar.activation(act_hi[:, k, half * HALF:(half + 1) * HALF], ps[:, n % 4], ACT.Copy,
                                     scale=gain_sb[:, k:k + 1]).then_inc(h_hi_ready, 1)
            act.wait_ge(windows_stored, 32)
            split_hi(act, None, 0, 0)

            with act.Fori(0, PAIRS) as i:
                for c in range(A_FIRST):
                    split_hi(act, i, PER, c + 1)
                    if c == 3:
                        v_hi(act, i, 0)
                        q_hi(act, i, 1, 0)
                    if c == 4:
                        q_hi(act, i, 1, 1)
                    if c == 5:
                        k_hi(act, i, 2, 0)
                for slot in range(A_SLOTS + 3):
                    s = slot - A_LEAD
                    if 1 <= s <= A_STEPS:
                        turned_hi(act, i, A_STEPS, s - 1, spans((s - 1) // 2) * P)
                    if 4 <= s <= A_STEPS + 2 and s % 2 == 0:
                        oT_take(act, i, (s - 4) // 2, 0, 1)
                    if 2 <= s <= A_STEPS + 1:
                        o_rest_of(act, i, s - 2, [(s % 2, 2 * (s % 2))])
                    if 0 <= s < A_STEPS:
                        a_exp(act, i, 0, s)
                    if slot in A_SPLITS:
                        split_hi(act, i, PER, A_FIRST + A_SPLITS[slot] + 1)
                    if slot == 0:
                        k_hi(act, i, 2, 1)
                    m, h = A_TAKES.get(slot, (None, 0))
                    if m == 0:
                        z_exp(act, i, 3, h, 0, A_GATES)
                    elif m:
                        gate_exp(act, i, 3 + m, h, m - 1, A_GATES, 3 if m == 1 else None)
                    m, h = A_TAKES.get(slot - 2, (None, 0))
                    if m:
                        gate_store(act, i, 2 * m, SIGS_A, m - 1, A_GATES, h)
                pair_store(act, i, 0, 1)

            for c in range(4):
                split_hi(act, None, 0, AT_B0 + c + 1)
                if c == 3:
                    v_hi(act, None, PAIRS)
                    k_hi(act, None, B0_TILE + 1, 0)
            k_hi(act, None, B0_TILE + 1, 1)
            for kv, before in b_rounds():
                with act.Fori(0, B_ROUNDS) as i:
                    for u in range(ROUND_PAIRS_B):
                        pair = before + u
                        g0, n0 = AT_B + pair * B_PIECES, A_DONE + pair * B_STEPS
                        sigs = PAIRS * SIGS_A + pair * SIGS_B
                        gate = GATES_BEFORE_B + pair
                        for c in range(B_FIRST):
                            split_hi(act, i, PER, g0 + c + 1)
                        q_hi(act, i, g0 // 2, 0)
                        for slot in range(B_SLOTS + 3):
                            s = slot - B_LEAD
                            if 1 <= s <= B_STEPS:
                                b_turned_hi(act, i, n0, s - 1)
                            if 3 <= s <= B_STEPS + 2:
                                oT_take(act, i, s - 3, PAIRS + pair, 2)
                            if 2 <= s <= B_STEPS + 1:
                                n = n0 + s - 2
                                o_rest_of(act, i, n, [(a, 2 * (n % 2) + a) for a in range(2)])
                            if 0 <= s < B_STEPS:
                                b_exp(act, i, n0, s)
                            if slot in B_SPLITS:
                                split_hi(act, i, PER, g0 + B_FIRST + B_SPLITS[slot] + 1)
                            if slot == 0:
                                q_hi(act, i, g0 // 2, 1)
                            m, h = B_TAKES.get(slot, (None, 0))
                            if m == 0:
                                z_exp(act, i, g0 // 2 + 1, h, gate, 2)
                            elif m:
                                gate_exp(act, i, g0 // 2 + 2, h, z_tile=g0 // 2 + 1)
                            m, h = B_TAKES.get(slot - 2, (None, 0))
                            if m:
                                gate_store(act, i, sigs + 2, 2 * SIGS_B, gate, 2, h)
                        pair_store(act, i, PAIRS + pair, 2)

            sigs = PAIRS * (SIGS_A + SIGS_B)
            for c in range(2 * TAIL_TILES + 1):
                if c < 2 * TAIL_TILES:
                    split_hi(act, None, 0, AT_TAIL + c + 1)
                if c:
                    j, h = (c - 1) // 2, (c - 1) % 2
                    gate_exp(act, None, TAIL_TILE + j, h, GATES - TAIL_TILES + j)
                    gate_store(act, None, sigs + 2 * j, 0, GATES - TAIL_TILES + j, 0, h)

            split_hi(act, None, 0, AT_MERGE + 1)
            act.wait_ge(piece_used, AT_MERGE)
            for k in range(KT):
                act.wait_ge(gated_loaded[k // 4], 16)
                nc.scalar.activation(act_hi[:, k], mixed[:, k], ACT.Copy).then_inc(conv_hi, 1)
            for c in range(1, 4):
                split_hi(act, None, 0, AT_MERGE + c + 1)
            with act.Fori(1, KT // 2) as i:
                for c in range(4):
                    split_hi(act, i, 4, AT_MERGE + c + 1)

            def squares(b, t):
                if QT * b + t >= 2:
                    act.wait_ge(y_squared, QT * b + t - 1)
                act.wait_ge(block_ready, QT * b + t + 1)
                nc.scalar.activation(sig[:, t % 2], y[:, t, b * HALF:(b + 1) * HALF], ACT.Square,
                                     accum_out=y_parts[:, t * OUT_BLOCKS + b:t * OUT_BLOCKS + b + 1])\
                    .then_inc(y_squared, 1)

            act.wait_ge(mixed_ready, 2 * KT)
            for b in range(OUT_BLOCKS):
                for c in range(KT // 2):
                    g = AT_OUT + b * KT // 2 + c + 1
                    if g < PIECES:
                        split_hi(act, None, 0, g)
                    if b == 0 and c == 0:
                        act.wait_ge(piece_used, AT_OUT)
                        for k in range(KT):
                            nc.scalar.activation(act_hi[:, k], mixed[:, k], ACT.Copy).then_inc(conv_hi, 1)
                    if b and c == 0:
                        for t in range(QT):
                            squares(b - 1, t)
            for t in range(QT + 1):
                if t < QT:
                    squares(OUT_BLOCKS - 1, t)
                if t:
                    act.wait_ge(y_summed, t)
                    nc.scalar.activation(rms[:, t - 1:t], y_stats[:, t - 1:t], ACT.Sqrt, bias=eps[:, :],
                                         scale=1.0 / D_MODEL).then_inc(y_rooted, 1)

        @block.vector
        def _(dve):
            nc.vector.memset(eps[:, :], EPS).then_inc(eps_ready, 1)
            for m in range(2):
                dve.wait_ge(ext_made, m + 1)
                nc.vector.tensor_copy(ext_sb[:, m], ps[:HEADS, m, :EXT]).then_inc(ext_copied, 1)

            def scale_x(t):
                dve.wait_ge(rooted, t + 1)
                nc.vector.reciprocal(rms[:, t:t + 1], rms[:, t:t + 1]).then_inc(rms_ready, 1)
                dve.wait_ge(rms_ready, t + 1)
                nc.vector.tensor_scalar(x_sb[:, t, :], x_sb[:, t, :], rms[:, t:t + 1], None, ALU.mult)\
                    .then_inc(x_scaled, 1)

            for t in range(4):
                scale_x(t)
            for n in range(2 * KT):
                half, k = divmod(n, KT)
                if half == 0 and k % 4 == 0:
                    scale_x(4 + k // 4)
                dve.wait_ge(h_hi_ready, n + 1)
                part_of = slice(half * HALF, (half + 1) * HALF)
                nc.vector.scalar_tensor_tensor(act_lo[:, k, part_of], ps[:, n % 4], gain_sb[:, k:k + 1],
                                               act_hi[:, k, part_of].bitcast(F32), ALU.mult, ALU.subtract)\
                    .then_inc(h_ready, 1)
            split_lo(dve, None, 0, 0)

            with dve.Fori(0, PAIRS) as i:
                for c in range(A_FIRST):
                    split_lo(dve, i, PER, c + 1)
                    if c in (1, 2):
                        v_copy(dve, i, 0, c - 1)
                    if c == 3:
                        v_lo(dve, i, 0)
                        q_lo(dve, i, 1, 1, 0)
                    if c == 4:
                        q_lo(dve, i, 2, 1, 1)
                    if c == 5:
                        k_lo(dve, i, 3, 2, 0)
                for slot in range(A_SLOTS + 3):
                    s = slot - A_LEAD
                    if 0 <= s < A_STEPS:
                        a_softmax(dve, i, 0, s, 0)
                    if 1 <= s <= A_STEPS:
                        turned_lo(dve, i, A_STEPS, s - 1, spans((s - 1) // 2) * P)
                        a_inverse(dve, i, 0, s - 1)
                    if 2 <= s <= A_STEPS + 1:
                        o_whole(dve, i, s - 2, [(s % 2, 2 * (s % 2))], (s - 2) // 2, 0, 1)
                    if slot in A_SPLITS:
                        split_lo(dve, i, PER, A_FIRST + A_SPLITS[slot] + 1)
                    if slot == 0:
                        k_lo(dve, i, 4, 2, 1)
                        k_double(dve, i, 2)
                    m, h = A_TAKES.get(slot - 1, (None, 0))
                    if m is not None:
                        sig_inverse(dve, i, 2 * m, SIGS_A, 3 + m, h, (0, 2) if m == 0 else None)

            for c in range(4):
                split_lo(dve, None, 0, AT_B0 + c + 1)
                if c in (1, 2):
                    v_copy(dve, None, B0_TILE, c - 1)
                if c == 3:
                    v_lo(dve, None, PAIRS)
                    k_lo(dve, None, 4 * PAIRS + 1, B0_TILE + 1, 0)
            k_lo(dve, None, 4 * PAIRS + 2, B0_TILE + 1, 1)
            k_double(dve, None, B0_TILE + 1)
            for kv, before in b_rounds():
                with dve.Fori(0, B_ROUNDS) as i:
                    for u in range(ROUND_PAIRS_B):
                        pair = before + u
                        g0, n0 = AT_B + pair * B_PIECES, A_DONE + pair * B_STEPS
                        sigs = PAIRS * SIGS_A + pair * SIGS_B
                        for c in range(B_FIRST):
                            split_lo(dve, i, PER, g0 + c + 1)
                        parts = 4 * PAIRS + 2 + 2 * pair
                        q_lo(dve, i, parts + 1, g0 // 2, 0)
                        for slot in range(B_SLOTS + 3):
                            s = slot - B_LEAD
                            if 0 <= s < B_STEPS:
                                b_softmax(dve, i, n0, s, pair)
                            if 1 <= s <= B_STEPS:
                                b_turned_lo(dve, i, n0, s - 1)
                                b_inverse(dve, i, n0, s - 1, pair)
                            if 2 <= s <= B_STEPS + 1:
                                n = n0 + s - 2
                                o_whole(dve, i, n, [(a, 2 * (n % 2) + a) for a in range(2)], s - 2,
                                        PAIRS + pair, 2)
                            if slot in B_SPLITS:
                                split_lo(dve, i, PER, g0 + B_FIRST + B_SPLITS[slot] + 1)
                            if slot == 0:
                                q_lo(dve, i, parts + 2, g0 // 2, 1)
                            m, h = B_TAKES.get(slot - 1, (None, 0))
                            if m is not None:
                                sig_inverse(dve, i, sigs + 2 * m, 2 * SIGS_B, g0 // 2 + 1 + m, h,
                                            (2 * (PAIRS + pair), 4) if m == 0 else None)

            sigs = PAIRS * (SIGS_A + SIGS_B)
            for c in range(2 * TAIL_TILES + 1):
                if c < 2 * TAIL_TILES:
                    split_lo(dve, None, 0, AT_TAIL + c + 1)
                if c:
                    sig_inverse(dve, None, sigs + 2 * ((c - 1) // 2), 0, TAIL_TILE + (c - 1) // 2, (c - 1) % 2)

            def convert_lo(k, n):
                dve.wait_ge(conv_hi, n + 1)
                nc.vector.tensor_tensor(act_lo[:, k], mixed[:, k], act_hi[:, k].bitcast(F32), ALU.subtract)\
                    .then_inc(conv_ready, 1)

            def merge_take(i, m):
                for h in range(2):
                    n = 2 * m + h
                    part_of = slice(h * HALF, (h + 1) * HALF)
                    tile = mixed[:, at(i, 2, m)]
                    dve.wait_ge(piece_used, at(i, 4, AT_MERGE + 2 * m + 2))
                    dve.wait_ge(gates_loaded, at(i, 4 * 32, 32 * (n + 1)))
                    nc.vector.tensor_tensor(tile[:, part_of], ps[:, 4 * m + h], sig[:, 0], ALU.mult)\
                        .then_inc(a_scaled, 1)
                    nc.vector.tensor_tensor(sig[:, 1], ps[:, 4 * m + 2 + h], sig[:, 1], ALU.mult)\
                        .then_inc(b_scaled, 1)

            split_lo(dve, None, 0, AT_MERGE + 1)
            for k in range(KT):
                convert_lo(k, k)
            dve.wait_ge(conv_ready, KT)
            for c in range(1, 4):
                split_lo(dve, None, 0, AT_MERGE + c + 1)
                if c == 2:
                    merge_take(None, 0)
            merge_take(None, 1)
            with dve.Fori(1, KT // 2) as i:
                for c in range(4):
                    split_lo(dve, i, 4, AT_MERGE + c + 1)
                    if c == 2:
                        merge_take(i, 0)
                merge_take(i, 1)

            for b in range(OUT_BLOCKS):
                for c in range(KT // 2):
                    g = AT_OUT + b * KT // 2 + c + 1
                    if g < PIECES:
                        split_lo(dve, None, 0, g)
                    if b == 0 and c == 0:
                        for k in range(KT):
                            convert_lo(k, KT + k)
                dve.wait_ge(residual_loaded[b], 16)
                last_block = b == OUT_BLOCKS - 1
                for t in range(QT + (2 if last_block else 0)):
                    if t < QT - 1:
                        dve.wait_ge(bank_summed, (QT - 1) * b + t + 1)
                    elif t == QT - 1:
                        dve.wait_ge(piece_used, AT_OUT + (b + 1) * KT // 2)
                    if t < QT:
                        part_of = y[:, t, b * HALF:(b + 1) * HALF]
                        nc.vector.tensor_tensor(part_of, part_of, ps[:, t], ALU.add).then_inc(block_ready, 1)
                    if last_block and 1 <= t <= QT:
                        dve.wait_ge(y_squared, QT * b + t)
                        nc.vector.tensor_reduce(y_stats[:, t - 1:t], y_parts[:, (t - 1) * OUT_BLOCKS:t * OUT_BLOCKS],
                                                axis=AX.X, op=ALU.add).then_inc(y_summed, 1)
                    if last_block and t >= 2:
                        r = t - 2
                        dve.wait_ge(y_rooted, r + 1)
                        nc.vector.reciprocal(rms[:, r:r + 1], rms[:, r:r + 1]).then_inc(y_inv, 1)
                        dve.wait_ge(y_inv, r + 1)
                        if r == 0:
                            dve.wait_ge(final_gain_loaded, 16)
                        dve.wait_ge(block_ready, QT * b + r + 1)
                        nc.vector.scalar_tensor_tensor(y[:, r, :], y[:, r, :], rms[:, r:r + 1], final_gain_sb[:, :],
                                                       ALU.mult, ALU.mult).then_inc(y_scaled, 1)

        @block.gpsimd
        def _(pool):
            pool.wait_ge(consts_ready, 16 * 7)
            with pool.Fori(0, PAIRS) as i:
                mask_bias(pool, i, 0, 16, 16, 0)
                gate_pair(pool, i, 0, 1, 3)
            for kv, before in b_rounds():
                with pool.Fori(0, B_ROUNDS) as i:
                    for u in range(ROUND_PAIRS_B):
                        pair = before + u
                        tile = (AT_B + pair * B_PIECES) // 2
                        mask_bias(pool, i, 1, 16 * PAIRS + 32 * (pair + 1), 64, 0)
                        gate_pair(pool, i, PAIRS + pair, 2, tile + 1)

            def merge_add(i, m):
                for h in range(2):
                    part_of = mixed[:, at(i, 2, m)][:, h * HALF:(h + 1) * HALF]
                    pool.wait_ge(b_scaled, at(i, 4, 2 * m + h + 1))
                    nc.gpsimd.tensor_tensor(part_of, part_of, sig[:, 1], ALU.add).then_inc(mixed_ready, 1)

            for m in range(2):
                merge_add(None, m)
            with pool.Fori(1, KT // 2) as i:
                for m in range(2):
                    merge_add(i, m)


def kernel(**inputs):
    import concourse.bacc as bacc
    from concourse.bass_utils import run_bass_kernel_spmd

    a = {k: np.asarray(v) for k, v in inputs.items()}
    w_in = a["w_in"].reshape(KT, P, -1, P)
    tiles = w_in[:, :, in_tile_order()].transpose(2, 1, 0, 3)
    pieces = [tiles.reshape(-1, P, 2, COLS).transpose(0, 2, 1, 3).reshape(-1, P, COLS)]
    branch = np.stack([a[n].reshape(WIDTH // P, P, KT, P) for n in ("w_branch_a", "w_branch_b")])
    pieces.append(branch.transpose(3, 0, 2, 1, 4).reshape(-1, P, COLS))
    last = a["w_out"].reshape(KT // 2, 2, P, OUT_BLOCKS, HALF)
    pieces.append(last.transpose(3, 0, 2, 1, 4).reshape(-1, P, COLS))
    weights = np.concatenate(pieces)
    assert weights.shape[0] == PIECES
    sel_a, sel_b = selections()
    arrays = {
        "x": a["x"],
        "gain": a["norm_gain"].reshape(KT, P).T,
        "final_gain": a["final_gain"],
        "weights": weights,
        "table_a": a["rel_bias_a"][:, 1:].T.reshape(2, P, HEADS).transpose(1, 0, 2),
        "table_b": a["t5_bias"],
        "sinks": a["sinks_b"],
        "sel_a": sel_a.reshape(2, P, EXT).transpose(1, 0, 2),
        "sel_b": sel_b,
        "mask": masks(),
        "ident": np.eye(P, dtype=np.float32),
    }
    arrays = {f"{k}_in": np.ascontiguousarray(v) for k, v in arrays.items()}
    nc = bacc.Bacc("TRN2", target_bir_lowering=False, num_devices=1, dynamic_dma_scratch_size=512)
    args = [nc.dram_tensor(k, v.shape, F32, kind="ExternalInput").ap() for k, v in arrays.items()]
    out = nc.dram_tensor("out", (1, SEQ, D_MODEL), F32, kind="ExternalOutput").ap()
    build(nc, *args, out)
    r = run_bass_kernel_spmd(nc, [arrays], core_ids=[0])
    return r.results[0]["out"]
```

```python
import math
from contextlib import ExitStack

import numpy as np

import concourse.bass as bass
from concourse import mybir

F32 = mybir.dt.float32
F32R = mybir.dt.float32r
ALU = mybir.AluOpType
ACT = mybir.ActivationFunctionType
AX = mybir.AxisListType

P = 128
HALF = 512
NEG = -1e30
EPS = 1e-6

D_MODEL, SEQ, CHUNK = 2048, 1024, 64
HEADS, HEAD_DIM = 16, 64
KV_HEADS = 2
A_PREV, B_PREV = 8, 1
REL_CLIP = 128
T5_BUCKETS, T5_MAX_DIST = 32, 128
WIDTH = HEADS * HEAD_DIM
KV_WIDTH = KV_HEADS * HEAD_DIM

PAIRS = HEADS // 2
KT = D_MODEL // P
QT = SEQ // P
SPAN = A_PREV * CHUNK // P + 1
PIECE = 8
COLS = PIECE * P
EXT = 3 * P
BIAS_ROWS = 2 * P

IN_WIDTHS = [WIDTH, WIDTH, WIDTH, WIDTH, WIDTH, KV_WIDTH, KV_WIDTH, WIDTH, D_MODEL, D_MODEL]
STARTS = [sum(IN_WIDTHS[:i]) // P for i in range(len(IN_WIDTHS))]
QA, KA, VA, ZA, QB, KB, VB, ZB, GA, GB = STARTS
GATES = 2 * D_MODEL // P

A_GATES, B_GATES = 2, 1
A_TILES = 4 + A_GATES
B_TILES = 2 + B_GATES
TAIL_TILES = GATES - PAIRS * (A_GATES + B_GATES)
OUT_BLOCKS = D_MODEL // HALF

A_PIECES = 2 * A_TILES
B_PIECES = 2 * B_TILES
AT_B0 = PAIRS * A_PIECES
AT_B = AT_B0 + 4
AT_TAIL = AT_B + PAIRS * B_PIECES
AT_MERGE = AT_TAIL + 2 * TAIL_TILES
AT_OUT = AT_MERGE + 2 * KT
PIECES = AT_OUT + OUT_BLOCKS * KT // 2
PER_PIECE = PIECE * 2 * 3

A_LEAD, B_LEAD = 3, 2
A_STEPS, B_STEPS = 2 * QT, QT
A_SLOTS = A_LEAD + A_STEPS + 2
B_SLOTS = B_LEAD + B_STEPS + 2


def in_tile_order():
    order = []
    for p in range(PAIRS):
        order += [VA + p, QA + p, KA + p, ZA + p] + [GA + A_GATES * p + j for j in range(A_GATES)]
    order += [VB, KB]
    for p in range(PAIRS):
        order += [QB + p, ZB + p] + [GA + A_GATES * PAIRS + B_GATES * p + j for j in range(B_GATES)]
    order += [GA + (A_GATES + B_GATES) * PAIRS + j for j in range(TAIL_TILES)]
    return order


def t5_bucket(rel_pos):
    nb = T5_BUCKETS // 2
    ret = (rel_pos > 0).astype(np.int32) * nb
    n = np.abs(rel_pos)
    exact = nb // 2
    large = exact + (np.log(np.maximum(n, 1) / exact) / np.log(T5_MAX_DIST / exact) * (nb - exact)).astype(np.int32)
    return (ret + np.where(n < exact, n, np.minimum(large, nb - 1))).astype(np.int32)


def selections():
    rel = 2 * P - 1 - np.arange(EXT)
    row = np.clip(rel, -REL_CLIP, REL_CLIP) + REL_CLIP - 1
    a = np.zeros((BIAS_ROWS, EXT), np.float32)
    n = np.arange(EXT)
    used = n < EXT - 1
    a[row[used], n[used]] = 1
    a[BIAS_ROWS - 1] -= used
    b = np.zeros((T5_BUCKETS, EXT), np.float32)
    b[t5_bucket(-rel)[used], n[used]] = 1
    return a, b


def masks():
    q = np.arange(P)[:, None] // CHUNK
    k = np.arange(2 * P)[None, :] // CHUNK - 2
    out = []
    for prev in (A_PREV, B_PREV):
        out.append(np.where((k <= q) & (k >= q - prev), 0.0, NEG).astype(np.float32))
    return np.stack(out, 1)


def at(i, per, base):
    return base if i is None else i * per + base


ROUND_TILES = A_TILES
ROUND_PAIRS_B = 2
B0_TILE, B_TILE = AT_B0 // 2, AT_B // 2
TAIL_TILE = AT_TAIL // 2
assert B_TILES * ROUND_PAIRS_B == ROUND_TILES and B0_TILE % 2 == B_TILE % 2 == TAIL_TILE % 2 == 0


def build(nc, x, gain, final_gain, weights, table_a, table_b, sinks, sel_a, sel_b, mask, ident_in, out):
    gates_dram = nc.dram_tensor("gates_dram", (GATES, P, SEQ), F32, kind="Internal").ap()
    gated_dram = nc.dram_tensor("gated_dram", (2 * PAIRS, P, SEQ), F32, kind="Internal").ap()
    bias_dram = nc.dram_tensor("bias_dram", (2, HEADS, P, 2 * P), F32, kind="Internal").ap()
    ext_dram = nc.dram_tensor("ext_dram", (2, HEADS, EXT), F32, kind="Internal").ap()

    with ExitStack() as ctx:
        place = [640]

        def sb(name, shape, dt=F32, where=None):
            size = 4 * math.prod(shape[1:])
            size += -size % 32
            start = place[0] if where is None else where[0]
            if where is None:
                place[0] += size
            else:
                where[0] += size
            return nc.alloc_sbuf_tensor_at(name, shape, dt, offset=start)

        def sem(name):
            return ctx.enter_context(nc.semaphore(name))

        act_hi = sb("act_hi", [P, KT, SEQ], F32R)
        act_lo = sb("act_lo", [P, KT, SEQ], F32R)
        raw = sb("raw", [P, 2, COLS])
        w_hi = sb("w_hi", [P, 2, COLS], F32R)
        w_lo = sb("w_lo", [P, 2, COLS], F32R)
        ident = sb("ident", [P, P])
        masks_sb = sb("masks_sb", [P, 2, 2 * P])
        gain_sb = sb("gain_sb", [P, KT])
        sig = sb("sig", [P, 2, HALF])
        small = sb("small", [P, 80])
        overlay = place[0]

        def over(name, shape, dt, tensor_at):
            return nc.alloc_sbuf_tensor_at(name, shape, dt, offset=tensor_at)

        x_sb = over("x_sb", [P, QT, D_MODEL], F32, overlay)
        w_hi_at, w_lo_at, raw_at = (640 + 8 * KT * SEQ + n * 8 * COLS for n in (1, 2, 0))
        sel_a_sb = over("sel_a_sb", [P, 2, EXT], F32, w_hi_at)
        sel_b_sb = over("sel_b_sb", [T5_BUCKETS, EXT], F32, w_hi_at + 4096)
        table_a_sb = over("table_a_sb", [P, 2, HEADS], F32, w_hi_at + 6144)
        table_b_sb = over("table_b_sb", [T5_BUCKETS, HEADS], F32, w_hi_at + 7168)
        ext_sb = over("ext_sb", [HEADS, 2, EXT], F32, w_lo_at)

        here = [overlay]
        q_stack = sb("q_stack", [P, 2, SEQ], F32R, where=here)
        k_hi2 = sb("k_hi2", [P, 2, SEQ], F32R, where=here)
        k_lo2 = sb("k_lo2", [P, 2, SEQ], F32R, where=here)
        v_parts = sb("v_parts", [P, QT, 2, 2, HEAD_DIM], F32R, where=here)
        vT = sb("vT", [P, SEQ], where=here)
        z_raw = sb("z_raw", [P, SEQ], where=here)
        probs = sb("probs", [P, 2, SPAN * P], where=here)
        pT = sb("pT", [P, 2, 2, SPAN * P], F32R, where=here)
        o_sum = sb("o_sum", [P, HALF], where=here)
        oT = sb("oT", [P, SEQ], where=here)
        bias = sb("bias", [P, 2, 2 * P], where=here)
        sink = sb("sink", [P, 2], where=here)
        att_end = here[0]

        mixed = over("mixed", [P, KT, SEQ], F32, overlay)
        y = over("y", [P, QT, D_MODEL], F32, overlay)
        final_gain_sb = over("final_gain_sb", [P, D_MODEL], F32, raw_at)
        end = max(att_end, overlay + 4 * KT * SEQ)
        assert end <= nc.sbuf_usable_end, (end, nc.sbuf_usable_end)

        sumsq = small[:, 0:QT]
        rms = small[:, QT:2 * QT]
        eps = small[:, 16:17]
        neg_max = small[:, 17:21]
        exp_sum = small[:, 21:25]
        exp_inv = small[:, 25:29]
        exp_sink = small[:, 29:33]
        keys_max = small[:, 33:35]
        whole_sum = small[:, 35:37]
        y_parts = small[:, 40:40 + QT * OUT_BLOCKS]
        y_stats = small[:, 72:80]

        ps = ctx.enter_context(nc.psum_tensor("ps", [P, 8, HALF], F32))
        flat = ps[:, :, :].rearrange("p b n -> p (b n)")
        TURN = 3
        S = flat[:, 3 * HALF:5 * HALF]
        T = flat[:, 5 * HALF:7 * HALF]
        O = flat[:, 7 * HALF:8 * HALF]

        x_ready = [sem(f"x_ready{t}") for t in range(QT)]
        consts_ready = sem("consts_ready")
        eps_ready = sem("eps_ready")
        squared = sem("squared")
        rooted = sem("rooted")
        rms_ready = sem("rms_ready")
        x_scaled = sem("x_scaled")
        x_turned = sem("x_turned")
        h_hi_ready = sem("h_hi_ready")
        h_ready = sem("h_ready")
        ext_made = sem("ext_made")
        ext_copied = sem("ext_copied")
        ext_stored = sem("ext_stored")
        windows_stored = sem("windows_stored")

        raw_ready = [sem("raw_ready0"), sem("raw_ready1")]
        hi_ready = sem("hi_ready")
        lo_ready = sem("lo_ready")
        piece_used = sem("piece_used")
        half_summed = sem("half_summed")
        bank_taken = [sem(f"bank_taken{b}") for b in range(3)]
        part_hi = sem("part_hi")

        v_turned = sem("v_turned")
        v_hi_ready = sem("v_hi_ready")
        v_ready = sem("v_ready")
        k_doubled = sem("k_doubled")
        bias_ready = sem("bias_ready")
        bias_masked = sem("bias_masked")
        scores_ready = sem("scores_ready")
        biased = sem("biased")
        max_found = sem("max_found")
        max_ready = sem("max_ready")
        exp_ready = sem("exp_ready")
        sink_added = sem("sink_added")
        inv_ready = sem("inv_ready")
        turned = sem("turned")
        pT_hi_ready = sem("pT_hi_ready")
        pT_ready = sem("pT_ready")
        pv_ready = sem("pv_ready")
        probs_ready = sem("probs_ready")
        rest_ready = sem("rest_ready")
        o_taken = sem("o_taken")
        o_added = sem("o_added")
        gated_ready = sem("gated_ready")
        gated_stored = sem("gated_stored")
        z_sig_ready = sem("z_sig_ready")
        z_applied = sem("z_applied")
        gate_stored = [sem("gate_stored0"), sem("gate_stored1")]

        gated_loaded = [sem(f"gated_loaded{k}") for k in range(4)]
        conv_hi = sem("conv_hi")
        conv_ready = sem("conv_ready")
        gates_loaded = sem("gates_loaded")
        gates_ready = sem("gates_ready")
        a_scaled = sem("a_scaled")
        b_scaled = sem("b_scaled")
        mixed_ready = sem("mixed_ready")
        residual_loaded = [sem(f"residual_loaded{b}") for b in range(OUT_BLOCKS)]
        bank_summed = sem("bank_summed")
        block_ready = sem("block_ready")
        y_squared = sem("y_squared")
        y_summed = sem("y_summed")
        y_rooted = sem("y_rooted")
        y_inv = sem("y_inv")
        final_gain_loaded = sem("final_gain_loaded")
        y_scaled = sem("y_scaled")
        out_stored = sem("out_stored")

        BIASED_A = 2 * QT + 2 * (QT - SPAN + 1)

        def spans(t):
            return min(t + 1, SPAN)

        def raw_wait(eng, i, per, g):
            eng.wait_ge(raw_ready[g % 2], at(i, 8 * per, 16 * (g // 2 + 1)))

        def split_hi(act, i, per, g):
            raw_wait(act, i, per, g)
            if g >= 2 or i is not None:
                act.wait_ge(piece_used, at(i, per, g - 1))
            nc.scalar.activation(w_hi[:, g % 2], raw[:, g % 2], ACT.Copy).then_inc(hi_ready, 1)

        def split_lo(dve, i, per, g):
            dve.wait_ge(hi_ready, at(i, per, g + 1))
            nc.vector.tensor_tensor(w_lo[:, g % 2], raw[:, g % 2], w_hi[:, g % 2].bitcast(F32),
                                    ALU.subtract).then_inc(lo_ready, 1)

        def bank(tile, h):
            return (2 * tile + h) % TURN

        def project(pe, i, per, g, tile, first, last):
            b = g % 2
            if first >= last:
                return
            for n in range(first, last):
                h, k, m = n // (3 * PIECE), n // 3 % PIECE, n % 3
                if n == 0:
                    pe.wait_ge(lo_ready, at(i, per, g + 1))
                if b == 0 and n % (3 * PIECE) == 0 and (i is not None or 2 * tile + h >= TURN):
                    pe.wait_ge(bank_taken[bank(tile, h)], at(i, per // TURN, (2 * tile + h) // TURN))
                w, a = ((w_hi, act_hi), (w_hi, act_lo), (w_lo, act_hi))[m]
                kt = PIECE * b + k
                mm = nc.tensor.matmul(ps[:, bank(tile, h)], w[:, b, k * P:(k + 1) * P],
                                      a[:, kt, h * HALF:(h + 1) * HALF],
                                      start=(kt == 0 and m == 0), stop=(kt == KT - 1 and m == 2))
                if n == PER_PIECE - 1:
                    mm.then_inc(piece_used, 1)
                elif b and n == 3 * PIECE - 1:
                    mm.then_inc(half_summed, 1)

        def taken(eng, i, tile, h, per=2 * ROUND_TILES):
            eng.wait_ge(bank_taken[bank(tile, h)], at(i, per // TURN, (2 * tile + h) // TURN + 1))

        def half_done(eng, i, tile, h, per=2 * ROUND_TILES):
            if h == 0:
                eng.wait_ge(half_summed, at(i, per // 2, tile + 1))
            else:
                eng.wait_ge(piece_used, at(i, per, 2 * tile + 2))

        def a_step(s):
            t, a = s // 2, s % 2
            return t, a, (SPAN + 1 - spans(t)) * P

        def a_scores(pe, i, n0, s):
            t, a, c0 = a_step(s)
            if s == 0:
                for h in range(2):
                    taken(pe, i, 1, h)
                pe.wait_ge(k_doubled, at(i, 1, 1))
            if i is not None or n0 + s:
                pe.wait_ge(exp_ready, at(i, A_STEPS, n0 + s))
            for lo, hi in ((c0, 4 * P), (max(c0, 4 * P), 6 * P)):
                if lo >= hi:
                    continue
                keys = (t + 1) * P - 6 * P
                for j, k in enumerate((k_hi2, k_lo2)):
                    mm = nc.tensor.matmul(S[:, lo:hi], q_stack[:, a, t * P:(t + 1) * P],
                                          k[:, a, keys + lo:keys + hi], start=(j == 0), stop=(j == 1))
            mm.then_inc(scores_ready, 1)

        def a_softmax(dve, i, n0, s, b0):
            t, a, c0 = a_step(s)
            near = max(c0, 4 * P)
            if s == 0:
                dve.wait_ge(bias_masked, at(i, 1, 1))
            dve.wait_ge(scores_ready, at(i, A_STEPS, n0 + s + 1))
            nc.vector.tensor_tensor(S[:, near:6 * P], S[:, near:6 * P], bias[:, a, near - 4 * P:],
                                    ALU.add).then_inc(biased, 1)
            if t >= SPAN - 1:
                nc.vector.memset(S[CHUNK:, c0:c0 + CHUNK], NEG).then_inc(biased, 1)
            done = sum(1 + (r // 2 >= SPAN - 1) for r in range(s + 1))
            dve.wait_ge(biased, at(i, BIASED_A, b0 + done))
            nc.vector.tensor_reduce(neg_max[:, 2 * a:2 * a + 1], S[:, c0:6 * P], axis=AX.X, op=ALU.max,
                                    negate=True).then_inc(max_ready, 1)

        def a_exp(act, i, n0, s):
            t, a, c0 = a_step(s)
            act.wait_ge(max_ready, at(i, A_STEPS, n0 + s + 1))
            nc.scalar.activation(probs[:, s % 2, :6 * P - c0], S[:, c0:6 * P], ACT.Exp,
                                 bias=neg_max[:, 2 * a:2 * a + 1],
                                 accum_out=exp_sum[:, 2 * a:2 * a + 1]).then_inc(exp_ready, 1)

        def a_normalise(dve, i, n0, s):
            t, a, c0 = a_step(s)
            inv = exp_inv[:, 2 * a:2 * a + 1]
            dve.wait_ge(exp_ready, at(i, A_STEPS, n0 + s + 1))
            nc.vector.reciprocal(inv, exp_sum[:, 2 * a:2 * a + 1]).then_inc(inv_ready, 1)
            dve.wait_ge(inv_ready, at(i, A_STEPS, n0 + s + 1))
            nc.vector.tensor_scalar(probs[:, s % 2, :6 * P - c0], probs[:, s % 2, :6 * P - c0], inv, None,
                                    ALU.mult).then_inc(probs_ready, 1)

        def a_turn(pe, i, n0, s):
            t, a, c0 = a_step(s)
            pe.wait_ge(probs_ready, at(i, A_STEPS, n0 + s + 1))
            if s == 0:
                pe.wait_ge(v_ready, at(i, 1, 1))
            if i is not None or n0 + s:
                pe.wait_ge(pT_ready, at(i, A_STEPS, n0 + s))
            for j in range(spans(t)):
                tr = nc.tensor.transpose(T[:, j * P:(j + 1) * P], probs[:, s % 2, j * P:(j + 1) * P], ident[:, :])
            tr.then_inc(turned, 1)

        def turned_hi(act, i, per, n, cols):
            act.wait_ge(turned, at(i, per, n + 1))
            if i is not None or n >= 2:
                act.wait_ge(pv_ready, at(i, per, n - 1))
            nc.scalar.activation(pT[:, n % 2, 0, cols], T[:, cols], ACT.Copy).then_inc(pT_hi_ready, 1)

        def turned_lo(dve, i, per, n, cols):
            dve.wait_ge(pT_hi_ready, at(i, per, n + 1))
            nc.vector.tensor_tensor(pT[:, n % 2, 1, cols], T[:, cols], pT[:, n % 2, 0, cols].bitcast(F32),
                                    ALU.subtract).then_inc(pT_ready, 1)

        def a_values(pe, i, n0, s):
            t, a, c0 = a_step(s)
            pe.wait_ge(pT_ready, at(i, A_STEPS, n0 + s + 1))
            if i is not None or n0 + s:
                pe.wait_ge(o_taken, at(i, A_STEPS, n0 + s))
            for j in range(spans(t)):
                mm = nc.tensor.matmul(O[:, :2 * P].rearrange("p (r n) -> p r n", r=2),
                                      v_parts[:, t + 1 - spans(t) + j, a].rearrange("p h d -> p (h d)"),
                                      pT[:, s % 2, :, j * P:(j + 1) * P],
                                      start=(j == 0), stop=(j == spans(t) - 1))
            mm.then_inc(pv_ready, 1)

        def o_half(n):
            return slice(n % 2 * HEAD_DIM, (n % 2 + 1) * HEAD_DIM)

        def o_rest(act, i, per, n, cols):
            act.wait_ge(pv_ready, at(i, per, n + 1))
            if i is not None or n >= 2:
                act.wait_ge(o_added, at(i, per, n - 1))
            nc.scalar.activation(o_sum[o_half(n), :cols], O[HEAD_DIM:, :cols], ACT.Copy).then_inc(rest_ready, 1)

        def o_take(dve, i, per, n, cols):
            dve.wait_ge(rest_ready, at(i, per, n + 1))
            nc.vector.tensor_tensor(o_sum[o_half(n), :cols], O[:HEAD_DIM, :cols], o_sum[o_half(n), :cols], ALU.add)\
                .then_inc(o_taken, 1)

        def oT_add(pool, i, per, n, heads, t, pairs, m):
            pool.wait_ge(o_taken, at(i, per, n + 1))
            if n % (A_STEPS if m == 1 else B_STEPS) == 0 and (i is not None or pairs):
                pool.wait_ge(gated_stored, at(i, 16 * m, 16 * pairs))
            for j, a in enumerate(heads):
                c, low = j * P, (len(heads) + j) * P
                last = nc.gpsimd.tensor_tensor(
                    oT[a * HEAD_DIM:(a + 1) * HEAD_DIM, t * P:(t + 1) * P], o_sum[o_half(n), c:c + P],
                    o_sum[o_half(n), low:low + P], ALU.add)
            last.then_inc(o_added, 1)

        def b_scores(pe, i, n0, s, kv, q_tile):
            if s == 0:
                for h in range(2):
                    taken(pe, i, q_tile, h)
                pe.wait_ge(k_doubled, PAIRS + 1)
            pe.wait_ge(exp_ready, at(i, 2 * B_STEPS, n0 + s))
            c0 = P if s == 0 else 0
            keys = (s - 1) * P
            for a in range(2):
                for j, k in enumerate((k_hi2, k_lo2)):
                    mm = nc.tensor.matmul(S[:, a * HALF + c0:a * HALF + 2 * P], q_stack[:, a, s * P:(s + 1) * P],
                                          k[:, kv, keys + c0:keys + 2 * P], start=(j == 0), stop=(j == 1))
            mm.then_inc(scores_ready, 1)

        SB = S.rearrange("p (a n) -> p a n", a=2)

        def b_softmax(dve, i, n0, s, pair):
            c0 = P if s == 0 else 0
            n, before = n0 + s, pair * B_STEPS + s
            if s == 0:
                dve.wait_ge(bias_masked, at(i, 2, PAIRS + pair + 1))
            dve.wait_ge(scores_ready, at(i, 2 * B_STEPS, n + 1))
            nc.vector.tensor_tensor(SB[:, :, c0:2 * P], SB[:, :, c0:2 * P], bias[:, :, c0:], ALU.add)\
                .then_inc(biased, 1)
            dve.wait_ge(biased, at(i, 2 * B_STEPS, PAIRS * BIASED_A + before + 1))
            nc.vector.tensor_reduce(keys_max, SB[:, :, c0:2 * P], axis=AX.X, op=ALU.max, negate=True)\
                .then_inc(max_found, 1)
            dve.wait_ge(max_found, at(i, 2 * B_STEPS, before + 1))
            nc.vector.scalar_tensor_tensor(neg_max[:, 2 * (n % 2):2 * (n % 2) + 2], sink[:, :], -1.0,
                                           keys_max, ALU.mult, ALU.min).then_inc(max_ready, 1)

        def b_exp(act, i, n0, s):
            c0 = P if s == 0 else 0
            n = n0 + s
            act.wait_ge(max_ready, at(i, 2 * B_STEPS, n + 1))
            for a in range(2):
                col = 2 * (n % 2) + a
                nc.scalar.activation(exp_sink[:, col:col + 1], sink[:, a:a + 1], ACT.Exp,
                                     bias=neg_max[:, col:col + 1])
                last = nc.scalar.activation(probs[:, n % 2, a * 2 * P + c0:(a + 1) * 2 * P],
                                            S[:, a * HALF + c0:a * HALF + 2 * P], ACT.Exp,
                                            bias=neg_max[:, col:col + 1],
                                            accum_out=exp_sum[:, col:col + 1])
            last.then_inc(exp_ready, 1)

        def b_normalise(dve, i, n0, s, pair):
            n, before = n0 + s, pair * B_STEPS + s
            two = slice(2 * (n % 2), 2 * (n % 2) + 2)
            c0 = P if s == 0 else 0
            dve.wait_ge(exp_ready, at(i, 2 * B_STEPS, n + 1))
            nc.vector.tensor_tensor(whole_sum, exp_sum[:, two], exp_sink[:, two], ALU.add).then_inc(sink_added, 1)
            dve.wait_ge(sink_added, at(i, 2 * B_STEPS, before + 1))
            nc.vector.reciprocal(exp_inv[:, two], whole_sum).then_inc(inv_ready, 1)
            dve.wait_ge(inv_ready, at(i, 2 * B_STEPS, n + 1))
            for a in range(2):
                part_of = probs[:, n % 2, a * 2 * P + c0:(a + 1) * 2 * P]
                last = nc.vector.tensor_scalar(part_of, part_of, exp_inv[:, 2 * (n % 2) + a:2 * (n % 2) + a + 1],
                                               None, ALU.mult)
            last.then_inc(probs_ready, 1)

        def b_turn(pe, i, n0, s):
            n = n0 + s
            if s == 0:
                pe.wait_ge(v_ready, PAIRS + 1)
            pe.wait_ge(probs_ready, at(i, 2 * B_STEPS, n + 1))
            pe.wait_ge(pT_ready, at(i, 2 * B_STEPS, n))
            for j in range(0 if s else 1, 2):
                for a in range(2):
                    tr = nc.tensor.transpose(T[:, (2 * j + a) * P:(2 * j + a + 1) * P],
                                             probs[:, n % 2, (2 * a + j) * P:(2 * a + j + 1) * P], ident[:, :])
            tr.then_inc(turned, 1)

        def b_cols(s):
            return slice(0 if s else 2 * P, 4 * P)

        def b_values(pe, i, n0, s, kv):
            n = n0 + s
            pe.wait_ge(pT_ready, at(i, 2 * B_STEPS, n + 1))
            pe.wait_ge(o_taken, at(i, 2 * B_STEPS, n))
            for j in range(0 if s else 1, 2):
                mm = nc.tensor.matmul(O.rearrange("p (r n) -> p r n", r=2),
                                      v_parts[:, s - 1 + j, kv].rearrange("p h d -> p (h d)"),
                                      pT[:, n % 2, :, 2 * j * P:2 * (j + 1) * P],
                                      start=(j == (0 if s else 1)), stop=(j == 1))
            mm.then_inc(pv_ready, 1)

        def q_hi(act, i, tile, h):
            half_done(act, i, tile, h)
            for a in range(2):
                last = nc.scalar.activation(q_stack[0:64, a, h * HALF:(h + 1) * HALF],
                                            ps[a * 64:a * 64 + 64, bank(tile, h)], ACT.Copy,
                                            scale=HEAD_DIM ** -0.5)
            last.then_inc(part_hi, 1)

        def q_lo(dve, i, n, tile, h):
            dve.wait_ge(part_hi, at(i, 4, n))
            for a in range(2):
                last = nc.vector.scalar_tensor_tensor(
                    q_stack[64:128, a, h * HALF:(h + 1) * HALF], ps[a * 64:a * 64 + 64, bank(tile, h)],
                    HEAD_DIM ** -0.5, q_stack[0:64, a, h * HALF:(h + 1) * HALF].bitcast(F32),
                    ALU.mult, ALU.subtract)
            last.then_inc(bank_taken[bank(tile, h)], 1)

        def k_hi(act, i, tile, h):
            half_done(act, i, tile, h)
            for a in range(2):
                last = nc.scalar.activation(k_hi2[0:64, a, h * HALF:(h + 1) * HALF],
                                            ps[a * 64:a * 64 + 64, bank(tile, h)], ACT.Copy)
            last.then_inc(part_hi, 1)

        def k_lo(dve, i, n, tile, h):
            dve.wait_ge(part_hi, at(i, 4, n))
            for a in range(2):
                last = nc.vector.tensor_tensor(
                    k_lo2[0:64, a, h * HALF:(h + 1) * HALF], ps[a * 64:a * 64 + 64, bank(tile, h)],
                    k_hi2[0:64, a, h * HALF:(h + 1) * HALF].bitcast(F32), ALU.subtract)
            last.then_inc(bank_taken[bank(tile, h)], 1)

        def k_double(dve, i, tile):
            for h in range(2):
                taken(dve, i, tile, h)
            for k in (k_hi2, k_lo2):
                last = nc.vector.tensor_copy(k[64:128, :, :], k[0:64, :, :])
            last.then_inc(k_doubled, 1)

        def v_copy(dve, i, tile, h):
            half_done(dve, i, tile, h)
            if i is not None or tile:
                dve.wait_ge(gated_ready, at(i, 1, tile // ROUND_TILES))
            nc.vector.tensor_copy(vT[:, h * HALF:(h + 1) * HALF], ps[:, bank(tile, h)])\
                .then_inc(bank_taken[bank(tile, h)], 1)

        def v_turn(pe, i, tile, pairs):
            for h in range(2):
                taken(pe, i, tile, h)
            if i is not None or pairs:
                pe.wait_ge(pT_ready, at(i, A_STEPS, A_STEPS * pairs))
            for t in range(QT):
                tr = nc.tensor.transpose(T[:, t * P:(t + 1) * P], vT[:, t * P:(t + 1) * P], ident[:, :])
            tr.then_inc(v_turned, 1)

        v_view = v_parts[:, :, :, :, :].rearrange("p t a h d -> p (t a) h d")
        T_view = T.rearrange("p (m d) -> p m d", d=HEAD_DIM)

        def v_hi(act, i, n):
            act.wait_ge(v_turned, at(i, 1, n + 1))
            nc.scalar.activation(v_view[:, :, 0, :], T_view, ACT.Copy).then_inc(v_hi_ready, 1)

        def v_lo(dve, i, n):
            dve.wait_ge(v_hi_ready, at(i, 1, n + 1))
            nc.vector.tensor_tensor(v_view[:, :, 1, :], T_view, v_view[:, :, 0, :].bitcast(F32),
                                    ALU.subtract).then_inc(v_ready, 1)

        def z_take(act, i, tile, h, pairs, m):
            half_done(act, i, tile, h)
            if i is not None or pairs:
                act.wait_ge(gated_ready, at(i, m, pairs))
            nc.scalar.activation(z_raw[:, h * HALF:(h + 1) * HALF], ps[:, bank(tile, h)], ACT.Copy)\
                .then_inc(bank_taken[bank(tile, h)], 1)

        def z_sigmoid(act, i, tile):
            for h in range(2):
                taken(act, i, tile, h)
            nc.scalar.activation(vT[:, :], z_raw[:, :], ACT.Sigmoid).then_inc(z_sig_ready, 1)

        def gate_take(act, i, tile, h, gates, m, per=2 * ROUND_TILES):
            half_done(act, i, tile, h, per)
            if i is not None or gates:
                act.wait_ge(gate_stored[h], at(i, 16 * m, 16 * gates))
            nc.scalar.activation(sig[:, h], ps[:, bank(tile, h)], ACT.Copy)\
                .then_inc(bank_taken[bank(tile, h)], 1)

        def gate_store(act, i, tile, gate, per_gate, h):
            taken(act, i, tile, h)
            act.dma_start(gates_dram[at(i, per_gate, gate), :, h * HALF:(h + 1) * HALF], sig[:, h])\
                .then_inc(gate_stored[h], 16)

        def gate_pair(pool, i, pairs, m, z_tile, n):
            for h in range(2):
                taken(pool, i, z_tile, h)
            pool.wait_ge(o_added, at(i, A_STEPS, n))
            nc.gpsimd.tensor_tensor(oT[:, :], oT[:, :], z_raw[:, :], ALU.mult).then_inc(z_applied, 1)
            pool.wait_ge(z_applied, at(i, m, pairs + 1))
            pool.wait_ge(z_sig_ready, at(i, m, pairs + 1))
            nc.gpsimd.tensor_tensor(oT[:, :], oT[:, :], vT[:, :], ALU.mult).then_inc(gated_ready, 1)

        def pair_store(sp, i, m, pairs):
            sp.wait_ge(gated_ready, at(i, m, pairs + 1))
            sp.dma_start(gated_dram[at(i, m, pairs)], oT[:, :]).then_inc(gated_stored, 16)

        def mask_bias(pool, i, mixer, loads, per, n):
            pool.wait_ge(bias_ready, at(i, per, loads))
            for a in range(2):
                last = nc.gpsimd.tensor_tensor(bias[:, a], bias[:, a], masks_sb[:, mixer], ALU.add)
            last.then_inc(bias_masked, 1)

        def slot_tasks(slots, tiles):
            total = tiles * 2 * PER_PIECE

            def after(products):
                return next(s for s in range(slots + 1) if s * total // slots >= products)

            splits = {after(c * PER_PIECE): c for c in range(2 * tiles)}
            takes = {after((4 * m + 3 + h) * PER_PIECE // 2): (m, h) for m in range(tiles) for h in range(2)}
            assert len(splits) == 2 * tiles and len(takes) == 2 * tiles
            return splits, takes

        A_LATE, B_LATE = 1 + A_GATES, 1 + B_GATES
        A_SPLITS, A_TAKES = slot_tasks(A_SLOTS, A_LATE)
        B_SPLITS, B_TAKES = slot_tasks(B_SLOTS, B_LATE)
        A_FIRST, B_FIRST = A_PIECES - 2 * A_LATE, B_PIECES - 2 * B_LATE
        PER = 2 * ROUND_TILES
        GATES_BEFORE_B = PAIRS * A_GATES
        B_ROUNDS = PAIRS // KV_HEADS // ROUND_PAIRS_B
        A_DONE = PAIRS * A_STEPS

        def slot_share(pe, i, slot, slots, tiles, g0):
            total = tiles * 2 * PER_PIECE
            first, last = slot * total // slots, (slot + 1) * total // slots
            for c in range(2 * tiles):
                project(pe, i, PER, g0 + c, (g0 + c) // 2, max(first - c * PER_PIECE, 0),
                        min(last - c * PER_PIECE, PER_PIECE))

        def b_rounds():
            for kv in range(KV_HEADS):
                yield kv, kv * (PAIRS // KV_HEADS)

        block = ctx.enter_context(nc.Block())

        @block.sync
        def _(sp):
            for t in range(QT):
                sp.dma_start(x_sb[:, t, :], x[0, t * P:(t + 1) * P, :]).then_inc(x_ready[t], 16)

            def load(i, per, g):
                if g >= 2:
                    sp.wait_ge(lo_ready, at(i, per, g - 1))
                sp.dma_start(raw[:, g % 2], weights[at(i, per, g)]).then_inc(raw_ready[g % 2], 16)

            load(None, 0, 0)
            load(None, 0, 1)
            sp.wait_ge(ext_copied, 2)
            sp.dma_start(ext_dram.rearrange("m h n -> h m n"), ext_sb[:, :, :]).then_inc(ext_stored, 16)
            sp.wait_ge(ext_stored, 16)
            for mixer in range(2):
                rows = bass.AP(ext_dram.tensor, mixer * HEADS * EXT + P - 1, [[EXT, HEADS], [-1, P], [1, 2 * P]])
                sp.dma_start(bias_dram[mixer], rows).then_inc(windows_stored, 16)
            sp.wait_ge(windows_stored, 32)

            def a_round(i):
                for c in range(A_PIECES):
                    if c == 2:
                        heads = slice(0, 2)
                        if i is not None:
                            pair_store(sp, i, 1, -1)
                            heads = bass.ds(2 * i, 2)
                            sp.wait_ge(biased, at(i, BIASED_A, 0))
                        sp.dma_start(bias[:, :, :], bias_dram[0, heads].rearrange("h p n -> p h n"))\
                            .then_inc(bias_ready, 16)
                    load(i, PER, 2 + c)

            a_round(None)
            with sp.Fori(1, PAIRS) as i:
                a_round(i)
            for c in range(4):
                load(None, 0, AT_B0 + 2 + c)
            for kv, before in b_rounds():
                with sp.Fori(0, B_ROUNDS) as i:
                    for u in range(ROUND_PAIRS_B):
                        pair = before + u
                        head = i * 4 + 2 * pair
                        sp.wait_ge(exp_ready, at(i, 2 * B_STEPS, A_DONE + pair * B_STEPS))
                        sp.dma_start(bias[:, :, :], bias_dram[1, bass.ds(head, 2)].rearrange("h p n -> p h n"))\
                            .then_inc(bias_ready, 16)
                        sp.dma_start(sink[:, :], sinks[bass.ds(head, 2)].partition_broadcast(P))\
                            .then_inc(bias_ready, 16)
                        pair_store(sp, i, 2, PAIRS + pair - 1)
                        for c in range(B_PIECES):
                            load(i, PER, AT_B + pair * B_PIECES + 2 + c)
            pair_store(sp, None, 0, 2 * PAIRS - 1)
            for c in range(2 * TAIL_TILES):
                load(None, 0, AT_TAIL + 2 + c)
                if c % 2 and c < 8:
                    sp.wait_ge(gated_stored, 16 * 2 * PAIRS)
                    k = 4 * (c // 2)
                    sp.dma_start(mixed[:, k:k + 4], gated_dram[k:k + 4].rearrange("k p n -> p k n"))\
                        .then_inc(gated_loaded[c // 2], 16)

            def load_gates(i, m):
                for b in range(2):
                    load(i, 4, AT_MERGE + 2 + 2 * m + b)
                for h in range(2):
                    n = 2 * m + h
                    if i is not None or n:
                        sp.wait_ge(mixed_ready, at(i, 4, n))
                    for branch in range(2):
                        sp.dma_start(sig[:, branch],
                                     gates_dram[at(i, 2, branch * KT + m), :, h * HALF:(h + 1) * HALF])\
                            .then_inc(gates_loaded, 16)

            for b in range(2):
                sp.wait_ge(gate_stored[b], 16 * GATES)
            for m in range(2):
                load_gates(None, m)
            with sp.Fori(1, KT // 2) as i:
                for m in range(2):
                    load_gates(i, m)
            for c in range(KT // 2):
                load(None, 0, AT_OUT + 2 + c)
                if c == 3:
                    sp.wait_ge(conv_ready, 2 * KT)
                    for b in range(OUT_BLOCKS):
                        sp.dma_start(y[:, :, b * HALF:(b + 1) * HALF],
                                     x[0].rearrange("(t p) n -> p t n", p=P)[:, :, b * HALF:(b + 1) * HALF])\
                            .then_inc(residual_loaded[b], 16)
            with sp.Fori(1, OUT_BLOCKS - 1) as i:
                for c in range(KT // 2):
                    load(i, KT // 2, AT_OUT + 2 + c)
            for g in range(AT_OUT + (OUT_BLOCKS - 1) * KT // 2 + 2, PIECES):
                load(None, 0, g)
            sp.wait_ge(lo_ready, PIECES)
            sp.dma_start(final_gain_sb[:, :], final_gain.partition_broadcast(P)).then_inc(final_gain_loaded, 16)
            for t in range(QT):
                sp.wait_ge(y_scaled, t + 1)
                sp.dma_start(out[0, t * P:(t + 1) * P, :], y[:, t, :]).then_inc(out_stored, 16)
            sp.wait_ge(out_stored, 16 * QT)

        @block.tensor
        def _(pe):
            pe.wait_ge(consts_ready, 16 * 7)
            for r in range(2):
                mm = nc.tensor.matmul(ps[:HEADS, 0, :EXT], table_a_sb[:, r], sel_a_sb[:, r], start=(r == 0), stop=(r == 1))
            mm.then_inc(ext_made, 1)
            nc.tensor.matmul(ps[:HEADS, 1, :EXT], table_b_sb[:, :], sel_b_sb[:, :], start=True, stop=True)\
                .then_inc(ext_made, 1)
            pe.wait_ge(ext_copied, 2)
            for half in range(2):
                for t in range(4):
                    pe.wait_ge(x_scaled, 4 * half + t + 1)
                for k in range(KT):
                    n = half * KT + k
                    if n >= 4:
                        pe.wait_ge(h_ready, n - 3)
                    for t in range(4):
                        tr = nc.tensor.transpose(ps[:, n % 4, t * P:(t + 1) * P],
                                                 x_sb[:, 4 * half + t, k * P:(k + 1) * P], ident[:, :])
                    tr.then_inc(x_turned, 1)
            pe.wait_ge(h_ready, 2 * KT)

            def a_round(i):
                for c in range(A_FIRST):
                    if c == 3:
                        v_turn(pe, i, 0, 0)
                    project(pe, i, PER, c, c // 2, 0, PER_PIECE)
                for slot in range(A_SLOTS):
                    s = slot - A_LEAD
                    if 0 <= s < A_STEPS:
                        a_scores(pe, i, 0, s)
                    if 1 <= s <= A_STEPS:
                        a_turn(pe, i, 0, s - 1)
                    if 2 <= s <= A_STEPS + 1:
                        a_values(pe, i, 0, s - 2)
                    slot_share(pe, i, slot, A_SLOTS, A_LATE, A_FIRST)

            a_round(None)
            with pe.Fori(1, PAIRS) as i:
                a_round(i)

            for c in range(4):
                if c == 3:
                    v_turn(pe, None, B0_TILE, PAIRS)
                project(pe, None, 0, AT_B0 + c, B0_TILE + c // 2, 0, PER_PIECE)
            for kv, before in b_rounds():
                with pe.Fori(0, B_ROUNDS) as i:
                    for u in range(ROUND_PAIRS_B):
                        pair = before + u
                        g0, n0 = AT_B + pair * B_PIECES, A_DONE + pair * B_STEPS
                        for c in range(B_FIRST):
                            project(pe, i, PER, g0 + c, (g0 + c) // 2, 0, PER_PIECE)
                        for slot in range(B_SLOTS):
                            s = slot - B_LEAD
                            if 0 <= s < B_STEPS:
                                b_scores(pe, i, n0, s, kv, g0 // 2)
                            if 1 <= s <= B_STEPS:
                                b_turn(pe, i, n0, s - 1)
                            if 2 <= s <= B_STEPS + 1:
                                b_values(pe, i, n0, s - 2, kv)
                            slot_share(pe, i, slot, B_SLOTS, B_LATE, g0 + B_FIRST)

            with pe.Fori(0, TAIL_TILES // TURN) as i:
                for c in range(2 * TURN):
                    project(pe, i, 2 * TURN, AT_TAIL + c, TAIL_TILE + c // 2, 0, PER_PIECE)
            for c in range(2 * (TAIL_TILES - TAIL_TILES % TURN), 2 * TAIL_TILES):
                project(pe, None, 0, AT_TAIL + c, TAIL_TILE + c // 2, 0, PER_PIECE)

            def merge_piece(i, c):
                g, tile, branch = AT_MERGE + c, c // 2, c % 2
                pe.wait_ge(lo_ready, at(i, 4, g + 1))
                if i is None and tile == 0:
                    for h in range(2 * (TAIL_TILE + TAIL_TILES) - TURN, 2 * (TAIL_TILE + TAIL_TILES)):
                        taken(pe, None, h // 2, h % 2)
                    pe.wait_ge(o_taken, A_DONE + PAIRS * B_STEPS)
                elif i is None:
                    pass
                else:
                    pe.wait_ge(a_scaled if branch == 0 else b_scaled, at(i, 4, 2 * tile - 2))
                for k in range(PIECE):
                    if i is None and tile == 0:
                        pe.wait_ge(conv_ready, PIECE * branch + k + 1)
                    for m, (w, a, half) in enumerate(((w_hi, act_hi, 0), (w_hi, act_lo, 0), (w_hi, act_hi, 1),
                                                      (w_hi, act_lo, 1), (w_lo, act_hi, 0), (w_lo, act_hi, 1))):
                        mm = nc.tensor.matmul(ps[:, 4 * tile + 2 * branch + half], w[:, g % 2, k * P:(k + 1) * P],
                                              a[:, PIECE * branch + k, half * HALF:(half + 1) * HALF],
                                              start=(k == 0 and m in (0, 2)), stop=(k == PIECE - 1 and m >= 4))
                mm.then_inc(piece_used, 1)

            for c in range(4):
                merge_piece(None, c)
            with pe.Fori(1, KT // 2) as i:
                for c in range(4):
                    merge_piece(i, c)

            def out_block(i):
                for c in range(KT // 2):
                    g = AT_OUT + c
                    pe.wait_ge(lo_ready, at(i, KT // 2, g + 1))
                    if i is None:
                        pe.wait_ge(conv_ready, KT + 2 * c + 2)
                    for t in range(QT):
                        if c == 0 and i is None:
                            pe.wait_ge(b_scaled, 2 * KT - (2 if t < 4 else 0))
                        elif c == 0:
                            pe.wait_ge(block_ready, at(i, QT, t + 1 - QT))
                        for kk in range(2):
                            k = 2 * c + kk
                            for m, (a, w) in enumerate(((act_hi, w_hi), (act_hi, w_lo), (act_lo, w_hi))):
                                mm = nc.tensor.matmul(ps[:, t], a[:, k, t * P:(t + 1) * P],
                                                      w[:, g % 2, kk * HALF:(kk + 1) * HALF],
                                                      start=(k == 0 and m == 0), stop=(k == KT - 1 and m == 2))
                        if t == QT - 1:
                            mm.then_inc(piece_used, 1)
                        elif c == KT // 2 - 1:
                            mm.then_inc(bank_summed, 1)

            out_block(None)
            with pe.Fori(1, OUT_BLOCKS) as i:
                out_block(i)

        @block.scalar
        def _(act):
            act.dma_start(table_a_sb[:, :, :], table_a).then_inc(consts_ready, 16)
            act.dma_start(sel_a_sb[:, :, :], sel_a).then_inc(consts_ready, 16)
            act.dma_start(table_b_sb[:, :], table_b).then_inc(consts_ready, 16)
            act.dma_start(sel_b_sb[:, :], sel_b).then_inc(consts_ready, 16)
            act.dma_start(ident[:, :], ident_in).then_inc(consts_ready, 16)
            act.dma_start(masks_sb[:, :, :], mask).then_inc(consts_ready, 16)
            act.dma_start(gain_sb[:, :], gain).then_inc(consts_ready, 16)
            act.wait_ge(eps_ready, 1)

            def square(t):
                act.wait_ge(x_ready[t], 16)
                nc.scalar.activation(flat[:, 4 * HALF:8 * HALF], x_sb[:, t, :], ACT.Square,
                                     accum_out=sumsq[:, t:t + 1]).then_inc(squared, 1)
                act.wait_ge(squared, t + 1)
                nc.scalar.activation(rms[:, t:t + 1], sumsq[:, t:t + 1], ACT.Sqrt, bias=eps[:, :],
                                     scale=1.0 / D_MODEL).then_inc(rooted, 1)

            for t in range(4):
                square(t)
            for n in range(2 * KT):
                half, k = divmod(n, KT)
                if half == 0 and k % 4 == 0:
                    square(4 + k // 4)
                act.wait_ge(x_turned, n + 1)
                if n == 0:
                    act.wait_ge(consts_ready, 16 * 7)
                nc.scalar.activation(act_hi[:, k, half * HALF:(half + 1) * HALF], ps[:, n % 4], ACT.Copy,
                                     scale=gain_sb[:, k:k + 1]).then_inc(h_hi_ready, 1)
            act.wait_ge(windows_stored, 32)
            split_hi(act, None, 0, 0)

            def a_round(i):
                for c in range(A_FIRST):
                    split_hi(act, i, PER, c + 1)
                    if c == 3:
                        v_hi(act, i, 0)
                        q_hi(act, i, 1, 0)
                    if c == 4:
                        q_hi(act, i, 1, 1)
                    if c == 5:
                        k_hi(act, i, 2, 0)
                for slot in range(A_SLOTS + 2):
                    s = slot - A_LEAD
                    if 1 <= s <= A_STEPS:
                        turned_hi(act, i, A_STEPS, s - 1, slice(0, spans((s - 1) // 2) * P))
                    if 0 <= s < A_STEPS:
                        a_exp(act, i, 0, s)
                    if 2 <= s <= A_STEPS + 1:
                        o_rest(act, i, A_STEPS, s - 2, 2 * P)
                    if slot in A_SPLITS:
                        split_hi(act, i, PER, A_FIRST + A_SPLITS[slot] + 1)
                    if slot == 0:
                        k_hi(act, i, 2, 1)
                    m, h = A_TAKES.get(slot - 1, (None, 0))
                    if m:
                        gate_store(act, i, 3 + m, m - 1, A_GATES, h)
                    m, h = A_TAKES.get(slot, (None, 0))
                    if m == 0:
                        z_take(act, i, 3, h, 0, 1)
                    elif m:
                        gate_take(act, i, 3 + m, h, m - 1, A_GATES)
                z_sigmoid(act, i, 3)

            a_round(None)
            with act.Fori(1, PAIRS) as i:
                a_round(i)
            for c in range(4):
                split_hi(act, None, 0, AT_B0 + c + 1)
                if c == 3:
                    v_hi(act, None, PAIRS)
                    k_hi(act, None, B0_TILE + 1, 0)
            k_hi(act, None, B0_TILE + 1, 1)
            for kv, before in b_rounds():
                with act.Fori(0, B_ROUNDS) as i:
                    for u in range(ROUND_PAIRS_B):
                        pair = before + u
                        g0, n0 = AT_B + pair * B_PIECES, A_DONE + pair * B_STEPS
                        gate = GATES_BEFORE_B + pair
                        for c in range(B_FIRST):
                            split_hi(act, i, PER, g0 + c + 1)
                        q_hi(act, i, g0 // 2, 0)
                        for slot in range(B_SLOTS + 2):
                            s = slot - B_LEAD
                            if 1 <= s <= B_STEPS:
                                turned_hi(act, i, 2 * B_STEPS, n0 + s - 1, b_cols(s - 1))
                            if 0 <= s < B_STEPS:
                                b_exp(act, i, n0, s)
                            if 2 <= s <= B_STEPS + 1:
                                o_rest(act, i, 2 * B_STEPS, n0 + s - 2, 4 * P)
                            if slot in B_SPLITS:
                                split_hi(act, i, PER, g0 + B_FIRST + B_SPLITS[slot] + 1)
                            if slot == 0:
                                q_hi(act, i, g0 // 2, 1)
                            m, h = B_TAKES.get(slot - 1, (None, 0))
                            if m:
                                gate_store(act, i, g0 // 2 + 2, gate, 2, h)
                            m, h = B_TAKES.get(slot, (None, 0))
                            if m == 0:
                                z_take(act, i, g0 // 2 + 1, h, PAIRS + pair, 2)
                            elif m:
                                gate_take(act, i, g0 // 2 + 2, h, gate, 2)
                        z_sigmoid(act, i, g0 // 2 + 1)

            def tail_take(n):
                gate_take(act, None, TAIL_TILE + n // 2, n % 2, GATES - TAIL_TILES + n // 2, 0)

            def tail_store(n):
                gate_store(act, None, TAIL_TILE + n // 2, GATES - TAIL_TILES + n // 2, 0, n % 2)

            last = 2 * TAIL_TILES - 1
            for c in range(2 * TAIL_TILES):
                split_hi(act, None, 0, AT_TAIL + c + 1)
                if c >= 2:
                    tail_store(c - 2)
                if c:
                    tail_take(c - 1)

            def convert_hi(k):
                act.wait_ge(gated_loaded[k // 4], 16)
                nc.scalar.activation(act_hi[:, k], mixed[:, k], ACT.Copy).then_inc(conv_hi, 1)

            def gates_sigmoid(i, n):
                act.wait_ge(gates_loaded, at(i, 4 * 32, 32 * (n + 1)))
                nc.scalar.activation(sig[:, :, :], sig[:, :, :], ACT.Sigmoid).then_inc(gates_ready, 1)

            act.wait_ge(piece_used, AT_MERGE - 1)
            for k in range(KT // 2):
                convert_hi(k)
                if k == 3:
                    tail_store(last - 1)
            tail_take(last)
            split_hi(act, None, 0, AT_MERGE + 1)
            act.wait_ge(piece_used, AT_MERGE)
            for k in range(KT // 2, KT):
                convert_hi(k)
                if k == KT // 2:
                    tail_store(last)
            for c in range(1, 4):
                split_hi(act, None, 0, AT_MERGE + c + 1)
                gates_sigmoid(None, c - 1)
            with act.Fori(1, KT // 2) as i:
                for c in range(4):
                    split_hi(act, i, 4, AT_MERGE + c + 1)
                    gates_sigmoid(i, c - 1)
            def squares(b, t):
                if QT * b + t >= 2:
                    act.wait_ge(y_squared, QT * b + t - 1)
                act.wait_ge(block_ready, QT * b + t + 1)
                nc.scalar.activation(sig[:, t % 2], y[:, t, b * HALF:(b + 1) * HALF], ACT.Square,
                                     accum_out=y_parts[:, t * OUT_BLOCKS + b:t * OUT_BLOCKS + b + 1])\
                    .then_inc(y_squared, 1)

            def convert_mixed_hi(k):
                act.wait_ge(mixed_ready, 2 * (k + 1))
                nc.scalar.activation(act_hi[:, k], mixed[:, k], ACT.Copy).then_inc(conv_hi, 1)

            act.wait_ge(piece_used, AT_OUT - 1)
            for k in range(KT // 2):
                convert_mixed_hi(k)
            for b in range(OUT_BLOCKS):
                for c in range(KT // 2):
                    g = AT_OUT + b * KT // 2 + c + 1
                    if g < PIECES:
                        split_hi(act, None, 0, g)
                    if b == 0 and c == 0:
                        gates_sigmoid(None, 2 * KT - 1)
                        act.wait_ge(piece_used, AT_OUT)
                        for k in range(KT // 2, KT):
                            convert_mixed_hi(k)
                    if b and c == 0:
                        for t in range(QT):
                            squares(b - 1, t)
            for t in range(QT + 1):
                if t < QT:
                    squares(OUT_BLOCKS - 1, t)
                if t:
                    act.wait_ge(y_summed, t)
                    nc.scalar.activation(rms[:, t - 1:t], y_stats[:, t - 1:t], ACT.Sqrt, bias=eps[:, :],
                                         scale=1.0 / D_MODEL).then_inc(y_rooted, 1)

        @block.vector
        def _(dve):
            nc.vector.memset(eps[:, :], EPS).then_inc(eps_ready, 1)
            for m in range(2):
                dve.wait_ge(ext_made, m + 1)
                nc.vector.tensor_copy(ext_sb[:, m], ps[:HEADS, m, :EXT]).then_inc(ext_copied, 1)

            def scale_x(t):
                dve.wait_ge(rooted, t + 1)
                nc.vector.reciprocal(rms[:, t:t + 1], rms[:, t:t + 1]).then_inc(rms_ready, 1)
                dve.wait_ge(rms_ready, t + 1)
                nc.vector.tensor_scalar(x_sb[:, t, :], x_sb[:, t, :], rms[:, t:t + 1], None, ALU.mult)\
                    .then_inc(x_scaled, 1)

            for t in range(4):
                scale_x(t)
            for n in range(2 * KT):
                half, k = divmod(n, KT)
                if half == 0 and k % 4 == 0:
                    scale_x(4 + k // 4)
                dve.wait_ge(h_hi_ready, n + 1)
                part_of = slice(half * HALF, (half + 1) * HALF)
                nc.vector.scalar_tensor_tensor(act_lo[:, k, part_of], ps[:, n % 4], gain_sb[:, k:k + 1],
                                               act_hi[:, k, part_of].bitcast(F32), ALU.mult, ALU.subtract)\
                    .then_inc(h_ready, 1)
            split_lo(dve, None, 0, 0)

            def a_round(i):
                for c in range(A_FIRST):
                    split_lo(dve, i, PER, c + 1)
                    if c in (1, 2):
                        v_copy(dve, i, 0, c - 1)
                    if c == 3:
                        v_lo(dve, i, 0)
                        q_lo(dve, i, 1, 1, 0)
                    if c == 4:
                        q_lo(dve, i, 2, 1, 1)
                    if c == 5:
                        k_lo(dve, i, 3, 2, 0)
                for slot in range(A_SLOTS):
                    s = slot - A_LEAD
                    if 0 <= s < A_STEPS:
                        a_softmax(dve, i, 0, s, 0)
                    if 1 <= s <= A_STEPS:
                        turned_lo(dve, i, A_STEPS, s - 1, slice(0, spans((s - 1) // 2) * P))
                    if 0 <= s < A_STEPS:
                        a_normalise(dve, i, 0, s)
                    if 2 <= s <= A_STEPS + 1:
                        o_take(dve, i, A_STEPS, s - 2, 2 * P)
                    if slot in A_SPLITS:
                        split_lo(dve, i, PER, A_FIRST + A_SPLITS[slot] + 1)
                    if slot == 0:
                        k_lo(dve, i, 4, 2, 1)
                        k_double(dve, i, 2)

            a_round(None)
            with dve.Fori(1, PAIRS) as i:
                a_round(i)
            for c in range(4):
                split_lo(dve, None, 0, AT_B0 + c + 1)
                if c in (1, 2):
                    v_copy(dve, None, B0_TILE, c - 1)
                if c == 3:
                    v_lo(dve, None, PAIRS)
                    k_lo(dve, None, 4 * PAIRS + 1, B0_TILE + 1, 0)
            k_lo(dve, None, 4 * PAIRS + 2, B0_TILE + 1, 1)
            k_double(dve, None, B0_TILE + 1)
            for kv, before in b_rounds():
                with dve.Fori(0, B_ROUNDS) as i:
                    for u in range(ROUND_PAIRS_B):
                        pair = before + u
                        g0, n0 = AT_B + pair * B_PIECES, A_DONE + pair * B_STEPS
                        for c in range(B_FIRST):
                            split_lo(dve, i, PER, g0 + c + 1)
                        parts = 4 * PAIRS + 2 + 2 * pair
                        q_lo(dve, i, parts + 1, g0 // 2, 0)
                        for slot in range(B_SLOTS):
                            s = slot - B_LEAD
                            if 0 <= s < B_STEPS:
                                b_softmax(dve, i, n0, s, pair)
                            if 1 <= s <= B_STEPS:
                                turned_lo(dve, i, 2 * B_STEPS, n0 + s - 1, b_cols(s - 1))
                            if 0 <= s < B_STEPS:
                                b_normalise(dve, i, n0, s, pair)
                            if 2 <= s <= B_STEPS + 1:
                                o_take(dve, i, 2 * B_STEPS, n0 + s - 2, 4 * P)
                            if slot in B_SPLITS:
                                split_lo(dve, i, PER, g0 + B_FIRST + B_SPLITS[slot] + 1)
                            if slot == 0:
                                q_lo(dve, i, parts + 2, g0 // 2, 1)

            def convert_lo(k, n):
                dve.wait_ge(conv_hi, n + 1)
                nc.vector.tensor_tensor(act_lo[:, k], mixed[:, k], act_hi[:, k].bitcast(F32), ALU.subtract)\
                    .then_inc(conv_ready, 1)

            def merge_take(i, m, bank0):
                for h in range(2):
                    n = 2 * m + h
                    part_of = slice(h * HALF, (h + 1) * HALF)
                    tile = mixed[:, at(i, 2, m)]
                    dve.wait_ge(piece_used, at(i, 4, AT_MERGE + 2 * m + 2))
                    dve.wait_ge(gates_ready, at(i, 4, n + 1))
                    nc.vector.tensor_tensor(tile[:, part_of], ps[:, bank0 + h], sig[:, 0], ALU.mult)\
                        .then_inc(a_scaled, 1)
                    nc.vector.tensor_tensor(sig[:, 1], ps[:, bank0 + 2 + h], sig[:, 1], ALU.mult)\
                        .then_inc(b_scaled, 1)

            for c in range(2 * TAIL_TILES):
                split_lo(dve, None, 0, AT_TAIL + c + 1)
            for k in range(KT // 2):
                convert_lo(k, k)
            split_lo(dve, None, 0, AT_MERGE + 1)
            for k in range(KT // 2, KT):
                convert_lo(k, k)
            dve.wait_ge(conv_ready, KT)
            split_lo(dve, None, 0, AT_MERGE + 2)
            split_lo(dve, None, 0, AT_MERGE + 3)
            merge_take(None, 0, 0)
            split_lo(dve, None, 0, AT_MERGE + 4)
            with dve.Fori(1, KT // 2) as i:
                split_lo(dve, i, 4, AT_MERGE + 1)
                merge_take(i, -1, 4)
                split_lo(dve, i, 4, AT_MERGE + 2)
                split_lo(dve, i, 4, AT_MERGE + 3)
                merge_take(i, 0, 0)
                split_lo(dve, i, 4, AT_MERGE + 4)
            for k in range(KT // 2):
                convert_lo(k, KT + k)
            split_lo(dve, None, 0, AT_OUT + 1)
            merge_take(None, KT - 1, 4)
            for k in range(KT // 2, KT):
                convert_lo(k, KT + k)

            for b in range(OUT_BLOCKS):
                for c in range(KT // 2):
                    g = AT_OUT + b * KT // 2 + c + 1
                    if AT_OUT + 1 < g < PIECES:
                        split_lo(dve, None, 0, g)
                dve.wait_ge(residual_loaded[b], 16)
                last_block = b == OUT_BLOCKS - 1
                for t in range(QT + (2 if last_block else 0)):
                    if t < QT - 1:
                        dve.wait_ge(bank_summed, (QT - 1) * b + t + 1)
                    elif t == QT - 1:
                        dve.wait_ge(piece_used, AT_OUT + (b + 1) * KT // 2)
                    if t < QT:
                        part_of = y[:, t, b * HALF:(b + 1) * HALF]
                        nc.vector.tensor_tensor(part_of, part_of, ps[:, t], ALU.add).then_inc(block_ready, 1)
                    if last_block and 1 <= t <= QT:
                        dve.wait_ge(y_squared, QT * b + t)
                        nc.vector.tensor_reduce(y_stats[:, t - 1:t], y_parts[:, (t - 1) * OUT_BLOCKS:t * OUT_BLOCKS],
                                                axis=AX.X, op=ALU.add).then_inc(y_summed, 1)
                    if last_block and t >= 2:
                        r = t - 2
                        dve.wait_ge(y_rooted, r + 1)
                        nc.vector.reciprocal(rms[:, r:r + 1], rms[:, r:r + 1]).then_inc(y_inv, 1)
                        dve.wait_ge(y_inv, r + 1)
                        if r == 0:
                            dve.wait_ge(final_gain_loaded, 16)
                        dve.wait_ge(block_ready, QT * b + r + 1)
                        nc.vector.scalar_tensor_tensor(y[:, r, :], y[:, r, :], rms[:, r:r + 1], final_gain_sb[:, :],
                                                       ALU.mult, ALU.mult).then_inc(y_scaled, 1)

        @block.gpsimd
        def _(pool):
            pool.wait_ge(consts_ready, 16 * 7)
            def a_round(i):
                mask_bias(pool, i, 0, 16, 16, 0)
                for s in range(A_STEPS):
                    oT_add(pool, i, A_STEPS, s, (s % 2,), s // 2, 0, 1)
                gate_pair(pool, i, 0, 1, 3, A_STEPS)

            a_round(None)
            with pool.Fori(1, PAIRS) as i:
                a_round(i)
            for kv, before in b_rounds():
                with pool.Fori(0, B_ROUNDS) as i:
                    for u in range(ROUND_PAIRS_B):
                        pair = before + u
                        tile = (AT_B + pair * B_PIECES) // 2
                        n0 = A_DONE + pair * B_STEPS
                        mask_bias(pool, i, 1, 16 * PAIRS + 32 * (pair + 1), 64, 0)
                        for s in range(B_STEPS):
                            oT_add(pool, i, 2 * B_STEPS, n0 + s, (0, 1), s, PAIRS + pair, 2)
                        gate_pair(pool, i, PAIRS + pair, 2, tile + 1, n0 + B_STEPS)

            def merge_add(i, m):
                for h in range(2):
                    part_of = mixed[:, at(i, 2, m)][:, h * HALF:(h + 1) * HALF]
                    pool.wait_ge(b_scaled, at(i, 4, 2 * m + h + 1))
                    nc.gpsimd.tensor_tensor(part_of, part_of, sig[:, 1], ALU.add).then_inc(mixed_ready, 1)

            for m in range(2):
                merge_add(None, m)
            with pool.Fori(1, KT // 2) as i:
                for m in range(2):
                    merge_add(i, m)


def kernel(**inputs):
    import concourse.bacc as bacc
    from concourse.bass_utils import run_bass_kernel_spmd

    a = {k: np.asarray(v) for k, v in inputs.items()}
    w_in = a["w_in"].reshape(KT, P, -1, P)
    tiles = w_in[:, :, in_tile_order()].transpose(2, 1, 0, 3)
    pieces = [tiles.reshape(-1, P, 2, COLS).transpose(0, 2, 1, 3).reshape(-1, P, COLS)]
    branch = np.stack([a[n].reshape(WIDTH // P, P, KT, P) for n in ("w_branch_a", "w_branch_b")])
    pieces.append(branch.transpose(3, 0, 2, 1, 4).reshape(-1, P, COLS))
    last = a["w_out"].reshape(KT // 2, 2, P, OUT_BLOCKS, HALF)
    pieces.append(last.transpose(3, 0, 2, 1, 4).reshape(-1, P, COLS))
    weights = np.concatenate(pieces)
    assert weights.shape[0] == PIECES
    sel_a, sel_b = selections()
    arrays = {
        "x": a["x"],
        "gain": a["norm_gain"].reshape(KT, P).T,
        "final_gain": a["final_gain"],
        "weights": weights,
        "table_a": a["rel_bias_a"][:, 1:].T.reshape(2, P, HEADS).transpose(1, 0, 2),
        "table_b": a["t5_bias"],
        "sinks": a["sinks_b"],
        "sel_a": sel_a.reshape(2, P, EXT).transpose(1, 0, 2),
        "sel_b": sel_b,
        "mask": masks(),
        "ident": np.eye(P, dtype=np.float32),
    }
    arrays = {f"{k}_in": np.ascontiguousarray(v) for k, v in arrays.items()}
    nc = bacc.Bacc("TRN2", target_bir_lowering=False, num_devices=1, dynamic_dma_scratch_size=512)
    args = [nc.dram_tensor(k, v.shape, F32, kind="ExternalInput").ap() for k, v in arrays.items()]
    out = nc.dram_tensor("out", (1, SEQ, D_MODEL), F32, kind="ExternalOutput").ap()
    build(nc, *args, out)
    r = run_bass_kernel_spmd(nc, [arrays], core_ids=[0])
    return r.results[0]["out"]
```

```python
import math
from contextlib import ExitStack

import numpy as np

import concourse.bass as bass
from concourse import mybir

F32 = mybir.dt.float32
F32R = mybir.dt.float32r
ALU = mybir.AluOpType
ACT = mybir.ActivationFunctionType
AX = mybir.AxisListType

P = 128
HALF = 512
NEG = -1e30
EPS = 1e-6

D_MODEL, SEQ, CHUNK = 2048, 1024, 64
HEADS, HEAD_DIM = 16, 64
KV_HEADS = 2
A_PREV, B_PREV = 8, 1
REL_CLIP = 128
T5_BUCKETS, T5_MAX_DIST = 32, 128
WIDTH = HEADS * HEAD_DIM
KV_WIDTH = KV_HEADS * HEAD_DIM

PAIRS = HEADS // 2
KT = D_MODEL // P
QT = SEQ // P
SPAN = A_PREV * CHUNK // P + 1
PIECE = 8
COLS = PIECE * P
EXT = 3 * P
BIAS_ROWS = 2 * P

IN_WIDTHS = [WIDTH, WIDTH, WIDTH, WIDTH, WIDTH, KV_WIDTH, KV_WIDTH, WIDTH, D_MODEL, D_MODEL]
STARTS = [sum(IN_WIDTHS[:i]) // P for i in range(len(IN_WIDTHS))]
QA, KA, VA, ZA, QB, KB, VB, ZB, GA, GB = STARTS
GATES = 2 * D_MODEL // P

A_GATES, B_GATES = 2, 1
A_TILES = 4 + A_GATES
B_TILES = 2 + B_GATES
TAIL_TILES = GATES - PAIRS * (A_GATES + B_GATES)
OUT_BLOCKS = D_MODEL // HALF

A_PIECES = 2 * A_TILES
B_PIECES = 2 * B_TILES
AT_B0 = PAIRS * A_PIECES
AT_B = AT_B0 + 4
AT_TAIL = AT_B + PAIRS * B_PIECES
AT_MERGE = AT_TAIL + 2 * TAIL_TILES
AT_OUT = AT_MERGE + 2 * KT
PIECES = AT_OUT + OUT_BLOCKS * KT // 2
PER_PIECE = PIECE * 2 * 3
BLOCK = KT // 2
GROUP = QT // 2
AT_LAST = PIECES - BLOCK
USES = PIECES + BLOCK

A_LEAD, B_LEAD = 3, 1
A_STEPS, B_STEPS = 2 * QT, QT
A_SLOTS = A_LEAD + A_STEPS + 2
B_SLOTS = B_LEAD + B_STEPS + 2


def in_tile_order():
    order = []
    for p in range(PAIRS):
        order += [VA + p, QA + p, KA + p, ZA + p] + [GA + A_GATES * p + j for j in range(A_GATES)]
    order += [VB, KB]
    for p in range(PAIRS):
        order += [QB + p, ZB + p] + [GA + A_GATES * PAIRS + B_GATES * p + j for j in range(B_GATES)]
    order += [GA + (A_GATES + B_GATES) * PAIRS + j for j in range(TAIL_TILES)]
    return order


def t5_bucket(rel_pos):
    nb = T5_BUCKETS // 2
    ret = (rel_pos > 0).astype(np.int32) * nb
    n = np.abs(rel_pos)
    exact = nb // 2
    large = exact + (np.log(np.maximum(n, 1) / exact) / np.log(T5_MAX_DIST / exact) * (nb - exact)).astype(np.int32)
    return (ret + np.where(n < exact, n, np.minimum(large, nb - 1))).astype(np.int32)


def selections():
    rel = 2 * P - 1 - np.arange(EXT)
    row = np.clip(rel, -REL_CLIP, REL_CLIP) + REL_CLIP - 1
    a = np.zeros((BIAS_ROWS, EXT), np.float32)
    n = np.arange(EXT)
    used = n < EXT - 1
    a[row[used], n[used]] = 1
    a[BIAS_ROWS - 1] -= used
    b = np.zeros((T5_BUCKETS, EXT), np.float32)
    b[t5_bucket(-rel)[used], n[used]] = 1
    return a, b


def masks():
    q = np.arange(P)[:, None] // CHUNK
    k = np.arange(2 * P)[None, :] // CHUNK - 2
    out = []
    for prev in (A_PREV, B_PREV):
        out.append(np.where((k <= q) & (k >= q - prev), 0.0, NEG).astype(np.float32))
    return np.stack(out, 1)


def at(i, per, base):
    return base if i is None else i * per + base


ROUND_TILES = A_TILES
ROUND_PAIRS_B = 2
B0_TILE, B_TILE = AT_B0 // 2, AT_B // 2
TAIL_TILE = AT_TAIL // 2
assert B_TILES * ROUND_PAIRS_B == ROUND_TILES and B0_TILE % 2 == B_TILE % 2 == TAIL_TILE % 2 == 0


def build(nc, x, gain, final_gain, weights, table_a, table_b, sinks, sel_a, sel_b, mask, ident_in, out):
    gates_dram = nc.dram_tensor("gates_dram", (GATES, P, SEQ), F32, kind="Internal").ap()
    gated_dram = nc.dram_tensor("gated_dram", (2 * PAIRS, P, SEQ), F32, kind="Internal").ap()
    bias_dram = nc.dram_tensor("bias_dram", (2, HEADS, P, 2 * P), F32, kind="Internal").ap()
    ext_dram = nc.dram_tensor("ext_dram", (2, HEADS, EXT), F32, kind="Internal").ap()

    with ExitStack() as ctx:
        place = [640]

        def sb(name, shape, dt=F32, where=None):
            size = 4 * math.prod(shape[1:])
            size += -size % 32
            start = place[0] if where is None else where[0]
            if where is None:
                place[0] += size
            else:
                where[0] += size
            return nc.alloc_sbuf_tensor_at(name, shape, dt, offset=start)

        def sem(name):
            return ctx.enter_context(nc.semaphore(name))

        act_hi = sb("act_hi", [P, KT, SEQ], F32R)
        act_lo = sb("act_lo", [P, KT, SEQ], F32R)
        raw = sb("raw", [P, 2, COLS])
        w_hi = sb("w_hi", [P, 2, COLS], F32R)
        w_lo = sb("w_lo", [P, 2, COLS], F32R)
        ident = sb("ident", [P, P])
        masks_at = place[0]
        masks_sb = sb("masks_sb", [P, 2, 2 * P])
        gain_sb = sb("gain_sb", [P, KT])
        sig_at = place[0]
        sig = sb("sig", [P, 2, HALF])
        small = sb("small", [P, 80])
        overlay = place[0]

        def over(name, shape, dt, tensor_at):
            return nc.alloc_sbuf_tensor_at(name, shape, dt, offset=tensor_at)

        x_sb = over("x_sb", [P, QT, D_MODEL], F32, overlay)
        squares_out = act_lo[:, 0:4, HALF:2 * HALF]

        here = [overlay]
        q_stack = sb("q_stack", [P, 2, SEQ], F32R, where=here)
        k_hi2 = sb("k_hi2", [P, 2, SEQ], F32R, where=here)
        k_lo2 = sb("k_lo2", [P, 2, SEQ], F32R, where=here)
        v_parts = sb("v_parts", [P, QT, 2, 2, HEAD_DIM], F32R, where=here)
        vT = sb("vT", [P, SEQ], where=here)
        z_raw = sb("z_raw", [P, SEQ], where=here)
        probs_at = here[0]
        probs = sb("probs", [P, 2, SPAN * P], where=here)
        pT = sb("pT", [P, 2, 2, SPAN * P], F32R, where=here)
        o_sum = sb("o_sum", [P, HALF], where=here)
        oT = sb("oT", [P, SEQ], where=here)
        bias = sb("bias", [P, 2, 2 * P], where=here)
        sink = sb("sink", [P, 2], where=here)
        att_end = here[0]

        sel_a_sb = over("sel_a_sb", [P, 2, EXT], F32, sig_at)
        table_a_sb = over("table_a_sb", [P, 2, HEADS], F32, masks_at)
        table_b_sb = over("table_b_sb", [T5_BUCKETS, HEADS], F32, masks_at + 8 * HEADS)
        sel_b_sb = over("sel_b_sb", [T5_BUCKETS, EXT], F32, masks_at + 12 * HEADS)
        ext_sb = over("ext_sb", [HEADS, 2, EXT], F32, probs_at)

        mixed = over("mixed", [P, KT, SEQ], F32, overlay)
        y = over("y", [P, QT, D_MODEL], F32, overlay)
        final_gain_sb = over("final_gain_sb", [P, HALF], F32, masks_at)
        end = max(att_end, overlay + 4 * KT * SEQ)
        assert end <= nc.sbuf_usable_end, (end, nc.sbuf_usable_end)

        sumsq = small[:, 0:QT]
        rms = small[:, QT:2 * QT]
        eps = small[:, 16:17]
        neg_max = small[:, 17:21]
        exp_sum = small[:, 21:25]
        exp_inv = small[:, 25:29]
        exp_sink = small[:, 29:33]
        keys_max = small[:, 33:35]
        whole_sum = small[:, 35:37]
        y_parts = small[:, 40:40 + QT * OUT_BLOCKS]
        y_stats = small[:, 72:80]

        ps = ctx.enter_context(nc.psum_tensor("ps", [P, 8, HALF], F32))
        flat = ps[:, :, :].rearrange("p b n -> p (b n)")
        TURN = 3
        S = flat[:, 3 * HALF:5 * HALF]
        T = flat[:, 5 * HALF:7 * HALF]
        O = flat[:, 7 * HALF:8 * HALF]

        x_ready = [sem(f"x_ready{t}") for t in range(QT)]
        ident_ready = sem("ident_ready")
        gain_ready = sem("gain_ready")
        tables_ready = sem("tables_ready")
        masks_ready = sem("masks_ready")
        eps_ready = sem("eps_ready")
        squared = sem("squared")
        rooted = sem("rooted")
        rms_ready = sem("rms_ready")
        x_scaled = sem("x_scaled")
        x_turned = sem("x_turned")
        h_hi_ready = sem("h_hi_ready")
        h_ready = sem("h_ready")
        ext_made = sem("ext_made")
        ext_copied = sem("ext_copied")
        ext_stored = sem("ext_stored")
        windows_stored = sem("windows_stored")

        raw_ready = [sem("raw_ready0"), sem("raw_ready1")]
        hi_ready = sem("hi_ready")
        lo_ready = sem("lo_ready")
        piece_used = sem("piece_used")
        half_summed = sem("half_summed")
        bank_taken = [sem(f"bank_taken{b}") for b in range(3)]
        part_hi = sem("part_hi")

        v_turned = sem("v_turned")
        v_hi_ready = sem("v_hi_ready")
        v_ready = sem("v_ready")
        k_doubled = sem("k_doubled")
        bias_ready = sem("bias_ready")
        bias_masked = sem("bias_masked")
        scores_ready = sem("scores_ready")
        biased = sem("biased")
        max_found = sem("max_found")
        max_ready = sem("max_ready")
        exp_ready = sem("exp_ready")
        sink_added = sem("sink_added")
        inv_ready = sem("inv_ready")
        turned = sem("turned")
        pT_hi_ready = sem("pT_hi_ready")
        pT_ready = sem("pT_ready")
        pv_ready = sem("pv_ready")
        probs_ready = sem("probs_ready")
        rest_ready = sem("rest_ready")
        o_taken = sem("o_taken")
        o_added = sem("o_added")
        gated_ready = sem("gated_ready")
        gated_stored = sem("gated_stored")
        z_sig_ready = sem("z_sig_ready")
        z_applied = sem("z_applied")
        gate_stored = [sem("gate_stored0"), sem("gate_stored1")]

        gated_loaded = [sem(f"gated_loaded{k}") for k in range(4)]
        conv_hi = sem("conv_hi")
        conv_ready = sem("conv_ready")
        gates_loaded = sem("gates_loaded")
        gates_ready = sem("gates_ready")
        a_scaled = sem("a_scaled")
        b_scaled = sem("b_scaled")
        mixed_ready = sem("mixed_ready")
        residual_loaded = sem("residual_loaded")
        bank_summed = sem("bank_summed")
        block_ready = sem("block_ready")
        y_squared = sem("y_squared")
        y_summed = sem("y_summed")
        y_rooted = sem("y_rooted")
        y_inv = sem("y_inv")
        final_gain_loaded = sem("final_gain_loaded")
        gain_applied = sem("gain_applied")
        y_scaled_act = sem("y_scaled_act")
        y_scaled_pool = sem("y_scaled_pool")
        y_scaled_dve = sem("y_scaled_dve")
        out_stored = sem("out_stored")

        BIASED_A = 2 * QT + 2 * (QT - SPAN + 1)

        def spans(t):
            return min(t + 1, SPAN)

        def raw_wait(eng, i, per, g):
            eng.wait_ge(raw_ready[g % 2], at(i, 8 * per, 16 * (g // 2 + 1)))

        def split_hi(act, i, per, g):
            raw_wait(act, i, per, g)
            if g >= 2 or i is not None:
                act.wait_ge(piece_used, at(i, per, g - 1))
            nc.scalar.activation(w_hi[:, g % 2], raw[:, g % 2], ACT.Copy).then_inc(hi_ready, 1)

        def split_lo(dve, i, per, g):
            dve.wait_ge(hi_ready, at(i, per, g + 1))
            nc.vector.tensor_tensor(w_lo[:, g % 2], raw[:, g % 2], w_hi[:, g % 2].bitcast(F32),
                                    ALU.subtract).then_inc(lo_ready, 1)

        def bank(tile, h):
            return (2 * tile + h) % TURN

        def merge_bank(tile, branch, half):
            return 4 * tile + 2 * (1 - branch) + half

        def project(pe, i, per, g, tile, first, last):
            b = g % 2
            if first >= last:
                return
            for n in range(first, last):
                h, k, m = n // (3 * PIECE), n // 3 % PIECE, n % 3
                if n == 0:
                    pe.wait_ge(lo_ready, at(i, per, g + 1))
                if b == 0 and n % (3 * PIECE) == 0 and (i is not None or 2 * tile + h >= TURN):
                    pe.wait_ge(bank_taken[bank(tile, h)], at(i, per // TURN, (2 * tile + h) // TURN))
                w, a = ((w_hi, act_hi), (w_hi, act_lo), (w_lo, act_hi))[m]
                kt = PIECE * b + k
                mm = nc.tensor.matmul(ps[:, bank(tile, h)], w[:, b, k * P:(k + 1) * P],
                                      a[:, kt, h * HALF:(h + 1) * HALF],
                                      start=(kt == 0 and m == 0), stop=(kt == KT - 1 and m == 2))
                if n == PER_PIECE - 1:
                    mm.then_inc(piece_used, 1)
                elif b and n == 3 * PIECE - 1:
                    mm.then_inc(half_summed, 1)

        def taken(eng, i, tile, h, per=2 * ROUND_TILES):
            eng.wait_ge(bank_taken[bank(tile, h)], at(i, per // TURN, (2 * tile + h) // TURN + 1))

        def half_done(eng, i, tile, h, per=2 * ROUND_TILES):
            if h == 0:
                eng.wait_ge(half_summed, at(i, per // 2, tile + 1))
            else:
                eng.wait_ge(piece_used, at(i, per, 2 * tile + 2))

        def a_step(s):
            t, a = s // 2, s % 2
            return t, a, (SPAN + 1 - spans(t)) * P

        def a_scores(pe, i, n0, s):
            t, a, c0 = a_step(s)
            if s == 0:
                for h in range(2):
                    taken(pe, i, 1, h)
                pe.wait_ge(k_doubled, at(i, 1, 1))
            if i is not None or n0 + s:
                pe.wait_ge(exp_ready, at(i, A_STEPS, n0 + s))
            for lo, hi in ((c0, 4 * P), (max(c0, 4 * P), 6 * P)):
                if lo >= hi:
                    continue
                keys = (t + 1) * P - 6 * P
                for j, k in enumerate((k_hi2, k_lo2)):
                    mm = nc.tensor.matmul(S[:, lo:hi], q_stack[:, a, t * P:(t + 1) * P],
                                          k[:, a, keys + lo:keys + hi], start=(j == 0), stop=(j == 1))
            mm.then_inc(scores_ready, 1)

        def a_softmax(dve, i, n0, s, b0):
            t, a, c0 = a_step(s)
            near = max(c0, 4 * P)
            if s == 0:
                dve.wait_ge(bias_masked, at(i, 1, 1))
            dve.wait_ge(scores_ready, at(i, A_STEPS, n0 + s + 1))
            nc.vector.tensor_tensor(S[:, near:6 * P], S[:, near:6 * P], bias[:, a, near - 4 * P:],
                                    ALU.add).then_inc(biased, 1)
            if t >= SPAN - 1:
                nc.vector.memset(S[CHUNK:, c0:c0 + CHUNK], NEG).then_inc(biased, 1)
            done = sum(1 + (r // 2 >= SPAN - 1) for r in range(s + 1))
            dve.wait_ge(biased, at(i, BIASED_A, b0 + done))
            nc.vector.tensor_reduce(neg_max[:, 2 * a:2 * a + 1], S[:, c0:6 * P], axis=AX.X, op=ALU.max,
                                    negate=True).then_inc(max_ready, 1)

        def a_exp(act, i, n0, s):
            t, a, c0 = a_step(s)
            act.wait_ge(max_ready, at(i, A_STEPS, n0 + s + 1))
            nc.scalar.activation(probs[:, s % 2, :6 * P - c0], S[:, c0:6 * P], ACT.Exp,
                                 bias=neg_max[:, 2 * a:2 * a + 1],
                                 accum_out=exp_sum[:, 2 * a:2 * a + 1]).then_inc(exp_ready, 1)

        def a_normalise(dve, i, n0, s):
            t, a, c0 = a_step(s)
            inv = exp_inv[:, 2 * a:2 * a + 1]
            dve.wait_ge(exp_ready, at(i, A_STEPS, n0 + s + 1))
            nc.vector.reciprocal(inv, exp_sum[:, 2 * a:2 * a + 1]).then_inc(inv_ready, 1)
            dve.wait_ge(inv_ready, at(i, A_STEPS, n0 + s + 1))
            nc.vector.tensor_scalar(probs[:, s % 2, :6 * P - c0], probs[:, s % 2, :6 * P - c0], inv, None,
                                    ALU.mult).then_inc(probs_ready, 1)

        def a_turn(pe, i, n0, s):
            t, a, c0 = a_step(s)
            pe.wait_ge(probs_ready, at(i, A_STEPS, n0 + s + 1))
            if s == 0:
                pe.wait_ge(v_ready, at(i, 1, 1))
            if i is not None or n0 + s:
                pe.wait_ge(pT_ready, at(i, A_STEPS, n0 + s))
            for j in range(spans(t)):
                tr = nc.tensor.transpose(T[:, j * P:(j + 1) * P], probs[:, s % 2, j * P:(j + 1) * P], ident[:, :])
            tr.then_inc(turned, 1)

        def turned_hi(act, i, per, n, cols):
            act.wait_ge(turned, at(i, per, n + 1))
            if i is not None or n >= 2:
                act.wait_ge(pv_ready, at(i, per, n - 1))
            nc.scalar.activation(pT[:, n % 2, 0, cols], T[:, cols], ACT.Copy).then_inc(pT_hi_ready, 1)

        def turned_lo(dve, i, per, n, cols):
            dve.wait_ge(pT_hi_ready, at(i, per, n + 1))
            nc.vector.tensor_tensor(pT[:, n % 2, 1, cols], T[:, cols], pT[:, n % 2, 0, cols].bitcast(F32),
                                    ALU.subtract).then_inc(pT_ready, 1)

        def a_values(pe, i, n0, s):
            t, a, c0 = a_step(s)
            pe.wait_ge(pT_ready, at(i, A_STEPS, n0 + s + 1))
            if i is not None or n0 + s:
                pe.wait_ge(o_taken, at(i, A_STEPS, n0 + s))
            for j in range(spans(t)):
                mm = nc.tensor.matmul(O[:, :2 * P].rearrange("p (r n) -> p r n", r=2),
                                      v_parts[:, t + 1 - spans(t) + j, a].rearrange("p h d -> p (h d)"),
                                      pT[:, s % 2, :, j * P:(j + 1) * P],
                                      start=(j == 0), stop=(j == spans(t) - 1))
            mm.then_inc(pv_ready, 1)

        def o_half(n):
            return slice(n % 2 * HEAD_DIM, (n % 2 + 1) * HEAD_DIM)

        def o_rest(act, i, per, n, cols):
            act.wait_ge(pv_ready, at(i, per, n + 1))
            if i is not None or n >= 2:
                act.wait_ge(o_added, at(i, per, n - 1))
            nc.scalar.activation(o_sum[o_half(n), :cols], O[HEAD_DIM:, :cols], ACT.Copy).then_inc(rest_ready, 1)

        def o_take(dve, i, per, n, cols):
            dve.wait_ge(rest_ready, at(i, per, n + 1))
            nc.vector.tensor_tensor(o_sum[o_half(n), :cols], O[:HEAD_DIM, :cols], o_sum[o_half(n), :cols], ALU.add)\
                .then_inc(o_taken, 1)

        def oT_add(pool, i, per, n, heads, t, pairs, m):
            pool.wait_ge(o_taken, at(i, per, n + 1))
            if n % (A_STEPS if m == 1 else B_STEPS) == 0 and (i is not None or pairs):
                pool.wait_ge(gated_stored, at(i, 16 * m, 16 * pairs))
            for j, a in enumerate(heads):
                c, low = j * P, (len(heads) + j) * P
                last = nc.gpsimd.tensor_tensor(
                    oT[a * HEAD_DIM:(a + 1) * HEAD_DIM, t * P:(t + 1) * P], o_sum[o_half(n), c:c + P],
                    o_sum[o_half(n), low:low + P], ALU.add)
            last.then_inc(o_added, 1)

        def b_scores(pe, i, n0, s, kv, q_tile):
            if s == 0:
                for h in range(2):
                    taken(pe, i, q_tile, h)
                pe.wait_ge(k_doubled, PAIRS + 1)
            pe.wait_ge(exp_ready, at(i, 2 * B_STEPS, n0 + s))
            c0 = P if s == 0 else 0
            keys = (s - 1) * P
            for a in range(2):
                for j, k in enumerate((k_hi2, k_lo2)):
                    mm = nc.tensor.matmul(S[:, a * HALF + c0:a * HALF + 2 * P], q_stack[:, a, s * P:(s + 1) * P],
                                          k[:, kv, keys + c0:keys + 2 * P], start=(j == 0), stop=(j == 1))
            mm.then_inc(scores_ready, 1)

        SB = S.rearrange("p (a n) -> p a n", a=2)

        def b_softmax(dve, i, n0, s, pair):
            c0 = P if s == 0 else 0
            n, before = n0 + s, pair * B_STEPS + s
            if s == 0:
                dve.wait_ge(bias_masked, at(i, 2, PAIRS + pair + 1))
            dve.wait_ge(scores_ready, at(i, 2 * B_STEPS, n + 1))
            nc.vector.tensor_tensor(SB[:, :, c0:2 * P], SB[:, :, c0:2 * P], bias[:, :, c0:], ALU.add)\
                .then_inc(biased, 1)
            dve.wait_ge(biased, at(i, 2 * B_STEPS, PAIRS * BIASED_A + before + 1))
            nc.vector.tensor_reduce(keys_max, SB[:, :, c0:2 * P], axis=AX.X, op=ALU.max, negate=True)\
                .then_inc(max_found, 1)
            dve.wait_ge(max_found, at(i, 2 * B_STEPS, before + 1))
            nc.vector.scalar_tensor_tensor(neg_max[:, 2 * (n % 2):2 * (n % 2) + 2], sink[:, :], -1.0,
                                           keys_max, ALU.mult, ALU.min).then_inc(max_ready, 1)

        def b_exp(act, i, n0, s):
            c0 = P if s == 0 else 0
            n = n0 + s
            act.wait_ge(max_ready, at(i, 2 * B_STEPS, n + 1))
            for a in range(2):
                col = 2 * (n % 2) + a
                nc.scalar.activation(exp_sink[:, col:col + 1], sink[:, a:a + 1], ACT.Exp,
                                     bias=neg_max[:, col:col + 1])
                last = nc.scalar.activation(probs[:, n % 2, a * 2 * P + c0:(a + 1) * 2 * P],
                                            S[:, a * HALF + c0:a * HALF + 2 * P], ACT.Exp,
                                            bias=neg_max[:, col:col + 1],
                                            accum_out=exp_sum[:, col:col + 1])
            last.then_inc(exp_ready, 1)

        def b_normalise(dve, i, n0, s, pair):
            n, before = n0 + s, pair * B_STEPS + s
            two = slice(2 * (n % 2), 2 * (n % 2) + 2)
            c0 = P if s == 0 else 0
            dve.wait_ge(exp_ready, at(i, 2 * B_STEPS, n + 1))
            nc.vector.tensor_tensor(whole_sum, exp_sum[:, two], exp_sink[:, two], ALU.add).then_inc(sink_added, 1)
            dve.wait_ge(sink_added, at(i, 2 * B_STEPS, before + 1))
            nc.vector.reciprocal(exp_inv[:, two], whole_sum).then_inc(inv_ready, 1)
            dve.wait_ge(inv_ready, at(i, 2 * B_STEPS, n + 1))
            for a in range(2):
                part_of = probs[:, n % 2, a * 2 * P + c0:(a + 1) * 2 * P]
                last = nc.vector.tensor_scalar(part_of, part_of, exp_inv[:, 2 * (n % 2) + a:2 * (n % 2) + a + 1],
                                               None, ALU.mult)
            last.then_inc(probs_ready, 1)

        def b_turn(pe, i, n0, s):
            n = n0 + s
            if s == 0:
                pe.wait_ge(v_ready, PAIRS + 1)
            pe.wait_ge(probs_ready, at(i, 2 * B_STEPS, n + 1))
            pe.wait_ge(pT_ready, at(i, 2 * B_STEPS, n))
            for j in range(0 if s else 1, 2):
                for a in range(2):
                    tr = nc.tensor.transpose(T[:, (2 * j + a) * P:(2 * j + a + 1) * P],
                                             probs[:, n % 2, (2 * a + j) * P:(2 * a + j + 1) * P], ident[:, :])
            tr.then_inc(turned, 1)

        def b_cols(s):
            return slice(0 if s else 2 * P, 4 * P)

        def b_values(pe, i, n0, s, kv):
            n = n0 + s
            pe.wait_ge(pT_ready, at(i, 2 * B_STEPS, n + 1))
            pe.wait_ge(o_taken, at(i, 2 * B_STEPS, n))
            for j in range(0 if s else 1, 2):
                mm = nc.tensor.matmul(O.rearrange("p (r n) -> p r n", r=2),
                                      v_parts[:, s - 1 + j, kv].rearrange("p h d -> p (h d)"),
                                      pT[:, n % 2, :, 2 * j * P:2 * (j + 1) * P],
                                      start=(j == (0 if s else 1)), stop=(j == 1))
            mm.then_inc(pv_ready, 1)

        def q_hi(act, i, tile, h):
            half_done(act, i, tile, h)
            for a in range(2):
                last = nc.scalar.activation(q_stack[0:64, a, h * HALF:(h + 1) * HALF],
                                            ps[a * 64:a * 64 + 64, bank(tile, h)], ACT.Copy,
                                            scale=HEAD_DIM ** -0.5)
            last.then_inc(part_hi, 1)

        def q_lo(dve, i, n, tile, h):
            dve.wait_ge(part_hi, at(i, 4, n))
            for a in range(2):
                last = nc.vector.scalar_tensor_tensor(
                    q_stack[64:128, a, h * HALF:(h + 1) * HALF], ps[a * 64:a * 64 + 64, bank(tile, h)],
                    HEAD_DIM ** -0.5, q_stack[0:64, a, h * HALF:(h + 1) * HALF].bitcast(F32),
                    ALU.mult, ALU.subtract)
            last.then_inc(bank_taken[bank(tile, h)], 1)

        def k_hi(act, i, tile, h):
            half_done(act, i, tile, h)
            for a in range(2):
                last = nc.scalar.activation(k_hi2[0:64, a, h * HALF:(h + 1) * HALF],
                                            ps[a * 64:a * 64 + 64, bank(tile, h)], ACT.Copy)
            last.then_inc(part_hi, 1)

        def k_lo(dve, i, n, tile, h):
            dve.wait_ge(part_hi, at(i, 4, n))
            for a in range(2):
                last = nc.vector.tensor_tensor(
                    k_lo2[0:64, a, h * HALF:(h + 1) * HALF], ps[a * 64:a * 64 + 64, bank(tile, h)],
                    k_hi2[0:64, a, h * HALF:(h + 1) * HALF].bitcast(F32), ALU.subtract)
            last.then_inc(bank_taken[bank(tile, h)], 1)

        def k_double(dve, i, tile):
            for h in range(2):
                taken(dve, i, tile, h)
            for k in (k_hi2, k_lo2):
                last = nc.vector.tensor_copy(k[64:128, :, :], k[0:64, :, :])
            last.then_inc(k_doubled, 1)

        def v_copy(dve, i, tile, h):
            half_done(dve, i, tile, h)
            if i is not None or tile:
                dve.wait_ge(gated_ready, at(i, 1, tile // ROUND_TILES))
            nc.vector.tensor_copy(vT[:, h * HALF:(h + 1) * HALF], ps[:, bank(tile, h)])\
                .then_inc(bank_taken[bank(tile, h)], 1)

        def v_turn(pe, i, tile, pairs):
            for h in range(2):
                taken(pe, i, tile, h)
            if i is not None or pairs:
                pe.wait_ge(pT_ready, at(i, A_STEPS, A_STEPS * pairs))
            for t in range(QT):
                tr = nc.tensor.transpose(T[:, t * P:(t + 1) * P], vT[:, t * P:(t + 1) * P], ident[:, :])
            tr.then_inc(v_turned, 1)

        v_view = v_parts[:, :, :, :, :].rearrange("p t a h d -> p (t a) h d")
        T_view = T.rearrange("p (m d) -> p m d", d=HEAD_DIM)

        def v_hi(act, i, n):
            act.wait_ge(v_turned, at(i, 1, n + 1))
            nc.scalar.activation(v_view[:, :, 0, :], T_view, ACT.Copy).then_inc(v_hi_ready, 1)

        def v_lo(dve, i, n):
            dve.wait_ge(v_hi_ready, at(i, 1, n + 1))
            nc.vector.tensor_tensor(v_view[:, :, 1, :], T_view, v_view[:, :, 0, :].bitcast(F32),
                                    ALU.subtract).then_inc(v_ready, 1)

        def z_take(act, i, tile, h, pairs, m):
            half_done(act, i, tile, h)
            if i is not None or pairs:
                act.wait_ge(gated_ready, at(i, m, pairs))
            nc.scalar.activation(z_raw[:, h * HALF:(h + 1) * HALF], ps[:, bank(tile, h)], ACT.Copy)\
                .then_inc(bank_taken[bank(tile, h)], 1)

        def z_sigmoid(act, i, tile):
            for h in range(2):
                taken(act, i, tile, h)
            nc.scalar.activation(vT[:, :], z_raw[:, :], ACT.Sigmoid).then_inc(z_sig_ready, 1)

        def gate_take(act, i, tile, h, gates, m, per=2 * ROUND_TILES):
            half_done(act, i, tile, h, per)
            if i is not None or gates:
                act.wait_ge(gate_stored[h], at(i, 16 * m, 16 * gates))
            nc.scalar.activation(sig[:, h], ps[:, bank(tile, h)], ACT.Copy)\
                .then_inc(bank_taken[bank(tile, h)], 1)

        def gate_store(act, i, tile, gate, per_gate, h):
            taken(act, i, tile, h)
            act.dma_start(gates_dram[at(i, per_gate, gate), :, h * HALF:(h + 1) * HALF], sig[:, h])\
                .then_inc(gate_stored[h], 16)

        def gate_pair(pool, i, pairs, m, z_tile, n):
            for h in range(2):
                taken(pool, i, z_tile, h)
            pool.wait_ge(o_added, at(i, A_STEPS, n))
            nc.gpsimd.tensor_tensor(oT[:, :], oT[:, :], z_raw[:, :], ALU.mult).then_inc(z_applied, 1)
            pool.wait_ge(z_applied, at(i, m, pairs + 1))
            pool.wait_ge(z_sig_ready, at(i, m, pairs + 1))
            nc.gpsimd.tensor_tensor(oT[:, :], oT[:, :], vT[:, :], ALU.mult).then_inc(gated_ready, 1)

        def pair_store(sp, i, m, pairs):
            sp.wait_ge(gated_ready, at(i, m, pairs + 1))
            sp.dma_start(gated_dram[at(i, m, pairs)], oT[:, :]).then_inc(gated_stored, 16)

        def mask_bias(pool, i, mixer, loads, per, n):
            pool.wait_ge(bias_ready, at(i, per, loads))
            for a in range(2):
                last = nc.gpsimd.tensor_tensor(bias[:, a], bias[:, a], masks_sb[:, mixer], ALU.add)
            last.then_inc(bias_masked, 1)

        def slot_tasks(slots, tiles):
            total = tiles * 2 * PER_PIECE

            def after(products):
                return next(s for s in range(slots + 1) if s * total // slots >= products)

            splits = {after(c * PER_PIECE): c for c in range(2 * tiles)}
            takes = {after((4 * m + 3 + h) * PER_PIECE // 2): (m, h) for m in range(tiles) for h in range(2)}
            assert len(splits) == 2 * tiles and len(takes) == 2 * tiles
            return splits, takes

        A_LATE, B_LATE = 1 + A_GATES, 1 + B_GATES
        A_SPLITS, A_TAKES = slot_tasks(A_SLOTS, A_LATE)
        B_SPLITS, B_TAKES = slot_tasks(B_SLOTS, B_LATE)
        A_FIRST, B_FIRST = A_PIECES - 2 * A_LATE, B_PIECES - 2 * B_LATE
        PER = 2 * ROUND_TILES
        GATES_BEFORE_B = PAIRS * A_GATES
        B_ROUNDS = PAIRS // KV_HEADS // ROUND_PAIRS_B
        A_DONE = PAIRS * A_STEPS

        def slot_share(pe, i, slot, slots, tiles, g0):
            total = tiles * 2 * PER_PIECE
            first, last = slot * total // slots, (slot + 1) * total // slots
            for c in range(2 * tiles):
                project(pe, i, PER, g0 + c, (g0 + c) // 2, max(first - c * PER_PIECE, 0),
                        min(last - c * PER_PIECE, PER_PIECE))

        def b_rounds():
            for kv in range(KV_HEADS):
                yield kv, kv * (PAIRS // KV_HEADS)

        block = ctx.enter_context(nc.Block())

        @block.sync
        def _(sp):
            def load_x(t):
                sp.dma_start(x_sb[:, t, :], x[0, t * P:(t + 1) * P, :]).then_inc(x_ready[t], 16)

            def load(i, per, g):
                if g >= 2:
                    sp.wait_ge(lo_ready, at(i, per, g - 1))
                piece = at(i, per, g if g < PIECES else g - BLOCK)
                sp.dma_start(raw[:, g % 2], weights[piece]).then_inc(raw_ready[g % 2], 16)

            load_x(0)
            sp.dma_start(ident[:, :], ident_in).then_inc(ident_ready, 16)
            sp.dma_start(gain_sb[:, :], gain).then_inc(gain_ready, 16)
            for t in range(1, 4):
                load_x(t)
            load(None, 0, 0)
            load_x(4)
            load_x(5)
            load(None, 0, 1)
            load_x(6)
            load_x(7)
            sp.dma_start(table_a_sb[:, :, :], table_a).then_inc(tables_ready, 16)
            sp.dma_start(sel_a_sb[:, :, :], sel_a).then_inc(tables_ready, 16)
            sp.dma_start(table_b_sb[:, :], table_b).then_inc(tables_ready, 16)
            sp.dma_start(sel_b_sb[:, :], sel_b).then_inc(tables_ready, 16)

            def windows(c):
                if c == 2:
                    sp.wait_ge(ext_copied, 2)
                    sp.dma_start(ext_dram.rearrange("m h n -> h m n"), ext_sb[:, :, :]).then_inc(ext_stored, 16)
                    sp.dma_start(masks_sb[:, :, :], mask).then_inc(masks_ready, 16)
                if c == 3:
                    sp.wait_ge(ext_stored, 16)
                    for mixer in range(2):
                        rows = bass.AP(ext_dram.tensor, mixer * HEADS * EXT + P - 1,
                                       [[EXT, HEADS], [-1, P], [1, 2 * P]])
                        sp.dma_start(bias_dram[mixer], rows).then_inc(windows_stored, 16)
                if c == 4:
                    sp.wait_ge(windows_stored, 32)

            def a_round(i):
                for c in range(A_PIECES):
                    if i is None:
                        windows(c)
                    if c == (4 if i is None else 2):
                        heads = slice(0, 2)
                        if i is not None:
                            pair_store(sp, i, 1, -1)
                            heads = bass.ds(2 * i, 2)
                            sp.wait_ge(biased, at(i, BIASED_A, 0))
                        sp.dma_start(bias[:, :, :], bias_dram[0, heads].rearrange("h p n -> p h n"))\
                            .then_inc(bias_ready, 16)
                    load(i, PER, 2 + c)

            a_round(None)
            with sp.Fori(1, PAIRS) as i:
                a_round(i)
            for c in range(4):
                load(None, 0, AT_B0 + 2 + c)
            for kv, before in b_rounds():
                with sp.Fori(0, B_ROUNDS) as i:
                    for u in range(ROUND_PAIRS_B):
                        pair = before + u
                        head = i * 4 + 2 * pair
                        sp.wait_ge(exp_ready, at(i, 2 * B_STEPS, A_DONE + pair * B_STEPS))
                        sp.dma_start(bias[:, :, :], bias_dram[1, bass.ds(head, 2)].rearrange("h p n -> p h n"))\
                            .then_inc(bias_ready, 16)
                        sp.dma_start(sink[:, :], sinks[bass.ds(head, 2)].partition_broadcast(P))\
                            .then_inc(bias_ready, 16)
                        pair_store(sp, i, 2, PAIRS + pair - 1)
                        for c in range(B_PIECES):
                            load(i, PER, AT_B + pair * B_PIECES + 2 + c)
            pair_store(sp, None, 0, 2 * PAIRS - 1)
            for c in range(2 * TAIL_TILES):
                load(None, 0, AT_TAIL + 2 + c)
                if c % 2 and c < 8:
                    sp.wait_ge(gated_stored, 16 * 2 * PAIRS)
                    k = 4 * (c // 2)
                    sp.dma_start(mixed[:, k:k + 4], gated_dram[k:k + 4].rearrange("k p n -> p k n"))\
                        .then_inc(gated_loaded[c // 2], 16)

            def load_gates(i, m):
                for b in range(2):
                    load(i, 4, AT_MERGE + 2 + 2 * m + b)
                for h in range(2):
                    n = 2 * m + h
                    if i is not None or n:
                        sp.wait_ge(mixed_ready, at(i, 4, n))
                    for branch in range(2):
                        sp.dma_start(sig[:, branch],
                                     gates_dram[at(i, 2, branch * KT + m), :, h * HALF:(h + 1) * HALF])\
                            .then_inc(gates_loaded, 16)

            for b in range(2):
                sp.wait_ge(gate_stored[b], 16 * GATES)
            for m in range(2):
                load_gates(None, m)
            with sp.Fori(1, KT // 2) as i:
                for m in range(2):
                    load_gates(i, m)
            for c in range(BLOCK):
                load(None, 0, AT_OUT + 2 + c)
                if c == 3:
                    sp.wait_ge(conv_ready, 2 * KT)
                    for b in range(OUT_BLOCKS):
                        sp.dma_start(y[:, :, b * HALF:(b + 1) * HALF],
                                     x[0].rearrange("(t p) n -> p t n", p=P)[:, :, b * HALF:(b + 1) * HALF])\
                            .then_inc(residual_loaded, 16)
                if c == 4:
                    sp.dma_start(final_gain_sb[:, :], final_gain[0:HALF].partition_broadcast(P))\
                        .then_inc(final_gain_loaded, 16)
            with sp.Fori(1, OUT_BLOCKS - 1) as i:
                for c in range(BLOCK):
                    load(i, BLOCK, AT_OUT + 2 + c)
                    if c == 4:
                        sp.wait_ge(gain_applied, i * QT)
                        sp.dma_start(final_gain_sb[:, :],
                                     final_gain[bass.ds(i * HALF, HALF)].partition_broadcast(P))\
                            .then_inc(final_gain_loaded, 16)

            def store(t):
                for scaled in (y_scaled_act, y_scaled_pool, y_scaled_dve):
                    sp.wait_ge(scaled, t + 1)
                sp.dma_start(out[0, t * P:(t + 1) * P, :], y[:, t, :]).then_inc(out_stored, 16)

            for c in range(2, 2 * BLOCK):
                load(None, 0, AT_LAST + c)
                if c == 4:
                    sp.wait_ge(gain_applied, (OUT_BLOCKS - 1) * QT)
                    sp.dma_start(final_gain_sb[:, :], final_gain[D_MODEL - HALF:].partition_broadcast(P))\
                        .then_inc(final_gain_loaded, 16)
                if c >= 2 * BLOCK - GROUP:
                    store(c - (2 * BLOCK - GROUP))
            for t in range(GROUP, QT):
                store(t)
            sp.wait_ge(out_stored, 16 * QT)

        @block.tensor
        def _(pe):
            pe.wait_ge(ident_ready, 16)
            for half in range(2):
                for t in range(4):
                    pe.wait_ge(x_scaled, 4 * half + t + 1)
                for k in range(KT + 3):
                    n = half * KT + k
                    if k < KT:
                        if n >= 4:
                            pe.wait_ge(h_ready, n - 3)
                        for t in range(4):
                            tr = nc.tensor.transpose(ps[:, 3 + n % 4, t * P:(t + 1) * P],
                                                     x_sb[:, 4 * half + t, k * P:(k + 1) * P], ident[:, :])
                        tr.then_inc(x_turned, 1)
                    if k >= 3:
                        first = 3 * PIECE * half + (k - 3) % PIECE * 3
                        pe.wait_ge(h_ready, n - 2)
                        project(pe, None, 0, (k - 3) // PIECE, 0, first, first + 3)
            pe.wait_ge(tables_ready, 16 * 4)
            for r in range(2):
                mm = nc.tensor.matmul(ps[:HEADS, 3, :EXT], table_a_sb[:, r], sel_a_sb[:, r],
                                      start=(r == 0), stop=(r == 1))
            mm.then_inc(ext_made, 1)
            nc.tensor.matmul(ps[:HEADS, 4, :EXT], table_b_sb[:, :], sel_b_sb[:, :], start=True, stop=True)\
                .then_inc(ext_made, 1)

            def a_round(i):
                for c in range(0 if i is not None else 2, A_FIRST):
                    if c == 3:
                        v_turn(pe, i, 0, 0)
                    if c == 3 and i is None:
                        pe.wait_ge(ext_copied, 2)
                    project(pe, i, PER, c, c // 2, 0, PER_PIECE)
                for slot in range(A_SLOTS):
                    s = slot - A_LEAD
                    if 0 <= s < A_STEPS:
                        a_scores(pe, i, 0, s)
                    if 1 <= s <= A_STEPS:
                        a_turn(pe, i, 0, s - 1)
                    if 2 <= s <= A_STEPS + 1:
                        a_values(pe, i, 0, s - 2)
                    slot_share(pe, i, slot, A_SLOTS, A_LATE, A_FIRST)

            a_round(None)
            with pe.Fori(1, PAIRS) as i:
                a_round(i)

            for c in range(4):
                if c == 3:
                    v_turn(pe, None, B0_TILE, PAIRS)
                project(pe, None, 0, AT_B0 + c, B0_TILE + c // 2, 0, PER_PIECE)
            for kv, before in b_rounds():
                with pe.Fori(0, B_ROUNDS) as i:
                    for u in range(ROUND_PAIRS_B):
                        pair = before + u
                        g0, n0 = AT_B + pair * B_PIECES, A_DONE + pair * B_STEPS
                        for c in range(B_FIRST):
                            project(pe, i, PER, g0 + c, (g0 + c) // 2, 0, PER_PIECE)
                        for slot in range(B_SLOTS):
                            s = slot - B_LEAD
                            if 0 <= s < B_STEPS:
                                b_scores(pe, i, n0, s, kv, g0 // 2)
                            if 1 <= s <= B_STEPS:
                                b_turn(pe, i, n0, s - 1)
                            if 2 <= s <= B_STEPS + 1:
                                b_values(pe, i, n0, s - 2, kv)
                            slot_share(pe, i, slot, B_SLOTS, B_LATE, g0 + B_FIRST)

            with pe.Fori(0, TAIL_TILES // TURN) as i:
                for c in range(2 * TURN):
                    project(pe, i, 2 * TURN, AT_TAIL + c, TAIL_TILE + c // 2, 0, PER_PIECE)
            for c in range(2 * (TAIL_TILES - TAIL_TILES % TURN), 2 * TAIL_TILES):
                project(pe, None, 0, AT_TAIL + c, TAIL_TILE + c // 2, 0, PER_PIECE)

            last_half = 2 * (TAIL_TILE + TAIL_TILES) - 1
            assert last_half % TURN == 1

            def merge_piece(i, c):
                g, tile, branch = AT_MERGE + c, c // 2, c % 2
                pe.wait_ge(lo_ready, at(i, 4, g + 1))
                if i is None and tile == 0:
                    for n in (last_half - 1, last_half) if branch else (last_half - 2,):
                        taken(pe, None, n // 2, n % 2)
                    pe.wait_ge(o_taken, A_DONE + PAIRS * B_STEPS)
                elif i is not None:
                    pe.wait_ge(a_scaled if branch == 0 else b_scaled, at(i, 4, 2 * tile - 2))
                for k in range(PIECE):
                    if i is None and tile == 0:
                        pe.wait_ge(conv_ready, PIECE * branch + k + 1)
                    for m, (w, a, half) in enumerate(((w_hi, act_hi, 0), (w_hi, act_lo, 0), (w_hi, act_hi, 1),
                                                      (w_hi, act_lo, 1), (w_lo, act_hi, 0), (w_lo, act_hi, 1))):
                        mm = nc.tensor.matmul(ps[:, merge_bank(tile, branch, half)], w[:, g % 2, k * P:(k + 1) * P],
                                              a[:, PIECE * branch + k, half * HALF:(half + 1) * HALF],
                                              start=(k == 0 and m in (0, 2)), stop=(k == PIECE - 1 and m >= 4))
                mm.then_inc(piece_used, 1)

            for c in range(4):
                merge_piece(None, c)
            with pe.Fori(1, KT // 2) as i:
                for c in range(4):
                    merge_piece(i, c)

            def out_products(g, c, t):
                for kk in range(2):
                    k = 2 * c + kk
                    for m, (a, w) in enumerate(((act_hi, w_hi), (act_hi, w_lo), (act_lo, w_hi))):
                        mm = nc.tensor.matmul(ps[:, t], a[:, k, t * P:(t + 1) * P],
                                              w[:, g % 2, kk * HALF:(kk + 1) * HALF],
                                              start=(k == 0 and m == 0), stop=(k == KT - 1 and m == 2))
                return mm

            def out_block(i):
                order = [(c, t) for c in range(BLOCK) for t in range(QT)]
                if i is None:
                    order[:2 * QT] = [(c, 4 * high + t) for high in range(2) for c in range(2) for t in range(4)]
                for c, t in order:
                    g = AT_OUT + c
                    if t in (0, 4):
                        pe.wait_ge(lo_ready, at(i, BLOCK, g + 1))
                        if i is None:
                            pe.wait_ge(conv_ready, KT + 2 * c + 2)
                    if c == 0 and i is None:
                        pe.wait_ge(b_scaled, 2 * KT - (2 if t < 4 else 0))
                    elif c == 0:
                        pe.wait_ge(block_ready, at(i, QT, t + 1 - QT))
                    mm = out_products(g, c, t)
                    if t == QT - 1:
                        mm.then_inc(piece_used, 1)
                    elif c == BLOCK - 1:
                        mm.then_inc(bank_summed, 1)

            out_block(None)
            with pe.Fori(1, OUT_BLOCKS - 1) as i:
                out_block(i)
            for group in range(2):
                tokens = range(group * GROUP, (group + 1) * GROUP)
                order = [(c, t) for c in range(BLOCK) for t in tokens]
                if group:
                    order[-2 * GROUP:] = [(c, t) for t in tokens for c in (BLOCK - 2, BLOCK - 1)]
                for c, t in order:
                    g = AT_LAST + group * BLOCK + c
                    if t == tokens[0]:
                        pe.wait_ge(lo_ready, g + 1)
                    if c == 0:
                        pe.wait_ge(block_ready, QT * (OUT_BLOCKS - 2) + t + 1)
                    mm = out_products(g, c, t)
                    if t == tokens[-1]:
                        mm.then_inc(piece_used, 1)
                    elif c == BLOCK - 1:
                        mm.then_inc(bank_summed, 1)

        @block.scalar
        def _(act):
            act.wait_ge(eps_ready, 1)

            def square(t):
                act.wait_ge(x_ready[t], 16)
                nc.scalar.activation(squares_out, x_sb[:, t, :].rearrange("p (k n) -> p k n", k=4), ACT.Square,
                                     accum_out=sumsq[:, t:t + 1]).then_inc(squared, 1)
                act.wait_ge(squared, t + 1)
                nc.scalar.activation(rms[:, t:t + 1], sumsq[:, t:t + 1], ACT.Sqrt, bias=eps[:, :],
                                     scale=1.0 / D_MODEL).then_inc(rooted, 1)

            for t in range(4):
                square(t)
            act.wait_ge(gain_ready, 16)
            for n in range(2 * KT):
                half, k = divmod(n, KT)
                if n == 2:
                    split_hi(act, None, 0, 0)
                if n == 8:
                    split_hi(act, None, 0, 1)
                if half == 0 and k % 4 == 3:
                    square(4 + k // 4)
                act.wait_ge(x_turned, n + 1)
                nc.scalar.activation(act_hi[:, k, half * HALF:(half + 1) * HALF], ps[:, 3 + n % 4], ACT.Copy,
                                     scale=gain_sb[:, k:k + 1]).then_inc(h_hi_ready, 1)

            def a_round(i):
                for c in range(A_FIRST):
                    if i is not None or c:
                        split_hi(act, i, PER, c + 1)
                    if c == 3:
                        v_hi(act, i, 0)
                        q_hi(act, i, 1, 0)
                    if c == 4:
                        q_hi(act, i, 1, 1)
                    if c == 5:
                        k_hi(act, i, 2, 0)
                for slot in range(A_SLOTS + 2):
                    s = slot - A_LEAD
                    if 1 <= s <= A_STEPS:
                        turned_hi(act, i, A_STEPS, s - 1, slice(0, spans((s - 1) // 2) * P))
                    if 0 <= s < A_STEPS:
                        a_exp(act, i, 0, s)
                    if 2 <= s <= A_STEPS + 1:
                        o_rest(act, i, A_STEPS, s - 2, 2 * P)
                    if slot in A_SPLITS:
                        split_hi(act, i, PER, A_FIRST + A_SPLITS[slot] + 1)
                    if slot == 0:
                        k_hi(act, i, 2, 1)
                    m, h = A_TAKES.get(slot - 1, (None, 0))
                    if m:
                        gate_store(act, i, 3 + m, m - 1, A_GATES, h)
                    m, h = A_TAKES.get(slot, (None, 0))
                    if m == 0:
                        z_take(act, i, 3, h, 0, 1)
                    elif m:
                        gate_take(act, i, 3 + m, h, m - 1, A_GATES)
                z_sigmoid(act, i, 3)

            a_round(None)
            with act.Fori(1, PAIRS) as i:
                a_round(i)
            for c in range(4):
                split_hi(act, None, 0, AT_B0 + c + 1)
                if c == 3:
                    v_hi(act, None, PAIRS)
                    k_hi(act, None, B0_TILE + 1, 0)
            k_hi(act, None, B0_TILE + 1, 1)
            for kv, before in b_rounds():
                with act.Fori(0, B_ROUNDS) as i:
                    for u in range(ROUND_PAIRS_B):
                        pair = before + u
                        g0, n0 = AT_B + pair * B_PIECES, A_DONE + pair * B_STEPS
                        gate = GATES_BEFORE_B + pair
                        for c in range(B_FIRST):
                            split_hi(act, i, PER, g0 + c + 1)
                        q_hi(act, i, g0 // 2, 0)
                        for slot in range(B_SLOTS + 2):
                            s = slot - B_LEAD
                            if 1 <= s <= B_STEPS:
                                turned_hi(act, i, 2 * B_STEPS, n0 + s - 1, b_cols(s - 1))
                            if 0 <= s < B_STEPS:
                                b_exp(act, i, n0, s)
                            if 2 <= s <= B_STEPS + 1:
                                o_rest(act, i, 2 * B_STEPS, n0 + s - 2, 4 * P)
                            if slot in B_SPLITS:
                                split_hi(act, i, PER, g0 + B_FIRST + B_SPLITS[slot] + 1)
                            if slot == 0:
                                q_hi(act, i, g0 // 2, 1)
                            m, h = B_TAKES.get(slot - 1, (None, 0))
                            if m:
                                gate_store(act, i, g0 // 2 + 2, gate, 2, h)
                            m, h = B_TAKES.get(slot, (None, 0))
                            if m == 0:
                                z_take(act, i, g0 // 2 + 1, h, PAIRS + pair, 2)
                            elif m:
                                gate_take(act, i, g0 // 2 + 2, h, gate, 2)
                        z_sigmoid(act, i, g0 // 2 + 1)

            def tail_take(n):
                gate_take(act, None, TAIL_TILE + n // 2, n % 2, GATES - TAIL_TILES + n // 2, 0)

            def tail_store(n):
                gate_store(act, None, TAIL_TILE + n // 2, GATES - TAIL_TILES + n // 2, 0, n % 2)

            last = 2 * TAIL_TILES - 1
            for c in range(2 * TAIL_TILES):
                split_hi(act, None, 0, AT_TAIL + c + 1)
                if c >= 2:
                    tail_store(c - 2)
                if c:
                    tail_take(c - 1)

            def convert_hi(k):
                act.wait_ge(gated_loaded[k // 4], 16)
                nc.scalar.activation(act_hi[:, k], mixed[:, k], ACT.Copy).then_inc(conv_hi, 1)

            def gates_sigmoid(i, n):
                act.wait_ge(gates_loaded, at(i, 4 * 32, 32 * (n + 1)))
                nc.scalar.activation(sig[:, :, :], sig[:, :, :], ACT.Sigmoid).then_inc(gates_ready, 1)

            act.wait_ge(piece_used, AT_MERGE - 1)
            for k in range(KT // 2):
                convert_hi(k)
                if k == 3:
                    tail_store(last - 1)
            tail_take(last)
            split_hi(act, None, 0, AT_MERGE + 1)
            act.wait_ge(piece_used, AT_MERGE)
            for k in range(KT // 2, KT):
                convert_hi(k)
                if k == KT // 2:
                    tail_store(last)
            for c in range(1, 4):
                split_hi(act, None, 0, AT_MERGE + c + 1)
                gates_sigmoid(None, c - 1)
            with act.Fori(1, KT // 2) as i:
                for c in range(4):
                    split_hi(act, i, 4, AT_MERGE + c + 1)
                    gates_sigmoid(i, c - 1)
            def squares(b, t):
                n = QT * b + t
                if n >= 2:
                    act.wait_ge(y_squared, n - 1)
                act.wait_ge(block_ready, n + 1)
                nc.scalar.activation(sig[:, t % 2], y[:, t, b * HALF:(b + 1) * HALF], ACT.Square,
                                     accum_out=y_parts[:, n:n + 1]).then_inc(y_squared, 1)

            def root(t):
                act.wait_ge(y_summed, t + 1)
                nc.scalar.activation(rms[:, t:t + 1], y_stats[:, t:t + 1], ACT.Sqrt, bias=eps[:, :],
                                     scale=1.0 / D_MODEL).then_inc(y_rooted, 1)

            def scale(t):
                if t == 0:
                    act.wait_ge(gain_applied, (OUT_BLOCKS - 1) * QT)
                act.wait_ge(y_inv, t + 1)
                part_of = y[:, t, :2 * HALF]
                nc.scalar.activation(part_of, part_of, ACT.Copy, scale=rms[:, t:t + 1]).then_inc(y_scaled_act, 1)

            def convert_mixed_hi(k):
                act.wait_ge(mixed_ready, 2 * (k + 1))
                nc.scalar.activation(act_hi[:, k], mixed[:, k], ACT.Copy).then_inc(conv_hi, 1)

            act.wait_ge(piece_used, AT_OUT - 1)
            for k in range(KT // 2):
                convert_mixed_hi(k)
            for c in range(BLOCK):
                split_hi(act, None, 0, AT_OUT + c + 1)
                if c == 0:
                    gates_sigmoid(None, 2 * KT - 1)
                    act.wait_ge(piece_used, AT_OUT)
                    for k in range(KT // 2, KT):
                        convert_mixed_hi(k)
            for b in range(1, OUT_BLOCKS):
                for c in range(BLOCK):
                    split_hi(act, None, 0, AT_OUT + b * BLOCK + c + 1)
                    if c == 0:
                        for t in range(QT):
                            squares(b - 1, t)
            for t in range(GROUP):
                squares(OUT_BLOCKS - 1, t)
            for c in range(BLOCK - 1):
                split_hi(act, None, 0, PIECES + c + 1)
                if c < GROUP:
                    root(c)
                if 1 <= c <= GROUP:
                    scale(c - 1)
            for t in range(GROUP, QT + 2):
                if t < QT:
                    squares(OUT_BLOCKS - 1, t)
                if GROUP < t <= QT:
                    root(t - 1)
                if t >= GROUP + 2:
                    scale(t - 2)

        @block.vector
        def _(dve):
            nc.vector.memset(eps[:, :], EPS).then_inc(eps_ready, 1)
            def scale_x(t):
                dve.wait_ge(rooted, t + 1)
                nc.vector.reciprocal(rms[:, t:t + 1], rms[:, t:t + 1]).then_inc(rms_ready, 1)
                dve.wait_ge(rms_ready, t + 1)
                nc.vector.tensor_scalar(x_sb[:, t, :], x_sb[:, t, :], rms[:, t:t + 1], None, ALU.mult)\
                    .then_inc(x_scaled, 1)

            for t in range(4):
                scale_x(t)
            for n in range(2 * KT):
                half, k = divmod(n, KT)
                if n == 3:
                    split_lo(dve, None, 0, 0)
                if n == 9:
                    split_lo(dve, None, 0, 1)
                if half == 0 and k % 4 == 3:
                    scale_x(4 + k // 4)
                dve.wait_ge(h_hi_ready, n + 1)
                part_of = slice(half * HALF, (half + 1) * HALF)
                nc.vector.scalar_tensor_tensor(act_lo[:, k, part_of], ps[:, 3 + n % 4], gain_sb[:, k:k + 1],
                                               act_hi[:, k, part_of].bitcast(F32), ALU.mult, ALU.subtract)\
                    .then_inc(h_ready, 1)

            def a_round(i):
                for c in range(A_FIRST):
                    if i is not None or c:
                        split_lo(dve, i, PER, c + 1)
                    if c in (1, 2):
                        v_copy(dve, i, 0, c - 1)
                    if c == 2 and i is None:
                        for m in range(2):
                            dve.wait_ge(ext_made, m + 1)
                            nc.vector.tensor_copy(ext_sb[:, m], ps[:HEADS, 3 + m, :EXT]).then_inc(ext_copied, 1)
                    if c == 3:
                        v_lo(dve, i, 0)
                        q_lo(dve, i, 1, 1, 0)
                    if c == 4:
                        q_lo(dve, i, 2, 1, 1)
                    if c == 5:
                        k_lo(dve, i, 3, 2, 0)
                for slot in range(A_SLOTS):
                    s = slot - A_LEAD
                    if 0 <= s < A_STEPS:
                        a_softmax(dve, i, 0, s, 0)
                    if 1 <= s <= A_STEPS:
                        turned_lo(dve, i, A_STEPS, s - 1, slice(0, spans((s - 1) // 2) * P))
                    if 0 <= s < A_STEPS:
                        a_normalise(dve, i, 0, s)
                    if 2 <= s <= A_STEPS + 1:
                        o_take(dve, i, A_STEPS, s - 2, 2 * P)
                    if slot in A_SPLITS:
                        split_lo(dve, i, PER, A_FIRST + A_SPLITS[slot] + 1)
                    if slot == 0:
                        k_lo(dve, i, 4, 2, 1)
                        k_double(dve, i, 2)

            a_round(None)
            with dve.Fori(1, PAIRS) as i:
                a_round(i)
            for c in range(4):
                split_lo(dve, None, 0, AT_B0 + c + 1)
                if c in (1, 2):
                    v_copy(dve, None, B0_TILE, c - 1)
                if c == 3:
                    v_lo(dve, None, PAIRS)
                    k_lo(dve, None, 4 * PAIRS + 1, B0_TILE + 1, 0)
            k_lo(dve, None, 4 * PAIRS + 2, B0_TILE + 1, 1)
            k_double(dve, None, B0_TILE + 1)
            for kv, before in b_rounds():
                with dve.Fori(0, B_ROUNDS) as i:
                    for u in range(ROUND_PAIRS_B):
                        pair = before + u
                        g0, n0 = AT_B + pair * B_PIECES, A_DONE + pair * B_STEPS
                        for c in range(B_FIRST):
                            split_lo(dve, i, PER, g0 + c + 1)
                        parts = 4 * PAIRS + 2 + 2 * pair
                        q_lo(dve, i, parts + 1, g0 // 2, 0)
                        for slot in range(B_SLOTS):
                            s = slot - B_LEAD
                            if 0 <= s < B_STEPS:
                                b_softmax(dve, i, n0, s, pair)
                            if 1 <= s <= B_STEPS:
                                turned_lo(dve, i, 2 * B_STEPS, n0 + s - 1, b_cols(s - 1))
                            if 0 <= s < B_STEPS:
                                b_normalise(dve, i, n0, s, pair)
                            if 2 <= s <= B_STEPS + 1:
                                o_take(dve, i, 2 * B_STEPS, n0 + s - 2, 4 * P)
                            if slot in B_SPLITS:
                                split_lo(dve, i, PER, g0 + B_FIRST + B_SPLITS[slot] + 1)
                            if slot == 0:
                                q_lo(dve, i, parts + 2, g0 // 2, 1)

            def convert_lo(k, n):
                dve.wait_ge(conv_hi, n + 1)
                nc.vector.tensor_tensor(act_lo[:, k], mixed[:, k], act_hi[:, k].bitcast(F32), ALU.subtract)\
                    .then_inc(conv_ready, 1)

            def merge_take(i, m, tile):
                for h in range(2):
                    n = 2 * m + h
                    part_of = slice(h * HALF, (h + 1) * HALF)
                    mixed_tile = mixed[:, at(i, 2, m)]
                    dve.wait_ge(piece_used, at(i, 4, AT_MERGE + 2 * m + 2))
                    dve.wait_ge(gates_ready, at(i, 4, n + 1))
                    nc.vector.tensor_tensor(mixed_tile[:, part_of], ps[:, merge_bank(tile, 0, h)], sig[:, 0], ALU.mult)\
                        .then_inc(a_scaled, 1)
                    nc.vector.tensor_tensor(sig[:, 1], ps[:, merge_bank(tile, 1, h)], sig[:, 1], ALU.mult)\
                        .then_inc(b_scaled, 1)

            for c in range(2 * TAIL_TILES):
                split_lo(dve, None, 0, AT_TAIL + c + 1)
            for k in range(KT // 2):
                convert_lo(k, k)
            split_lo(dve, None, 0, AT_MERGE + 1)
            for k in range(KT // 2, KT):
                convert_lo(k, k)
            dve.wait_ge(conv_ready, KT)
            split_lo(dve, None, 0, AT_MERGE + 2)
            split_lo(dve, None, 0, AT_MERGE + 3)
            merge_take(None, 0, 0)
            split_lo(dve, None, 0, AT_MERGE + 4)
            with dve.Fori(1, KT // 2) as i:
                split_lo(dve, i, 4, AT_MERGE + 1)
                merge_take(i, -1, 1)
                split_lo(dve, i, 4, AT_MERGE + 2)
                split_lo(dve, i, 4, AT_MERGE + 3)
                merge_take(i, 0, 0)
                split_lo(dve, i, 4, AT_MERGE + 4)
            for k in range(KT // 2):
                convert_lo(k, KT + k)
            split_lo(dve, None, 0, AT_OUT + 1)
            merge_take(None, KT - 1, 1)
            for k in range(KT // 2, KT):
                convert_lo(k, KT + k)

            def add(i, b, t):
                first = at(i, HALF, b * HALF)
                part_of = y[:, t, bass.ds(first, HALF)]
                nc.vector.tensor_tensor(part_of, part_of, ps[:, t], ALU.add).then_inc(block_ready, 1)

            def add_block(i, b):
                for t in range(QT):
                    if t < QT - 1:
                        dve.wait_ge(bank_summed, at(i, QT - 1, (QT - 1) * b + t + 1))
                    else:
                        dve.wait_ge(piece_used, at(i, BLOCK, AT_OUT + (b + 1) * BLOCK))
                    add(i, b, t)

            def total(t):
                dve.wait_ge(y_squared, QT * (OUT_BLOCKS - 1) + t + 1)
                nc.vector.tensor_reduce(y_stats[:, t:t + 1], y_parts[:, t::QT], axis=AX.X, op=ALU.add)\
                    .then_inc(y_summed, 1)

            def finish(t):
                dve.wait_ge(y_rooted, t + 1)
                nc.vector.reciprocal(rms[:, t:t + 1], rms[:, t:t + 1]).then_inc(y_inv, 1)
                dve.wait_ge(y_inv, t + 1)
                if t == 0:
                    dve.wait_ge(final_gain_loaded, 16 * OUT_BLOCKS)
                dve.wait_ge(block_ready, QT * (OUT_BLOCKS - 1) + t + 1)
                part_of = y[:, t, D_MODEL - HALF:]
                nc.vector.scalar_tensor_tensor(part_of, part_of, rms[:, t:t + 1], final_gain_sb[:, :],
                                               ALU.mult, ALU.mult).then_inc(y_scaled_dve, 1)

            for c in range(1, BLOCK):
                split_lo(dve, None, 0, AT_OUT + c + 1)
            dve.wait_ge(residual_loaded, 16 * OUT_BLOCKS)
            add_block(None, 0)
            with dve.Fori(1, OUT_BLOCKS - 1) as i:
                for c in range(BLOCK):
                    split_lo(dve, i, BLOCK, AT_OUT + c + 1)
                add_block(i, 0)
            for c in range(BLOCK):
                split_lo(dve, None, 0, AT_LAST + c + 1)
            for t in range(GROUP):
                if t < GROUP - 1:
                    dve.wait_ge(bank_summed, (QT - 1) * (OUT_BLOCKS - 1) + t + 1)
                else:
                    dve.wait_ge(piece_used, PIECES)
                add(None, OUT_BLOCKS - 1, t)
            for c in range(BLOCK - 1):
                split_lo(dve, None, 0, PIECES + c + 1)
                if c < GROUP:
                    total(c)
                if 1 <= c <= GROUP:
                    finish(c - 1)
            for t in range(GROUP, QT + 2):
                if t < QT - 1:
                    dve.wait_ge(bank_summed, (QT - 1) * (OUT_BLOCKS - 1) + t)
                elif t == QT - 1:
                    dve.wait_ge(piece_used, USES)
                if t < QT:
                    add(None, OUT_BLOCKS - 1, t)
                if GROUP < t <= QT:
                    total(t - 1)
                if t >= GROUP + 2:
                    finish(t - 2)

        @block.gpsimd
        def _(pool):
            pool.wait_ge(masks_ready, 16)
            def a_round(i):
                mask_bias(pool, i, 0, 16, 16, 0)
                for s in range(A_STEPS):
                    oT_add(pool, i, A_STEPS, s, (s % 2,), s // 2, 0, 1)
                gate_pair(pool, i, 0, 1, 3, A_STEPS)

            a_round(None)
            with pool.Fori(1, PAIRS) as i:
                a_round(i)
            for kv, before in b_rounds():
                with pool.Fori(0, B_ROUNDS) as i:
                    for u in range(ROUND_PAIRS_B):
                        pair = before + u
                        tile = (AT_B + pair * B_PIECES) // 2
                        n0 = A_DONE + pair * B_STEPS
                        mask_bias(pool, i, 1, 16 * PAIRS + 32 * (pair + 1), 64, 0)
                        for s in range(B_STEPS):
                            oT_add(pool, i, 2 * B_STEPS, n0 + s, (0, 1), s, PAIRS + pair, 2)
                        gate_pair(pool, i, PAIRS + pair, 2, tile + 1, n0 + B_STEPS)

            def merge_add(i, m):
                for h in range(2):
                    part_of = mixed[:, at(i, 2, m)][:, h * HALF:(h + 1) * HALF]
                    pool.wait_ge(b_scaled, at(i, 4, 2 * m + h + 1))
                    nc.gpsimd.tensor_tensor(part_of, part_of, sig[:, 1], ALU.add).then_inc(mixed_ready, 1)

            for m in range(2):
                merge_add(None, m)
            with pool.Fori(1, KT // 2) as i:
                for m in range(2):
                    merge_add(i, m)

            for b in range(OUT_BLOCKS - 1):
                pool.wait_ge(final_gain_loaded, 16 * (b + 1))
                for t in range(QT):
                    pool.wait_ge(y_squared, QT * b + t + 1)
                    part_of = y[:, t, b * HALF:(b + 1) * HALF]
                    nc.gpsimd.tensor_tensor(part_of, part_of, final_gain_sb[:, :], ALU.mult).then_inc(gain_applied, 1)
            pool.wait_ge(gain_applied, (OUT_BLOCKS - 1) * QT)
            for t in range(QT):
                pool.wait_ge(y_inv, t + 1)
                part_of = y[:, t, 2 * HALF:3 * HALF]
                nc.gpsimd.tensor_scalar(part_of, part_of, rms[:, t:t + 1], None, ALU.mult).then_inc(y_scaled_pool, 1)


def kernel(**inputs):
    import concourse.bacc as bacc
    from concourse.bass_utils import run_bass_kernel_spmd

    a = {k: np.asarray(v) for k, v in inputs.items()}
    w_in = a["w_in"].reshape(KT, P, -1, P)
    tiles = w_in[:, :, in_tile_order()].transpose(2, 1, 0, 3)
    pieces = [tiles.reshape(-1, P, 2, COLS).transpose(0, 2, 1, 3).reshape(-1, P, COLS)]
    branch = np.stack([a[n].reshape(WIDTH // P, P, KT, P) for n in ("w_branch_a", "w_branch_b")])
    pieces.append(branch.transpose(3, 0, 2, 1, 4).reshape(-1, P, COLS))
    last = a["w_out"].reshape(KT // 2, 2, P, OUT_BLOCKS, HALF)
    pieces.append(last.transpose(3, 0, 2, 1, 4).reshape(-1, P, COLS))
    weights = np.concatenate(pieces)
    assert weights.shape[0] == PIECES
    sel_a, sel_b = selections()
    arrays = {
        "x": a["x"],
        "gain": a["norm_gain"].reshape(KT, P).T,
        "final_gain": a["final_gain"],
        "weights": weights,
        "table_a": a["rel_bias_a"][:, 1:].T.reshape(2, P, HEADS).transpose(1, 0, 2),
        "table_b": a["t5_bias"],
        "sinks": a["sinks_b"],
        "sel_a": sel_a.reshape(2, P, EXT).transpose(1, 0, 2),
        "sel_b": sel_b,
        "mask": masks(),
        "ident": np.eye(P, dtype=np.float32),
    }
    arrays = {f"{k}_in": np.ascontiguousarray(v) for k, v in arrays.items()}
    nc = bacc.Bacc("TRN2", target_bir_lowering=False, num_devices=1, dynamic_dma_scratch_size=512)
    args = [nc.dram_tensor(k, v.shape, F32, kind="ExternalInput").ap() for k, v in arrays.items()]
    out = nc.dram_tensor("out", (1, SEQ, D_MODEL), F32, kind="ExternalOutput").ap()
    build(nc, *args, out)
    r = run_bass_kernel_spmd(nc, [arrays], core_ids=[0])
    return r.results[0]["out"]
```
